# Optimizing a Trainium2 kernel written in Bass

```python
import jax
import jax.numpy as jnp
from jax import lax
import numpy as np
import math

D_MODEL = 1024
BATCH = 1
SEQ = 256
DEPTH = 2

MEM_LEN = 256
EPS = 1e-6
N_EVEN = (DEPTH + 1) // 2
N_ODD = DEPTH // 2

MLSTM_HEADS = 4
MLSTM_DQK = 64
MLSTM_DV = 128
MLSTM_CHUNK = 64
GATE_SOFTCAP = 15.0

SB_HEADS = 4
SB_DH = 128
SB_BLOCK = 128

GDN_HEADS = 8
GDN_DK = 128
GDN_DV = 128
GDN_CONV = 4
GDN_CHUNK = 64

XA_HEADS = 4
XA_DH = D_MODEL // XA_HEADS
D_FF = 4 * D_MODEL

ML_QK = MLSTM_HEADS * MLSTM_DQK
ML_V = MLSTM_HEADS * MLSTM_DV
SB_W = SB_HEADS * SB_DH
AB_SIZES = (ML_QK, ML_QK, ML_V, ML_V, MLSTM_HEADS, MLSTM_HEADS, SB_W, SB_W, SB_W)
AB_IN = sum(AB_SIZES)
AB_OUT = ML_V + SB_W

GDN_QK = GDN_HEADS * GDN_DK
GDN_VW = GDN_HEADS * GDN_DV
GDN_CONV_CH = 2 * GDN_QK + GDN_VW
C_SIZES = (GDN_CONV_CH, GDN_VW, GDN_HEADS, GDN_HEADS)
C_IN = sum(C_SIZES)


def _split(y, sizes):
    return jnp.split(y, np.cumsum(sizes)[:-1].tolist(), axis=-1)

def rmsnorm(x, g):
    xf = x.astype(jnp.float32)
    y = xf * lax.rsqrt(jnp.mean(xf * xf, axis=-1, keepdims=True) + EPS)
    return (y * g.astype(jnp.float32)).astype(x.dtype)

def l2norm(x):
    xf = x.astype(jnp.float32)
    return xf * lax.rsqrt(jnp.sum(xf * xf, axis=-1, keepdims=True) + EPS)

def _to_chunks(a, L):
    B, T = a.shape[0], a.shape[1]
    a = a.reshape((B, T // L, L) + a.shape[2:])
    return jnp.moveaxis(a, (1, 3), (0, 2))

def _from_chunks(a):
    a = jnp.moveaxis(a, (0, 2), (1, 3))
    nc, L = a.shape[1], a.shape[2]
    return a.reshape((a.shape[0], nc * L) + a.shape[3:])

def mlstm(q, k, v, i_pre, f_pre):
    f32 = jnp.float32
    B, T, H, dk = q.shape
    dv = v.shape[-1]
    L = MLSTM_CHUNK
    log_i = GATE_SOFTCAP * jnp.tanh(i_pre.astype(f32) / GATE_SOFTCAP)
    log_f = jax.nn.log_sigmoid(f_pre.astype(f32))
    xs = (_to_chunks(q.astype(f32), L),
          _to_chunks(k.astype(f32) * (dk ** -0.5), L),
          _to_chunks(v.astype(f32), L),
          _to_chunks(log_i, L),
          _to_chunks(log_f, L))
    causal = jnp.tril(jnp.ones((L, L), dtype=bool))

    def step(carry, inp):
        C, n, m = carry
        qc, kc, vc, li, lf = inp
        b = jnp.cumsum(lf, axis=-1)
        d = jnp.where(causal, b[..., :, None] - b[..., None, :] + li[..., None, :], -jnp.inf)
        inter = b + m[..., None]
        m_t = jnp.maximum(inter, jnp.max(d, axis=-1))
        w_inter = jnp.exp(inter - m_t)
        s = jnp.einsum('bhtd,bhsd->bhts', qc, kc) * jnp.exp(d - m_t[..., None])
        num = jnp.einsum('bhts,bhsv->bhtv', s, vc) + w_inter[..., None] * jnp.einsum('bhvd,bhtd->bhtv', C, qc)
        den = jnp.sum(s, axis=-1) + w_inter * jnp.einsum('bhd,bhtd->bht', n, qc)
        h = num / jnp.maximum(jnp.abs(den), jnp.exp(-m_t))[..., None]
        m_new = m_t[..., -1]
        w_old = jnp.exp(b[..., -1] + m - m_new)
        w_s = jnp.exp(b[..., -1:] - b + li - m_new[..., None])
        C = w_old[..., None, None] * C + jnp.einsum('bhsv,bhsd->bhvd', vc * w_s[..., None], kc)
        n = w_old[..., None] * n + jnp.einsum('bhs,bhsd->bhd', w_s, kc)
        return (C, n, m_new), h

    init = (jnp.zeros((B, H, dv, dk), f32), jnp.zeros((B, H, dk), f32), jnp.zeros((B, H), f32))
    _, h = lax.scan(step, init, xs)
    return _from_chunks(h)

def stick_breaking(q, k, v):
    f32 = jnp.float32
    B, T, H, dh = q.shape
    scale = dh ** -0.5
    qf, kf, vf = q.astype(f32), k.astype(f32), v.astype(f32)
    outs = []
    for t0 in range(0, T, SB_BLOCK):
        t1 = t0 + SB_BLOCK
        z = jnp.einsum('bqhd,bkhd->bhqk', qf[:, t0:t1], kf[:, :t1]) * scale
        qpos = t0 + jnp.arange(SB_BLOCK)
        kpos = jnp.arange(t1)
        strict = kpos[None, :] < qpos[:, None]
        log_beta = jnp.where(strict, jax.nn.log_sigmoid(z), -jnp.inf)
        log_1m = jnp.where(strict, jax.nn.log_sigmoid(-z), 0.0)
        acc = lax.cumsum(log_1m, axis=3, reverse=True) - log_1m
        w = jnp.exp(log_beta + acc)
        outs.append(jnp.einsum('bhqk,bkhd->bqhd', w, vf[:, :t1]))
    return jnp.concatenate(outs, axis=1)

def short_conv(x, w):
    K = w.shape[0]
    T = x.shape[1]
    xp = jnp.pad(x, ((0, 0), (K - 1, 0), (0, 0)))
    return sum(xp[:, j:j + T] * w[j] for j in range(K))

def gated_deltanet(q, k, v, beta, log_alpha):
    f32 = jnp.float32
    B, T, H, dk = q.shape
    dv = v.shape[-1]
    L = GDN_CHUNK
    qc = _to_chunks(q.astype(f32) * (dk ** -0.5), L)
    kc = _to_chunks(k.astype(f32), L)
    vc = _to_chunks(v.astype(f32), L)
    bc = _to_chunks(beta.astype(f32), L)
    g = jnp.cumsum(_to_chunks(log_alpha.astype(f32), L), axis=-1)
    incl = jnp.tril(jnp.ones((L, L), dtype=bool))
    strict = jnp.tril(jnp.ones((L, L), dtype=bool), k=-1)
    decay = jnp.where(incl, jnp.exp(jnp.where(incl, g[..., :, None] - g[..., None, :], 0.0)), 0.0)
    kk = jnp.einsum('nbhtd,nbhsd->nbhts', kc, kc)
    lower = jnp.where(strict, bc[..., :, None] * kk * decay, 0.0)
    eye = jnp.eye(L, dtype=f32)
    rhs = jnp.concatenate([vc * bc[..., None], kc * (bc * jnp.exp(g))[..., None]], axis=-1)
    sol = lax.linalg.triangular_solve(lower + eye, rhs, left_side=True, lower=True, unit_diagonal=True)
    u_c, w_c = sol[..., :dv], sol[..., dv:]
    attn = jnp.einsum('nbhtd,nbhsd->nbhts', qc, kc) * decay
    q_dec = qc * jnp.exp(g)[..., None]
    g_last = g[..., -1]
    k_dec = kc * jnp.exp(g_last[..., None] - g)[..., None]

    def step(S, inp):
        u, wk, att, qd, kd, gl = inp
        v_new = u - jnp.einsum('bhtk,bhkv->bhtv', wk, S)
        o = jnp.einsum('bhtk,bhkv->bhtv', qd, S) + jnp.einsum('bhts,bhsv->bhtv', att, v_new)
        S = S * jnp.exp(gl)[..., None, None] + jnp.einsum('bhsk,bhsv->bhkv', kd, v_new)
        return S, o

    S0 = jnp.zeros((B, H, dk, dv), f32)
    _, o = lax.scan(step, S0, (u_c, w_c, attn, q_dec, k_dec, g_last))
    return _from_chunks(o)

def ab_mixer(h, w_in, b_i, b_f, head_gain, w_out):
    B, T, _ = h.shape
    mq, mk, mv, mo, mi, mf, sq, sk, sv = _split(h @ w_in, AB_SIZES)
    hm = mlstm(mq.reshape(B, T, MLSTM_HEADS, MLSTM_DQK),
               mk.reshape(B, T, MLSTM_HEADS, MLSTM_DQK),
               mv.reshape(B, T, MLSTM_HEADS, MLSTM_DV),
               mi + b_i, mf + b_f)
    hm = rmsnorm(hm, head_gain) * jax.nn.sigmoid(mo.reshape(B, T, MLSTM_HEADS, MLSTM_DV).astype(jnp.float32))
    hs = stick_breaking(sq.reshape(B, T, SB_HEADS, SB_DH),
                        sk.reshape(B, T, SB_HEADS, SB_DH),
                        sv.reshape(B, T, SB_HEADS, SB_DH))
    out = jnp.concatenate([hm.reshape(B, T, ML_V), hs.reshape(B, T, SB_W)], axis=-1).astype(h.dtype)
    return out @ w_out

def c_mixer(h, w_in, conv_w, a_log, dt_bias, head_gain, w_out):
    B, T, _ = h.shape
    qkv, gate, b, a = _split(h @ w_in, C_SIZES)
    qkv = jax.nn.silu(short_conv(qkv, conv_w))
    q, k, v = _split(qkv, (GDN_QK, GDN_QK, GDN_VW))
    q = l2norm(q.reshape(B, T, GDN_HEADS, GDN_DK))
    k = l2norm(k.reshape(B, T, GDN_HEADS, GDN_DK))
    v = v.reshape(B, T, GDN_HEADS, GDN_DV)
    beta = jax.nn.sigmoid(b.astype(jnp.float32))
    log_alpha = -jnp.exp(a_log.astype(jnp.float32)) * jax.nn.softplus(a.astype(jnp.float32) + dt_bias.astype(jnp.float32))
    o = gated_deltanet(q, k, v, beta, log_alpha)
    o = rmsnorm(o, head_gain) * jax.nn.silu(gate.reshape(B, T, GDN_HEADS, GDN_DV).astype(jnp.float32))
    return o.reshape(B, T, GDN_VW).astype(h.dtype) @ w_out

def mem_cross_attn(h, memn, wq, wk, wv, wo):
    B, T, _ = h.shape
    M = memn.shape[1]
    q = (h @ wq).reshape(B, T, XA_HEADS, XA_DH)
    k = (memn @ wk).reshape(B, M, XA_HEADS, XA_DH)
    v = (memn @ wv).reshape(B, M, XA_HEADS, XA_DH)
    s = jnp.einsum('bthd,bmhd->bhtm', q, k).astype(jnp.float32) * (XA_DH ** -0.5)
    p = jax.nn.softmax(s, axis=-1).astype(v.dtype)
    o = jnp.einsum('bhtm,bmhd->bthd', p, v).reshape(B, T, XA_HEADS * XA_DH)
    return o @ wo

def sq_relu_mlp(h, w1, w2):
    return jnp.square(jax.nn.relu(h @ w1)) @ w2

def first_inputs(seed: int = 0) -> dict:
    key = jax.random.key(seed)
    ks = jax.random.split(key, 32)
    f32 = jnp.float32

    def w(k, shape, fan_in):
        return jax.random.normal(k, shape, f32) * (fan_in ** -0.5)

    def gain(k, shape):
        return 1.0 + 0.02 * jax.random.normal(k, shape, f32)

    x = jax.random.normal(ks[0], (BATCH, SEQ, D_MODEL), f32)
    mem = jax.random.normal(ks[1], (BATCH, MEM_LEN, D_MODEL), f32)
    mix_norm = gain(ks[2], (DEPTH, D_MODEL))
    ab_w_in = w(ks[3], (N_EVEN, D_MODEL, AB_IN), D_MODEL)
    ab_b_i = 0.1 * jax.random.normal(ks[4], (N_EVEN, MLSTM_HEADS), f32)
    ab_b_f = jnp.linspace(3.0, 6.0, MLSTM_HEADS, dtype=f32)[None, :] + 0.1 * jax.random.normal(ks[5], (N_EVEN, MLSTM_HEADS), f32)
    ab_head_gain = gain(ks[6], (N_EVEN, MLSTM_HEADS, MLSTM_DV))
    ab_w_out = w(ks[7], (N_EVEN, AB_OUT, D_MODEL), AB_OUT)
    c_w_in = w(ks[8], (N_ODD, D_MODEL, C_IN), D_MODEL)
    c_conv_w = w(ks[9], (N_ODD, GDN_CONV, GDN_CONV_CH), GDN_CONV)
    c_a_log = jnp.log(jax.random.uniform(ks[10], (N_ODD, GDN_HEADS), f32, 1.0, 16.0))
    dt = jnp.exp(jax.random.uniform(ks[11], (N_ODD, GDN_HEADS), f32, float(np.log(1e-3)), float(np.log(1e-1))))
    c_dt_bias = dt + jnp.log(-jnp.expm1(-dt))
    c_head_gain = gain(ks[12], (N_ODD, GDN_DV))
    c_w_out = w(ks[13], (N_ODD, GDN_VW, D_MODEL), GDN_VW)
    xa_norm = gain(ks[14], (DEPTH, D_MODEL))
    mem_norm = gain(ks[15], (D_MODEL,))
    xa_wq = w(ks[16], (DEPTH, D_MODEL, D_MODEL), D_MODEL)
    xa_wk = w(ks[17], (DEPTH, D_MODEL, D_MODEL), D_MODEL)
    xa_wv = w(ks[18], (DEPTH, D_MODEL, D_MODEL), D_MODEL)
    xa_wo = w(ks[19], (DEPTH, D_MODEL, D_MODEL), D_MODEL)
    mlp_norm = gain(ks[20], (DEPTH, D_MODEL))
    mlp_w1 = w(ks[21], (DEPTH, D_MODEL, D_FF), D_MODEL)
    mlp_w2 = w(ks[22], (DEPTH, D_FF, D_MODEL), D_FF)
    final_norm = gain(ks[23], (D_MODEL,))
    return {'x': x, 'mem': mem, 'mix_norm': mix_norm,
            'ab_w_in': ab_w_in, 'ab_b_i': ab_b_i, 'ab_b_f': ab_b_f,
            'ab_head_gain': ab_head_gain, 'ab_w_out': ab_w_out,
            'c_w_in': c_w_in, 'c_conv_w': c_conv_w, 'c_a_log': c_a_log,
            'c_dt_bias': c_dt_bias, 'c_head_gain': c_head_gain, 'c_w_out': c_w_out,
            'xa_norm': xa_norm, 'mem_norm': mem_norm, 'xa_wq': xa_wq, 'xa_wk': xa_wk,
            'xa_wv': xa_wv, 'xa_wo': xa_wo, 'mlp_norm': mlp_norm, 'mlp_w1': mlp_w1,
            'mlp_w2': mlp_w2, 'final_norm': final_norm}

def first_block(x, mem, mix_norm, ab_w_in, ab_b_i, ab_b_f, ab_head_gain, ab_w_out,
              c_w_in, c_conv_w, c_a_log, c_dt_bias, c_head_gain, c_w_out,
              xa_norm, mem_norm, xa_wq, xa_wk, xa_wv, xa_wo,
              mlp_norm, mlp_w1, mlp_w2, final_norm):
    memn = rmsnorm(mem, mem_norm)
    for l in range(DEPTH):
        j = l // 2
        h = rmsnorm(x, mix_norm[l])
        if l % 2 == 0:
            x = x + ab_mixer(h, ab_w_in[j], ab_b_i[j], ab_b_f[j], ab_head_gain[j], ab_w_out[j])
        else:
            x = x + c_mixer(h, c_w_in[j], c_conv_w[j], c_a_log[j], c_dt_bias[j], c_head_gain[j], c_w_out[j])
        x = x + mem_cross_attn(rmsnorm(x, xa_norm[l]), memn, xa_wq[l], xa_wk[l], xa_wv[l], xa_wo[l])
        x = x + sq_relu_mlp(rmsnorm(x, mlp_norm[l]), mlp_w1[l], mlp_w2[l])
    return rmsnorm(x, final_norm)


N_MIXERS = 2
N_POOL_LAYERS = (DEPTH + 1) // 2
N_ATTN_LAYERS = DEPTH // 2

POOL_WINDOWS = (2, 4, 8, 16)
N_POOL_GROUPS = len(POOL_WINDOWS)
POOL_GC = D_MODEL // N_POOL_GROUPS

HEAD_DIM = 64
N_HEADS = D_MODEL // HEAD_DIM
N_KV_HEADS = 4
N_GROUPS = N_HEADS // N_KV_HEADS
WINDOW = 128
BLOCK = 128
QKV_DIM = (N_HEADS + 2 * N_KV_HEADS) * HEAD_DIM

D_FF_2 = 2816
CONV_W = 3

RMS_EPS = 1e-6


def rms_norm(x, g):
    xf = x.astype(jnp.float32)
    y = xf * lax.rsqrt(jnp.mean(xf * xf, axis=-1, keepdims=True) + RMS_EPS)
    return (y * g.astype(jnp.float32)).astype(x.dtype)

def alibi_slopes(n_heads):
    h = jnp.arange(1, n_heads + 1, dtype=jnp.float32)
    return jnp.exp2(-8.0 / n_heads * h)

def pool_mixer(h, w, b, scale):
    B, S, D = h.shape
    hf = h.astype(jnp.float32)
    csum = jnp.cumsum(hf, axis=1)
    t1 = jnp.arange(1, S + 1)
    outs = []
    for gi, win in enumerate(POOL_WINDOWS):
        sl = slice(gi * POOL_GC, (gi + 1) * POOL_GC)
        c = csum[..., sl]
        lo = jnp.pad(c, ((0, 0), (win, 0), (0, 0)))[:, :S]
        count = jnp.minimum(t1, win).astype(jnp.float32)
        mean = (c - lo) / count[None, :, None]
        outs.append(mean - hf[..., sl])
    p = jnp.stack(outs, axis=2).astype(h.dtype)
    y = jnp.einsum('bsgc,gcd->bsgd', p, w) + b
    return y.reshape(B, S, D) * scale

def swa_sink_attention(h, w_qkv, b_qkv, sinks, w_o):
    B, S, _ = h.shape
    nb = S // BLOCK
    qkv = h @ w_qkv + b_qkv
    q = qkv[..., :N_HEADS * HEAD_DIM].reshape(B, nb, BLOCK, N_KV_HEADS, N_GROUPS, HEAD_DIM)
    k = qkv[..., N_HEADS * HEAD_DIM:(N_HEADS + N_KV_HEADS) * HEAD_DIM].reshape(B, S, N_KV_HEADS, HEAD_DIM)
    v = qkv[..., (N_HEADS + N_KV_HEADS) * HEAD_DIM:].reshape(B, S, N_KV_HEADS, HEAD_DIM)

    def band(t):
        tp = jnp.pad(t, ((0, 0), (BLOCK, 0), (0, 0), (0, 0)))[:, :S]
        prev = tp.reshape(B, nb, BLOCK, N_KV_HEADS, HEAD_DIM)
        cur = t.reshape(B, nb, BLOCK, N_KV_HEADS, HEAD_DIM)
        return jnp.concatenate([prev, cur], axis=2)

    kb, vb = band(k), band(v)
    scores = jnp.einsum('bnqkgd,bnskd->bnkgqs', q, kb).astype(jnp.float32) * (HEAD_DIM ** -0.5)

    qi = jnp.arange(BLOCK)[:, None]
    kj = jnp.arange(2 * BLOCK)[None, :]
    dist = qi + BLOCK - kj
    key_pos = jnp.arange(nb)[:, None] * BLOCK - BLOCK + jnp.arange(2 * BLOCK)[None, :]
    mask = ((dist >= 0) & (dist < WINDOW))[None] & (key_pos >= 0)[:, None, :]

    slopes = alibi_slopes(N_HEADS).reshape(N_KV_HEADS, N_GROUPS)
    bias = -slopes[:, :, None, None] * dist.astype(jnp.float32)[None, None]
    scores = jnp.where(mask[None, :, None, None], scores + bias, -jnp.inf)

    sink = sinks.astype(jnp.float32).reshape(N_KV_HEADS, N_GROUPS)[None, None, :, :, None, None]
    m = jnp.maximum(jnp.max(scores, axis=-1, keepdims=True), sink)
    p = jnp.exp(scores - m)
    denom = jnp.sum(p, axis=-1, keepdims=True) + jnp.exp(sink - m)
    probs = (p / denom).astype(v.dtype)
    o = jnp.einsum('bnkgqs,bnskd->bnqkgd', probs, vb).reshape(B, S, N_HEADS * HEAD_DIM)
    return o @ w_o

def conv_glu_ffn(h, w_in, conv_w, conv_b, w_out):
    u = h @ w_in
    c = lax.conv_general_dilated(
        u, conv_w[:, None, :].astype(u.dtype), window_strides=(1,),
        padding=[(CONV_W - 1, 0)], dimension_numbers=('NWC', 'WIO', 'NWC'),
        feature_group_count=2 * D_FF_2) + conv_b
    a, g = c[..., :D_FF_2], c[..., D_FF_2:]
    return (a * jax.nn.silu(g)) @ w_out

def second_inputs(seed: int = 0) -> dict:
    key = jax.random.key(seed)
    ks = jax.random.split(key, 16)
    f32 = jnp.float32
    nrm = lambda k, shape, s: jax.random.normal(k, shape, f32) * s
    return {
        "x": nrm(ks[0], (BATCH, SEQ, D_MODEL), 1.0),
        "pool_w": nrm(ks[1], (N_POOL_LAYERS, N_POOL_GROUPS, POOL_GC, POOL_GC), POOL_GC ** -0.5),
        "pool_b": nrm(ks[2], (N_POOL_LAYERS, N_POOL_GROUPS, POOL_GC), 0.02),
        "pool_scale": 1.0 + nrm(ks[3], (N_POOL_LAYERS, D_MODEL), 0.05),
        "attn_w_qkv": nrm(ks[4], (N_ATTN_LAYERS, D_MODEL, QKV_DIM), D_MODEL ** -0.5),
        "attn_b_qkv": nrm(ks[5], (N_ATTN_LAYERS, QKV_DIM), 0.02),
        "attn_sinks": nrm(ks[6], (N_ATTN_LAYERS, N_HEADS), 0.5),
        "attn_w_o": nrm(ks[7], (N_ATTN_LAYERS, N_HEADS * HEAD_DIM, D_MODEL), (N_HEADS * HEAD_DIM) ** -0.5),
        "norm_mix": 1.0 + nrm(ks[8], (DEPTH, D_MODEL), 0.05),
        "norm_ffn": 1.0 + nrm(ks[9], (DEPTH, D_MODEL), 0.05),
        "ffn_w_in": nrm(ks[10], (DEPTH, D_MODEL, 2 * D_FF_2), D_MODEL ** -0.5),
        "ffn_conv_w": nrm(ks[11], (DEPTH, CONV_W, 2 * D_FF_2), CONV_W ** -0.5),
        "ffn_conv_b": nrm(ks[12], (DEPTH, 2 * D_FF_2), 0.02),
        "ffn_w_out": nrm(ks[13], (DEPTH, D_FF_2, D_MODEL), D_FF_2 ** -0.5),
        "norm_f": 1.0 + nrm(ks[14], (D_MODEL,), 0.05),
    }

def second_block(x, pool_w, pool_b, pool_scale, attn_w_qkv, attn_b_qkv, attn_sinks, attn_w_o,
              norm_mix, norm_ffn, ffn_w_in, ffn_conv_w, ffn_conv_b, ffn_w_out, norm_f):
    h = x
    for i in range(DEPTH):
        hn = rms_norm(h, norm_mix[i])
        j = i // N_MIXERS
        if i % N_MIXERS == 0:
            mix = pool_mixer(hn, pool_w[j], pool_b[j], pool_scale[j])
        else:
            mix = swa_sink_attention(hn, attn_w_qkv[j], attn_b_qkv[j], attn_sinks[j], attn_w_o[j])
        h = h + mix
        hn = rms_norm(h, norm_ffn[i])
        h = h + conv_glu_ffn(hn, ffn_w_in[i], ffn_conv_w[i], ffn_conv_b[i], ffn_w_out[i])
    return rms_norm(h, norm_f)


def setup_inputs(seed=0):
    out = dict(first_inputs(seed))
    for name, value in second_inputs(seed + 1).items():
        if name != "x":
            out[name + "_2"] = value
    return out


def reference(
    x, mem, mix_norm, ab_w_in, ab_b_i, ab_b_f, ab_head_gain, ab_w_out, c_w_in, c_conv_w,
    c_a_log, c_dt_bias, c_head_gain, c_w_out, xa_norm, mem_norm, xa_wq, xa_wk, xa_wv, xa_wo,
    mlp_norm, mlp_w1, mlp_w2, final_norm, pool_w_2, pool_b_2, pool_scale_2, attn_w_qkv_2,
    attn_b_qkv_2, attn_sinks_2, attn_w_o_2, norm_mix_2, norm_ffn_2, ffn_w_in_2, ffn_conv_w_2,
    ffn_conv_b_2, ffn_w_out_2, norm_f_2,
):
    x = first_block(
        x, mem, mix_norm, ab_w_in, ab_b_i, ab_b_f, ab_head_gain, ab_w_out, c_w_in, c_conv_w,
        c_a_log, c_dt_bias, c_head_gain, c_w_out, xa_norm, mem_norm, xa_wq, xa_wk, xa_wv, xa_wo,
        mlp_norm, mlp_w1, mlp_w2, final_norm,
    )
    return second_block(
        x, pool_w_2, pool_b_2, pool_scale_2, attn_w_qkv_2, attn_b_qkv_2, attn_sinks_2,
        attn_w_o_2, norm_mix_2, norm_ffn_2, ffn_w_in_2, ffn_conv_w_2, ffn_conv_b_2, ffn_w_out_2,
        norm_f_2,
    )


_drawn_inputs = setup_inputs


def setup_inputs(seed=0):
    import zlib

    import numpy as np

    out = dict(_drawn_inputs(seed))
    spreads = {}
    factors = {'ab_b_i': 8.0,
     'ab_head_gain': 5.332,
     'c_head_gain': 7.505,
     'xa_norm': 8.0,
     'mem_norm': 8.0,
     'pool_b_2': 2.81,
     'attn_b_qkv_2': 4.14,
     'ffn_conv_b_2': 3.289}
    for name, (base, spread) in spreads.items():
        noise = np.random.default_rng([zlib.crc32(name.encode()), seed]).standard_normal(out[name].shape)
        drawn = base * np.exp(spread * noise) if base else spread * noise
        out[name] = jnp.asarray(drawn.astype(out[name].dtype))
    for name, factor in factors.items():
        out[name] = (out[name] * factor).astype(out[name].dtype)
    return out
```

```python
import numpy as np

import concourse.bass as bass
from concourse import mybir
from contextlib import ExitStack

F32 = mybir.dt.float32
F32R = mybir.dt.float32r
ACT = mybir.ActivationFunctionType
ALU = mybir.AluOpType
AX = mybir.AxisListType
ds = bass.ds

P = 128
T = 256
TT = T // P
D = 1024
KT = D // P
RING = 4
NEG = -1e30
EPS = 1e-6
LEVELS = 7
WINDOWS = (2, 4, 8, 16)
SWA_HEADS = 16
FF = 4096
GLU = 2816
HID0 = {"mlp0": 0, "mlp1": FF // 512, "ffn0": 2 * (FF // 512), "ffn1": 2 * (FF // 512) + GLU // 256}
NORMS = ["mem", "ab", "xq0", "mlp0", "gdn", "xq1", "mlp1", "pool", "ffn0", "swa", "ffn1"]
XN_LAST = 2 * len(NORMS) + 2
POOL_SET = {"start": 3, "ab": 4, "gdn": 5, "ffn0": 6, "ffn1": 7}
MISC = 16 * 11


def shape_constants():
    i, j = np.arange(P)[:, None], np.arange(P)[None, :]
    parts = {}
    parts["ident"] = i == j
    parts["ones"] = np.ones((P, P))
    parts["suffix"] = i >= j
    parts["causal_min"] = np.concatenate([np.where(i <= j, 0, NEG), np.zeros((P, P))], 1)
    parts["strict"] = i < j
    parts["strict_min"] = np.where(i < j, 0, NEG)
    for b in range(LEVELS):
        parts[f"level{b}"] = ((i >> (b + 1)) == (j >> (b + 1))) & (((i >> b) & 1) == 0) & (((j >> b) & 1) == 1)
    for h in range(8):
        parts[f"select{h}"] = np.repeat(i == h, P, 1)
    s, t = np.arange(T)[:, None], np.arange(T)[None, :]
    for w in WINDOWS:
        m = ((s <= t) & (s > t - w)) / np.minimum(t + 1, w) - (s == t)
        parts[f"pool{w}"] = np.concatenate([m[:P], m[P:, P:]], 1)
    dist = np.concatenate([i - j, i + P - j, i - j], 1)
    parts["dist"] = dist
    parts["band_add"] = np.where((dist >= 0) & (dist < P), 0, NEG)
    at, arrays, n = {}, [], 0
    for name, v in parts.items():
        at[name] = (n, v.shape[1])
        arrays.append(v.astype(np.float32))
        n += v.shape[1]
    return np.ascontiguousarray(np.concatenate(arrays, 1)), at


CONST, CONST_AT = shape_constants()

VECTORS = [
    [("mem_norm", 0, 8), ("mix_norm", 0, 16), ("xa_norm", 0, 16), ("mlp_norm", 0, 16), ("norm_mix_2", 0, 16),
     ("ab_head_gain", 0, 4), ("c_head_gain", 0, 1), ("attn_b_qkv_2", 0, 12)],
    [("c_conv_w", 0, 96)],
    [("ffn_conv_w_2", 0, 88)],
    [("ffn_conv_w_2", 88, 44), ("ffn_conv_b_2", 0, 44)],
    [("ffn_conv_w_2", 132, 88)],
    [("ffn_conv_w_2", 220, 44), ("ffn_conv_b_2", 44, 44)],
]

STREAM = [("memkv", 32), ("ab_in", 24), ("ab_o", 8), ("xq0", 8), ("xo0", 8), ("mlp0", 64),
          ("gdn_in", 32), ("gdn_o", 8), ("xq1", 8), ("xo1", 8), ("mlp1", 64),
          ("pool", 2), ("ffn0", 66), ("qkv", 12), ("swa_o", 8), ("ffn1", 66)]
UNIT0, UNITS = {}, 0
for _name, _n in STREAM:
    UNIT0[_name] = UNITS
    UNITS += _n

TURNS = ["mem", "ab", "ab_o", "xq0", "xo0", "mlp0", "gdn", "gdn_o", "xq1", "xo1", "mlp1", "pool", "ffn0", "swa",
         "swa_o", "ffn1"]
ROOTS = [("mem", 2, 2, 1 / D), ("ab", 2, 2, 1 / D), ("ab_heads", 1, 8, 1 / 128), ("xq0", 2, 2, 1 / D),
         ("mlp0", 2, 2, 1 / D), ("gdn", 2, 2, 1 / D), ("gdn_heads", 1, 16, 1 / 128), ("xq1", 2, 2, 1 / D),
         ("mlp1", 2, 2, 1 / D), ("final1", 2, 2, 1 / D), ("pool", 2, 2, 1 / D), ("ffn0", 2, 2, 1 / D),
         ("swa", 2, 2, 1 / D), ("ffn1", 2, 2, 1 / D), ("final2", 2, 2, 1 / D)]
X_COUNT = {"ab": 0, "xq0": 2, "mlp0": 4, "gdn": 6, "xq1": 8, "mlp1": 10, "final1": 12, "pool": 14, "ffn0": 16,
           "swa": 18, "ffn1": 20, "final2": 22}
EVACS = [("memkv", 8), ("ab_in", 6), ("xq0", 2), ("gdn_in", 8), ("xq1", 2), ("qkv", 3)]
EVAC0, _n = {}, 0
for _name, _k in EVACS:
    EVAC0[_name] = _n
    _n += _k


def root_at(name):
    n = 0
    for k, (who, signals, _, _) in enumerate(ROOTS):
        n += signals
        if who == name:
            return n, k
    raise KeyError(name)


class Order:

    def __init__(self, eng, sem):
        self.eng, self.sem, self.count, self.turn = eng, sem, 0, 0

    def __call__(self, ins):
        ins.then_inc(self.sem, 1)
        self.count += 1
        self.eng.wait_ge(self.sem, self.turn + self.count)

    def loop(self, i, per):
        self.turn, self.start, self.per = i * per, self.count, per

    def end(self, turns):
        assert self.count - self.start == self.per, (self.count - self.start, self.per)
        self.turn, self.count = 0, self.start + turns * self.per


def program(nc, a, out):
    ctx = ExitStack()
    with ctx:
        first = (nc.sbuf_base + 63) // 64 * 64
        SLAB = 53120
        ctx.enter_context(nc.sbuf_tensor("slab", [P, SLAB], F32))
        place = [0]

        def at(name, shape, word, dt=F32):
            n = int(np.prod(shape))
            assert word + n <= SLAB, (name, word + n)
            return nc.alloc_sbuf_tensor_at(name, [P] + list(shape), dt, offset=first + 4 * word)

        def sb(name, shape, dt=F32):
            t = at(name, shape, place[0], dt)
            place[0] += (int(np.prod(shape)) + 7) // 8 * 8
            return t

        PS = ctx.enter_context(nc.psum_tensor("PS", [P, 8, 512], F32))
        x = sb("x", [TT, D])
        xn_at = place[0]
        xn = sb("xn", [TT, D])
        xt_at = place[0]
        XTh = sb("XTh", [KT, T], F32R)
        XTl = sb("XTl", [KT, T], F32R)
        w_raw = sb("w_raw", [RING, 2, 512])
        w_hi = sb("w_hi", [RING, 2, 512], F32R)
        w_lo = sb("w_lo", [RING, 2, 512], F32R)
        const = sb("const", [CONST.shape[1]])
        cols = sb("cols", [len(VECTORS), P])
        zeros = sb("zeros", [512], F32R)
        gate_w = sb("gate_w", [2, KT, 40])
        ss = sb("ss", [16])
        var = sb("var", [16])
        rstd = sb("rstd", [16])
        neghalf = sb("neghalf", [16])
        eps_col = sb("eps_col", [1])
        gbias = sb("gbias", [8])
        ffn_gain = sb("ffn_gain", [2, KT])
        sinks = sb("sinks", [SWA_HEADS])
        vbias = sb("vbias", [256])
        K1 = sb("K1", [KT, T])
        V1 = sb("V1", [TT, D])
        arena_at = place[0]
        shared_at = SLAB - 4096
        K0 = at("K0", [KT, T], shared_at)
        V0 = at("V0", [TT, D], shared_at + 2048)
        bc = at("bc", [4, D], shared_at)
        hid_hi = at("hid_hi", [2, 4, T], shared_at - 4096, F32R)
        hid_lo = at("hid_lo", [2, 4, T], shared_at - 2048, F32R)
        K_of, V_of = [K0, K1], [V0, V1]

        class Arena:

            def __init__(self, tag, start=arena_at, end=shared_at):
                self.tag, self.word, self.end = tag, start, end

            def __call__(self, name, *shape):
                t = at(f"{self.tag}_{name}", list(shape), self.word)
                self.word += (int(np.prod(shape)) + 7) // 8 * 8
                assert self.word <= self.end, (name, self.word - self.end)
                return t

        A = Arena("start")
        vec_rows = A("vec_rows", len(VECTORS), P)

        A = Arena("ab")
        ab_qk = A("qk", 4, T)
        ab_v = A("v", TT, 4, 132)
        ab_og = A("og", TT, 512)
        sb_q, sb_k = A("sq", 4, T), A("sk", 4, T)
        sb_v = A("sv", TT, 512)
        ab_rows = A("rows", 13, T)
        acol = A("acol", 2, 4)
        mcol = A("mcol", 2, 4)
        emcol = A("emcol", 2, 4)
        decay_at = A.word
        decay = A("decay", 4, 384)
        prob = A("prob", 4, 384)
        sb_zs, sb_sp = A("zs", 4, 384), A("sp", 4, 384)
        sb_ln = prob
        rden = A("rden", 4, 2)
        hsq = at("ab_hsq", [TT, 512], decay_at)
        hmix = xn

        A = Arena("xa")
        xa_q = A("q", KT, T)
        xa_p = A("p", 4, TT, T)
        xa_pt = A("pt", 4, 2, T)
        xa_m, xa_nm, xa_s, xa_r = A("m", 8), A("nm", 8), A("s", 8), A("r", 8)

        A = Arena("mlp", end=shared_at - 4096)
        relu = A("relu", 2, 4, T)
        relu2 = A("relu2", 2, 4, T)

        A = Arena("glu", end=shared_at - 4096)
        glu_pad = A("pad", 2, 4, 264)
        glu_acc = A("acc", 2, 4, T)
        glu_silu = A("silu", 2, 2, T)
        glu_prod = A("prod", 2, 2, T)

        A = Arena("gd", end=SLAB)
        gd_qkv = A("qkv", 24, T)
        gd_gate = A("gate", TT, D)
        gd_E = A("E", 2, 8, P)
        over = A.word
        gd_U = A("U", 2, 8, P)
        gd_X = A("X", 2, 8, P)
        gd_XT = A("XT", 2, 8, P)
        gd_bv = A("bv", 2, 8, P)
        gd_kd = A("kd", 8, P)
        gd_um = at("gd_um", [2, 8, P], arena_at + 16 * T)
        A = Arena("gdc", start=over, end=SLAB)
        gd_pad = A("pad", 2, 4, 264)
        gd_acc = A("acc", 2, 4, T)
        gd_sq = at("gd_sq", [8, T], over + 3 * 2048)
        gd_rows = at("gd_rows", [8, T], xn_at)
        gd_Y = at("gd_Y", [2, 8, P], xt_at)
        gd_S = at("gd_S", [8, P], xt_at + 2048)
        gd_vn = at("gd_vn", [8, P], xt_at + 3072)
        gd_o = xn
        gd_osqt = at("gd_osqt", [2, D], xt_at)
        A = Arena("gds", start=arena_at + 19472, end=SLAB)
        gd_gcol, gd_bcol = A("gcol", 2, 8), A("bcol", 2, 8)
        gd_eg, gd_beg, gd_kdc, gd_gl = A("eg", 8), A("beg", 8), A("kdc", 8), A("gl", 8)
        gd_nea = A("nea", 8)

        A = Arena("swa")
        sw_q = A("q", KT, T)
        sw_k = A("k", 4, T)
        sw_v = A("v", TT, T)
        sw_s = A("s", 4, 384)
        sw_pt = A("pt", 16, 384)
        sw_m, sw_nm, sw_sum = A("m", 2, 16), A("nm", 2, 16), A("sum", 2, 16)
        sw_es, sw_r = A("es", 2, 16), A("r", 2, 16)
        sw_qb = A("qb", 8)

        def C(name):
            n, w = CONST_AT[name]
            return const[:, n:n + w]

        def vec_at(name, k):
            for b, rows in enumerate(VECTORS):
                n = 0
                for who, r0, count in rows:
                    if who == name and r0 <= k < r0 + count:
                        return b, n + k - r0
                    n += count
            raise KeyError(name)

        def vec(name, k, i=0):
            b, n = vec_at(name, k)
            return cols[:, b, ds(n + i, 1)] if not isinstance(i, int) else cols[:, b, n + i:n + i + 1]

        ident, ones = C("ident"), C("ones")
        one_col = ones[:, 0:1]

        def f32(t):
            return t.bitcast(F32)

        def sem(name):
            return ctx.enter_context(nc.semaphore(name))

        raw_landed = [sem(f"raw_landed{s}") for s in range(RING)]
        hi_done, lo_done, w_used = sem("hi_done"), sem("lo_done"), sem("w_used")
        const_landed, vec_landed, x_landed = sem("const_landed"), sem("vec_landed"), sem("x_landed")
        mem_landed, misc_landed, bc_landed = sem("mem_landed"), sem("misc_landed"), sem("bc_landed")
        out_landed, gate_zeroed, pool_set = sem("out_landed"), sem("gate_zeroed"), sem("pool_set")
        vec_turned, vec_kept = sem("vec_turned"), sem("vec_kept")
        x_updates, evac_act, v_kept = sem("x_updates"), sem("evac_act"), sem("v_kept")
        sq_done, rstd_done, xn_ready = sem("sq_done"), sem("rstd_done"), sem("xn_ready")
        turned, xt_hi, xt_lo = sem("turned"), sem("xt_hi"), sem("xt_lo")
        act_order, dve_order, pool_order = sem("act_order"), sem("dve_order"), sem("pool_order")
        hid_in, hid_hi_done, hid_lo_done = sem("hid_in"), sem("hid_hi_done"), sem("hid_lo_done")
        glu_in, glu_conv, glu_silued, glu_mult = sem("glu_in"), sem("glu_conv"), sem("glu_silued"), sem("glu_mult")
        (ab_gates, ab_f, ab_lnf, ab_rows_done, ab_turned, ab_args, ab_decayed, ab_scores, ab_probs, ab_outs, ab_norm,
         ab_sq, ab_mixed) = [sem(f"ab_{n}_s") for n in (
             "gates", "f", "lnf", "rows", "turned", "args", "decayed", "scores", "probs", "outs", "norm", "sq", "mixed")]
        sb_z, sb_kept, sb_lned, sb_sped, sb_cum, sb_arg, sb_w, sb_out = [
            sem(f"sb_{n}_s") for n in ("z", "kept", "ln", "sp", "cum", "arg", "w", "out")]
        xa_scores, xa_max, xa_exp, xa_probs, xa_turned, xa_pt_act, xa_pt_dve = [
            sem(f"xa_{n}_s") for n in ("scores", "max", "exp", "probs", "turned", "pt_act", "pt_dve")]
        (gd_padded, gd_conv, gd_gates_s, gd_f, gd_lnf, gd_rows_s, gd_sqd, gd_sums, gd_rooted, gd_normed, gd_colt,
         gd_bcast, gd_args, gd_decayed, gd_bb, gd_kk, gd_qk, gd_vt, gd_kt, gd_made, gd_masked, gd_yps, gd_ysb, gd_xps,
         gd_xnew, gd_fin_pe, gd_fin_act, gd_fin_dve, gd_mixed, gd_osq_s) = [sem(f"gd_{n}_s") for n in (
             "padded", "conv", "gates", "f", "lnf", "rows", "sqd", "sums", "rooted", "normed", "colt", "bcast", "args",
             "decayed", "bb", "kk", "qk", "vt", "kt", "made", "masked", "yps", "ysb", "xps", "xnew", "fin_pe",
             "fin_act", "fin_dve", "mixed", "osq")]
        sw_scores, sw_max, sw_exp, sw_probs, sw_turned, sw_pted, sw_den = [
            sem(f"sw_{n}_s") for n in ("scores", "max", "exp", "probs", "turned", "pted", "den")]

        block = ctx.enter_context(nc.Block())

        def slot_of(u, i, per):
            assert per % RING == 0
            return u % RING, u + per * i, u // RING + (per // RING) * i


        @block.sync
        def _(sp):
            def load(u, src, i=0, per=0, halves=False):
                slot, n, _ = slot_of(u, i, per)
                if u >= RING:
                    sp.wait_ge(lo_done, n - RING + 1)
                dst = w_raw[:, slot].rearrange("p k (h n) -> p (k h) n", h=2) if halves else w_raw[:, slot]
                sp.dma_start(dst, src).then_inc(raw_landed[slot], 16)

            def rows_of(W, k, c):
                return W.rearrange("(k p) n -> p k n", p=P)[:, ds(k, 2), ds(c, 512)]

            def load_chunk(u, W, c, i=0, per=0):
                for j in range(4):
                    load(u + j, rows_of(W, 2 * j, c), i, per)

            def load_square(u, W):
                with sp.Fori(0, 2) as i:
                    load_chunk(u, W, i * 512, i, 4)

            def load_wide(u0, n, wu, load_first, load_second):
                per = 2 * (4 + wu)
                load_first(u0, 0, 0, 0)
                pairs = (n - 1) // 2
                with sp.Fori(0, pairs) as i:
                    for q in range(2):
                        u = u0 + 4 + q * (4 + wu)
                        load_first(u, q + 1 + 2 * i, i, per)
                        load_second(u + 4, q + 2 * i, i, per)
                for c in range(2 * pairs, n):
                    u = u0 + 4 + c * (4 + wu)
                    if c + 1 < n:
                        load_first(u, c + 1, 0, 0)
                        u += 4
                    load_second(u, c, 0, 0)

            def load_mlp(u0, W1, W2):
                load_wide(u0, FF // 512, 4,
                          lambda u, c, i, per: load_chunk(u, W1, c * 512, i, per),
                          lambda u, c, i, per: [load(u + 2 * k + h, rows_of(W2, c * 4 + 2 * k, h * 512), i, per)
                                                for k in range(2) for h in range(2)])

            def load_glu(u0, W1, W2):
                W = W1.rearrange("(p k) (h n) -> p (k h) n", p=P, h=2)

                def first_layer(u, c, i, per):
                    for j in range(4):
                        load(u + j, W[:, 4 * j:4 * j + 4, ds(c * 256, 256)], i, per, halves=True)
                load_wide(u0, GLU // 256, 2, first_layer,
                          lambda u, c, i, per: [load(u + h, rows_of(W2, c * 2, h * 512), i, per) for h in range(2)])

            sp.dma_start(const[:, :], a["const"]).then_inc(const_landed, 16)
            sp.dma_start(xn[:, :, :], a["mem"][0].rearrange("(t p) n -> p t n", p=P)).then_inc(mem_landed, 16)
            for b, rows in enumerate(VECTORS):
                n = 0
                for who, r0, count in rows:
                    src = a[who]
                    if len(src.shape) == 3:
                        src = src.rearrange("a b c -> (a b c)")
                    elif len(src.shape) == 2:
                        src = src.rearrange("a b -> (a b)")
                    src = src.rearrange("(r c) -> r c", c=P)[r0:r0 + count, :]
                    sp.dma_start(vec_rows[n:n + count, b, :], src).then_inc(vec_landed, 16)
                    n += count
            load_chunk(0, a["xa_wk"][0], 0)
            sp.dma_start(x[:, :, :], a["x"][0].rearrange("(t p) n -> p t n", p=P)).then_inc(x_landed, 16)
            sp.wait_ge(gate_zeroed, 1)
            abg = a["ab_w_in"][0].rearrange("(k p) n -> p k n", p=P)
            cg = a["c_w_in"][0].rearrange("(k p) n -> p k n", p=P)
            with nc.allow_non_contiguous_dma("gate columns and per-partition values"):
                for dst, src in (
                        (gate_w[:, 0, :, 0:4], abg[:, :, 1536:1540]), (gate_w[:, 0, :, 32:36], abg[:, :, 1540:1544]),
                        (gate_w[:, 1, :, 0:8], cg[:, :, 4096:4104]), (gate_w[:, 1, :, 32:40], cg[:, :, 4104:4112]),
                        (gbias[0:4, 0:1], a["ab_b_i"].rearrange("a n -> n a")),
                        (gbias[32:36, 0:1], a["ab_b_f"].rearrange("a n -> n a")),
                        (gbias[0:8, 1:2], a["c_a_log"].rearrange("a n -> n a")),
                        (gbias[32:40, 1:2], a["c_dt_bias"].rearrange("a n -> n a")),
                        (ffn_gain[:, :, :], a["norm_ffn_2"].rearrange("l (p k) -> p l k", p=P)),
                        (sinks[:, :], a["attn_sinks_2"].broadcast_to([P, SWA_HEADS])),
                        (vbias[:, :], a["attn_b_qkv_2"][:, 1280:1536].broadcast_to([P, 256]))):
                    sp.dma_start(dst, src).then_inc(misc_landed, 16)
            load_chunk(4, a["xa_wk"][0], 512)
            load_square(8, a["xa_wv"][0])
            load_square(16, a["xa_wk"][1])
            load_square(24, a["xa_wv"][1])

            def ab():
                for k, c in enumerate((0, 512, 1024, 1544, 2056, 2568)):
                    load_chunk(UNIT0["ab_in"] + 4 * k, a["ab_w_in"][0], c)
                load_square(UNIT0["ab_o"], a["ab_w_out"][0])

            def cross(l):
                load_square(UNIT0[f"xq{l}"], a["xa_wq"][l])
                load_square(UNIT0[f"xo{l}"], a["xa_wo"][l])
                if l == 1:
                    sp.wait_ge(x_updates, X_COUNT["xq1"])
                    for k, who in enumerate(("final_norm", "norm_f_2", "pool_b_2", "pool_scale_2")):
                        src = a[who]
                        if len(src.shape) == 3:
                            src = src.rearrange("a b c -> a (b c)")
                        elif len(src.shape) == 1:
                            src = src.rearrange("(a n) -> a n", a=1)
                        sp.dma_start(bc[:, k, :], src.broadcast_to([P, D])).then_inc(bc_landed, 16)

            def gdn():
                with sp.Fori(0, 8) as i:
                    load_chunk(UNIT0["gdn_in"], a["c_w_in"][0], i * 512, i, 4)
                load_square(UNIT0["gdn_o"], a["c_w_out"][0])

            def pool():
                for k in range(2):
                    u = UNIT0["pool"] + k
                    sp.wait_ge(lo_done, u - RING + 1)
                    sp.dma_start(w_raw[:, u % RING].rearrange("p g (k n) -> p (g k) n", k=2),
                                 a["pool_w_2"][0, 2 * k:2 * k + 2].rearrange("g (k p) n -> p (g k) n", p=P))\
                        .then_inc(raw_landed[u % RING], 16)

            def swa():
                with sp.Fori(0, 3) as i:
                    load_chunk(UNIT0["qkv"], a["attn_w_qkv_2"][0], i * 512, i, 4)
                load_square(UNIT0["swa_o"], a["attn_w_o_2"][0])

            ab()
            cross(0)
            load_mlp(UNIT0["mlp0"], a["mlp_w1"][0], a["mlp_w2"][0])
            gdn()
            cross(1)
            load_mlp(UNIT0["mlp1"], a["mlp_w1"][1], a["mlp_w2"][1])
            pool()
            load_glu(UNIT0["ffn0"], a["ffn_w_in_2"][0], a["ffn_w_out_2"][0])
            swa()
            load_glu(UNIT0["ffn1"], a["ffn_w_in_2"][1], a["ffn_w_out_2"][1])
            sp.wait_ge(xn_ready, XN_LAST)
            sp.dma_start(out[0].rearrange("(t p) n -> p t n", p=P), xn[:, :, :]).then_inc(out_landed, 16)
            sp.wait_ge(out_landed, 16)

        @block.gpsimd
        def _(pool):
            order = Order(pool, pool_order)
            pool.memset(gate_w[:, :, :, :], 0.0).then_inc(gate_zeroed, 1)
            pool.memset(f32(zeros[:, :]), 0.0).then_inc(pool_set, 1)
            pool.memset(neghalf[:, :], -0.5).then_inc(pool_set, 1)
            pool.memset(eps_col[:, :], EPS).then_inc(pool_set, 1)
            pool.wait_ge(pool_set, POOL_SET["start"])

            def root(name):
                signals, k = root_at(name)
                _, _, n, scale = ROOTS[k]
                pool.wait_ge(sq_done, signals)
                order(pool.tensor_scalar(var[:, :n], ss[:, :n], scale, EPS, ALU.mult, ALU.add))
                pool.tensor_tensor(rstd[:, :n], var[:, :n], neghalf[:, :n], ALU.pow).then_inc(rstd_done, 1)

            root("mem")
            pool.wait_ge(vec_kept, 1)
            pool.memset(ab_v[:, :, :, 128:129], 1.0).then_inc(pool_set, 1)
            root("ab")
            root("ab_heads")
            root("xq0")
            root("mlp0")
            pool.wait_ge(x_updates, X_COUNT["gdn"])
            pool.memset(gd_pad[:, :, :, 0:3], 0.0).then_inc(pool_set, 1)
            root("gdn")
            root("gdn_heads")
            root("xq1")
            root("mlp1")
            root("final1")
            root("pool")
            pool.wait_ge(x_updates, X_COUNT["ffn0"])
            pool.memset(glu_pad[:, :, :, 0:2], 0.0).then_inc(pool_set, 1)
            root("ffn0")
            root("swa")
            pool.wait_ge(x_updates, X_COUNT["ffn1"])
            pool.memset(glu_pad[:, :, :, 0:2], 0.0).then_inc(pool_set, 1)
            root("ffn1")
            root("final2")

        @block.scalar
        def _(act):
            order = Order(act, act_order)
            nxt = [0]

            def split(u, i=0, per=0):
                slot, n, uses = slot_of(u, i, per)
                if u >= RING:
                    act.wait_ge(w_used, n - RING + 1)
                act.wait_ge(raw_landed[slot], 16 * uses + 16)
                act.activation(w_hi[:, slot], w_raw[:, slot], ACT.Copy).then_inc(hi_done, 1)

            def splits(n):
                for _ in range(n):
                    if nxt[0] < UNITS:
                        split(nxt[0])
                    nxt[0] += 1

            def chunk_done(u, i=0, per=0):
                act.wait_ge(w_used, u + per * i + 1)

            def squares(src, dst=None):
                for t in range(TT):
                    act.activation(xn[:, t] if dst is None else dst[:, 4 * t:4 * t + 4].rearrange("p k t -> p (k t)"), src[:, t], ACT.Square,
                                   accum_out=ss[:, t:t + 1]).then_inc(sq_done, 1)

            def activations(turn, gain):
                n = TURNS.index(turn)
                for b in range(4):
                    act.wait_ge(turned, 4 * n + b + 1)
                    for k in (2 * b, 2 * b + 1):
                        act.activation(XTh[:, k], PS[:, 4 + b, (k % 2) * T:(k % 2) * T + T], ACT.Copy,
                                       scale=gain(k)).then_inc(xt_hi, 1)

            def norm(name, gain):
                act.wait_ge(x_updates, X_COUNT[name])
                squares(x)
                activations(name, gain)

            def square_evac(u0, evac, n=2):
                assert nxt[0] == u0 + RING, (nxt[0], u0)
                with act.Fori(0, n) as i:
                    for j in range(3):
                        split(u0 + RING + j, i, 4)
                    chunk_done(u0 + 3, i, 4)
                    evac(i).then_inc(evac_act, 1)
                    split(u0 + RING + 3, i, 4)
                nxt[0] += 4 * n

            def to_features(dst):
                return lambda i: act.activation(dst[:, ds(4 * i, 4), :].rearrange("p (b k) t -> p b k t", b=2),
                                                PS[:, ds(2 * i, 2), :].rearrange("p b (k t) -> p b k t", k=2), ACT.Copy)

            def to_tokens(dst, func=ACT.Copy):
                return lambda i: act.activation(dst[:, :, ds(512 * i, 512)], PS[:, ds(2 * i, 2), :], func)

            splits(4)
            act.wait_ge(mem_landed, 16)
            squares(xn, dst=K0)
            act.wait_ge(vec_kept, 1)
            activations("mem", lambda k: vec("mem_norm", k))
            for k, (dst, kind) in enumerate(((K0, to_features), (V0, to_tokens), (K1, to_features), (V1, to_tokens))):
                square_evac(8 * k, kind(dst))

            def ab():
                act.wait_ge(x_landed, 16)
                norm("ab", lambda k: vec("mix_norm", k))
                u = UNIT0["ab_in"]
                splits(3)
                chunk_done(u + 3)
                act.activation(ab_qk[:, 0:2], PS[:, 0, :].rearrange("p (k t) -> p k t", k=2), ACT.Copy)
                act.activation(ab_qk[:, 2:4], PS[:, 1, :].rearrange("p (k t) -> p k t", k=2), ACT.Copy,
                               scale=64 ** -0.5).then_inc(evac_act, 1)
                splits(1)
                act.wait_ge(ab_f, 1)
                act.activation(ab_rows[0:4, 2], ab_rows[0:4, 0], ACT.Tanh)
                order(act.activation(ab_rows[0:4, 3], ab_rows[0:4, 1], ACT.Abs))
                order(act.activation(ab_rows[0:4, 4], ab_rows[0:4, 3], ACT.Exp, scale=-1.0))
                act.activation(ab_rows[0:4, 5], ab_rows[0:4, 4], ACT.Ln, bias=1.0).then_inc(ab_lnf, 1)
                splits(3)
                chunk_done(u + 7)
                act.activation(ab_v[:, :, :, 0:128], PS[:, 2:4, :].rearrange("p t (h d) -> p t h d", h=4),
                               ACT.Copy).then_inc(evac_act, 1)
                splits(1)
                splits(3)
                chunk_done(u + 11)
                act.activation(ab_og[:, :, :], PS[:, 0:2, :], ACT.Sigmoid).then_inc(evac_act, 1)
                splits(1)
                act.wait_ge(ab_args, 1)
                act.activation(emcol[:, :, :], mcol[:, :, :], ACT.Exp)
                act.activation(decay[:, :, :], decay[:, :, :], ACT.Exp).then_inc(ab_decayed, 1)
                splits(3)
                chunk_done(u + 15)
                act.activation(sb_q[:, :, :].rearrange("p (b k) t -> p b k t", b=2),
                               PS[:, 2:4, :].rearrange("p b (k t) -> p b k t", k=2), ACT.Copy,
                               scale=128 ** -0.5).then_inc(evac_act, 1)
                splits(1)
                act.wait_ge(ab_norm, 1)
                act.activation(hsq[:, :, :], hmix[:, :, 0:512], ACT.Square).then_inc(ab_sq, 1)
                splits(3)
                chunk_done(u + 19)
                act.activation(sb_k[:, :, :].rearrange("p (b k) t -> p b k t", b=2),
                               PS[:, 0:2, :].rearrange("p b (k t) -> p b k t", k=2), ACT.Copy).then_inc(evac_act, 1)
                splits(1)
                act.wait_ge(sb_kept, 1)
                order(act.activation(sb_ln[:, :, :], sb_zs[:, :, :], ACT.Abs))
                order(act.activation(sb_ln[:, :, :], sb_ln[:, :, :], ACT.Exp, scale=-1.0))
                act.activation(sb_ln[:, :, :], sb_ln[:, :, :], ACT.Ln, bias=1.0).then_inc(sb_lned, 1)
                splits(3)
                chunk_done(u + 23)
                act.activation(sb_v[:, :, :], PS[:, 2:4, :], ACT.Copy).then_inc(evac_act, 1)
                act.wait_ge(sb_arg, 1)
                act.activation(sb_ln[:, :, :], sb_zs[:, :, :], ACT.Exp).then_inc(sb_w, 1)
                splits(1)
                act.wait_ge(sb_out, 1)
                act.activation(hmix[:, :, 512:].rearrange("p t (h d) -> p h t d", h=4),
                               PS[:, 0:4, :].rearrange("p h (t d) -> p h t d", t=2)[:, :, :, 0:128],
                               ACT.Copy).then_inc(ab_mixed, 1)
                activations("ab_o", lambda k: vec("ab_head_gain", k) if k < 4 else one_col)
                splits(8)

            def cross(l):
                norm(f"xq{l}", lambda k: vec("xa_norm", 8 * l + k))
                square_evac(UNIT0[f"xq{l}"], to_features(xa_q))

                def copy_pt(h):
                    act.wait_ge(xa_turned, 4 * l + h + 1)
                    act.activation(xa_pt[:, h], PS[:, h, :].rearrange("p (m t) -> p m t", m=2),
                                   ACT.Copy).then_inc(xa_pt_act, 1)
                for h in range(4):
                    act.wait_ge(xa_max, 4 * l + h + 1)
                    for t in range(TT):
                        act.activation(xa_p[:, h, t], PS[:, 4 + h, t * T:t * T + T], ACT.Exp, scale=1 / 16,
                                       bias=xa_nm[:, 2 * h + t:2 * h + t + 1],
                                       accum_out=xa_s[:, 2 * h + t:2 * h + t + 1]).then_inc(xa_exp, 1)
                for h in (0, 2):
                    copy_pt(h)
                activations(f"xo{l}", lambda k: one_col)
                splits(8)

            def mlp(l):
                norm(f"mlp{l}", lambda k: vec("mlp_norm", 8 * l + k))
                u0, n, wu = UNIT0[f"mlp{l}"], FF // 512, 4
                h0 = HID0[f"mlp{l}"]

                def hidden(c, q, u_last, i, per):
                    chunk_done(u_last, i, per)
                    act.activation(relu[:, q].rearrange("p (b k) t -> p b k t", b=2),
                                   PS[:, 2 * q:2 * q + 2, :].rearrange("p b (k t) -> p b k t", k=2),
                                   ACT.Relu).then_inc(hid_in, 1)
                    act.wait_ge(hid_in, c + (h0 + 1))
                    act.activation(hid_hi[:, q], relu[:, q], ACT.Square).then_inc(hid_hi_done, 1)

                splits(4)
                hidden(0, 0, u0 + 3, 0, 0)
                u1 = nxt[0]
                pairs = (n - 1) // 2
                per = 2 * (4 + wu)
                with act.Fori(0, pairs) as i:
                    for q in range(2):
                        for j in range(4 + wu):
                            split(u1 + q * (4 + wu) + j, i, per)
                            if j == wu - 1:
                                hidden(q + 1 + 2 * i, (q + 1) % 2, u0 + 7 + q * (4 + wu), i, per)
                nxt[0] = u1 + pairs * per
                splits(4)
                hidden(n - 1, (n - 1) % 2, u0 + 3 + 4 + (n - 2) * (4 + wu), 0, 0)
                splits(4)
                splits(4)

            def glu(l):
                norm(f"ffn{l}", lambda k: ffn_gain[:, l, k:k + 1])
                u0, n, wu = UNIT0[f"ffn{l}"], GLU // 256, 2
                h0, g0 = HID0[f"ffn{l}"], (GLU // 256) * l

                def tap(part, c, k):
                    return vec("ffn_conv_w_2", 132 * l + 88 + 22 * part + k, 2 * c)

                def hidden(c, q, u_last, i, per, fill):
                    chunk_done(u_last, i, per)
                    src = PS[:, 2 * q:2 * q + 2, :].rearrange("p b (k t) -> p b k t", k=2)
                    act.activation(glu_pad[:, q, :, 2:2 + T].rearrange("p (b k) t -> p b k t", b=2), src, ACT.Copy)
                    for f in range(4):
                        part, k = f // 2, f % 2
                        last = act.activation(glu_acc[:, q, f], PS[:, 2 * q + f // 2, (f % 2) * T:(f % 2) * T + T],
                                              ACT.Identity, scale=tap(part, c, k),
                                              bias=vec("ffn_conv_b_2", 44 * l + 22 * part + k, 2 * c))
                    last.then_inc(glu_in, 1)
                    fill[0]()
                    act.wait_ge(glu_conv, c + (g0 + 1))
                    act.activation(glu_silu[:, q], glu_acc[:, q, 2:4], ACT.Silu).then_inc(glu_silued, 1)
                    fill[1]()
                    act.wait_ge(glu_mult, c + (g0 + 1))
                    act.activation(hid_hi[:, q, 0:2], glu_prod[:, q], ACT.Copy).then_inc(hid_hi_done, 1)

                splits(4)
                u1 = nxt[0]
                hidden(0, 0, u0 + 3, 0, 0, (lambda: splits(1), lambda: splits(1)))
                assert nxt[0] == u1 + 2
                pairs = (n - 3) // 2
                per = 2 * (4 + wu)
                one = lambda: splits(1)
                with act.Fori(0, pairs) as i:
                    for q in range(2):
                        v = u1 + 2 + q * (4 + wu)
                        for j in range(4):
                            split(v + j, i, per)
                        hidden(q + 1 + 2 * i, (q + 1) % 2, u0 + 7 + q * (4 + wu), i, per,
                               (lambda v=v: split(v + 4, i, per), lambda v=v: split(v + 5, i, per)))
                nxt[0] = u1 + 2 + pairs * per
                splits(4)
                hidden(n - 2, (n - 2) % 2, u0 + 7 + (n - 3) * (4 + wu), 0, 0, (one, one))
                splits(2)
                hidden(n - 1, (n - 1) % 2, u0 + 7 + (n - 2) * (4 + wu), 0, 0, (lambda: None, lambda: None))
                splits(4)

            def gdn():
                norm("gdn", lambda k: vec("mix_norm", 8 + k))
                u0 = UNIT0["gdn_in"]
                act.wait_ge(pool_set, POOL_SET["gdn"])
                with act.Fori(0, 3) as i:
                    for q in range(2):
                        for j in range(3):
                            split(u0 + 4 + 4 * q + j, i, 8)
                        chunk_done(u0 + 4 * q + 3, i, 8)
                        act.activation(gd_pad[:, q, :, 3:3 + T].rearrange("p (b k) t -> p b k t", b=2),
                                       PS[:, 2 * q:2 * q + 2, :].rearrange("p b (k t) -> p b k t", k=2), ACT.Copy)
                        for f in range(4):
                            last = act.activation(gd_acc[:, q, f], PS[:, 2 * q + f // 2, (f % 2) * T:(f % 2) * T + T],
                                                  ACT.Copy, scale=vec("c_conv_w", 72 + 4 * q + f, 8 * i))
                        last.then_inc(gd_padded, 1)
                        split(u0 + 4 + 4 * q + 3, i, 8)
                        act.wait_ge(gd_conv, 2 * i + (q + 1))
                        act.activation(gd_qkv[:, ds(8 * i + 4 * q, 4), :], gd_acc[:, q], ACT.Silu).then_inc(evac_act, 1)
                nxt[0] += 24
                act.activation(gd_sq[:, :, :], gd_qkv[:, 0:8], ACT.Square).then_inc(gd_sqd, 1)
                act.wait_ge(gd_f, 1)
                act.activation(gd_rows[0:8, 0], PS[0:8, 7, 0:T], ACT.Sigmoid)
                order(act.activation(gd_rows[0:8, 2], gd_rows[0:8, 1], ACT.Abs))
                order(act.activation(gd_rows[0:8, 3], gd_rows[0:8, 2], ACT.Exp, scale=-1.0))
                act.activation(gd_nea[0:8, 1:2], gbias[0:8, 1:2], ACT.Exp)
                act.activation(gd_rows[0:8, 4], gd_rows[0:8, 3], ACT.Ln, bias=1.0).then_inc(gd_lnf, 1)
                for c in (6, 7):
                    splits(3)
                    chunk_done(u0 + 4 * c + 3)
                    act.activation(gd_gate[:, :, 512 * (c - 6):512 * (c - 5)], PS[:, 2 * (c % 2):2 * (c % 2) + 2, :],
                                   ACT.Silu).then_inc(evac_act, 1)
                    splits(1)
                    if c == 6:
                        act.wait_ge(gd_sums, 1)
                        act.activation(gd_sq[:, :, :].rearrange("p (b k) t -> p b k t", b=4),
                                       PS[:, 4:8, :].rearrange("p b (k t) -> p b k t", k=2), ACT.Sqrt,
                                       bias=eps_col[:, :]).then_inc(gd_rooted, 1)
                        act.wait_ge(gd_normed, 1)
                        act.activation(gd_sq[:, :, :], gd_qkv[:, 8:16], ACT.Square).then_inc(gd_sqd, 1)
                act.wait_ge(gd_sums, 2)
                act.activation(gd_sq[:, :, :].rearrange("p (b k) t -> p b k t", b=4),
                               PS[:, 4:8, :].rearrange("p b (k t) -> p b k t", k=2), ACT.Sqrt,
                               bias=eps_col[:, :]).then_inc(gd_rooted, 1)
                act.wait_ge(gd_args, 1)
                act.activation(gd_eg[:, :], gd_gcol[:, 1], ACT.Exp)
                act.activation(gd_kdc[:, :], gd_gl[:, :], ACT.Exp)
                act.activation(gd_E[:, :, :, :], gd_E[:, :, :, :], ACT.Exp).then_inc(gd_decayed, 1)
                with act.Fori(0, 6) as i:
                    for g in range(2):
                        act.wait_ge(gd_yps, 2 * i + (g + 1))
                        act.activation(gd_Y[:, g].rearrange("p (b k) t -> p b k t", b=2),
                                       PS[:, 4 * g:4 * g + 2, :].rearrange("p b (k t) -> p b k t", k=4),
                                       ACT.Copy).then_inc(gd_ysb, 1)
                for n, (dst, bank) in enumerate(((gd_vn, 0), (gd_S, 4), (gd_vn, 0))):
                    act.wait_ge(gd_fin_pe, n + 1 if n < 2 else 4)
                    act.activation(dst[:, :, :].rearrange("p (b k) t -> p b k t", b=2),
                                   PS[:, bank:bank + 2, :].rearrange("p b (k t) -> p b k t", k=4),
                                   ACT.Copy).then_inc(gd_fin_act, 1)
                act.activation(gd_o[:, 0].rearrange("p (b n) -> p b n", b=2), PS[:, 2:4, :], ACT.Copy)
                act.wait_ge(gd_fin_pe, 5)
                act.activation(gd_o[:, 1].rearrange("p (b n) -> p b n", b=2), PS[:, 4:6, :], ACT.Copy).then_inc(gd_fin_act, 1)
                act.wait_ge(gd_fin_dve, 2)
                act.activation(gd_osqt[:, :, :], gd_o[:, :, :], ACT.Square).then_inc(gd_osq_s, 1)
                activations("gdn_o", lambda k: vec("c_head_gain", 0))
                splits(8)

            def pool():
                act.wait_ge(x_updates, X_COUNT["final1"])
                squares(x)
                norm("pool", lambda k: vec("norm_mix_2", k))
                splits(2)

            def swa():
                norm("swa", lambda k: vec("norm_mix_2", 8 + k))
                u0 = UNIT0["qkv"]
                act.wait_ge(sw_den, 1)
                for c in range(2):
                    splits(3)
                    chunk_done(u0 + 4 * c + 3)
                    for f in range(4):
                        last = act.activation(sw_q[:, 4 * c + f], PS[:, 2 * (c % 2) + f // 2, (f % 2) * T:(f % 2) * T + T],
                                              ACT.Identity, scale=0.125, bias=sw_qb[:, 4 * c + f:4 * c + f + 1])
                    last.then_inc(evac_act, 1)
                    splits(1)
                splits(3)
                chunk_done(u0 + 11)
                for g in range(4):
                    r = slice(64 * (g % 2), 64 * (g % 2) + 64)
                    b, n = vec_at("attn_b_qkv_2", 8 + g // 2)
                    for half in range(2):
                        last = act.activation(sw_k[64 * half:64 * half + 64, g], PS[r, 0, (g // 2) * T:(g // 2) * T + T],
                                              ACT.Identity, bias=cols[r, b, n:n + 1])
                last.then_inc(evac_act, 1)
                splits(1)
                for grp in range(4):
                    act.wait_ge(sw_max, grp + 1)
                    for t in range(2):
                        act.activation(sw_es[:, t, 4 * grp:4 * grp + 4], sw_es[:, t, 4 * grp:4 * grp + 4], ACT.Exp)
                        for j in range(4):
                            h = 4 * grp + j
                            v = sw_s[:, j, 0:128] if t == 0 else sw_s[:, j, 128:384]
                            act.activation(v, v, ACT.Exp, bias=sw_nm[:, t, h:h + 1],
                                           accum_out=sw_sum[:, t, h:h + 1]).then_inc(sw_exp, 1)
                    act.wait_ge(sw_turned, grp + 1)
                    act.activation(sw_pt[:, 4 * grp:4 * grp + 4], PS[:, 0:4, 0:384], ACT.Copy).then_inc(sw_pted, 1)
                activations("swa_o", lambda k: one_col)
                splits(8)

            ab()
            cross(0)
            mlp(0)
            gdn()
            cross(1)
            mlp(1)
            pool()
            glu(0)
            swa()
            glu(1)
            act.wait_ge(x_updates, X_COUNT["final2"])
            squares(x)

        @block.vector
        def _(dve):
            order = Order(dve, dve_order)
            nxt = [0]

            def split(u, i=0, per=0):
                slot, n, _ = slot_of(u, i, per)
                dve.wait_ge(hi_done, n + 1)
                dve.tensor_tensor(w_lo[:, slot], w_raw[:, slot], f32(w_hi[:, slot]), ALU.subtract).then_inc(lo_done, 1)

            def splits(n):
                for _ in range(n):
                    if nxt[0] < UNITS:
                        split(nxt[0])
                    nxt[0] += 1

            def activations(turn, gain):
                n = TURNS.index(turn)
                for k in range(KT):
                    dve.wait_ge(xt_hi, 8 * n + 2 * (k // 2) + 2)
                    dve.scalar_tensor_tensor(XTl[:, k], PS[:, 4 + k // 2, (k % 2) * T:(k % 2) * T + T], gain(k),
                                             f32(XTh[:, k]), ALU.mult, ALU.subtract).then_inc(xt_lo, 1)

            def scale_rows(name, src):
                dve.wait_ge(rstd_done, root_at(name)[1] + 1)
                for t in range(TT):
                    dve.tensor_scalar(xn[:, t], src[:, t], rstd[:, t:t + 1], None, ALU.mult).then_inc(xn_ready, 1)

            def norm(name, gain):
                scale_rows(name, x)
                activations(name, gain)

            def square_splits(u0, n=2):
                with dve.Fori(0, n) as i:
                    for j in range(4):
                        split(u0 + RING + j, i, 4)
                nxt[0] += 4 * n

            def square_add(u0):
                with dve.Fori(0, 2) as i:
                    for j in range(3):
                        split(u0 + RING + j, i, 4)
                    dve.wait_ge(w_used, u0 + 4 + 4 * i)
                    xs = x[:, :, ds(512 * i, 512)]
                    dve.tensor_tensor(xs, PS[:, ds(2 * i, 2), :], xs, ALU.add).then_inc(x_updates, 1)
                    split(u0 + RING + 3, i, 4)
                nxt[0] += 8

            def wide_add(u_last):
                splits(3)
                dve.wait_ge(w_used, u_last + 1)
                for t in range(TT):
                    dve.tensor_tensor(x[:, t].rearrange("p (b n) -> p b n", b=2), PS[:, 4 + 2 * t:6 + 2 * t, :],
                                      x[:, t].rearrange("p (b n) -> p b n", b=2), ALU.add).then_inc(x_updates, 1)
                splits(1)

            def by_heads(v):
                return v.rearrange("p t (h d) -> p h t d", h=4)

            dve.wait_ge(vec_turned, 1)
            for b, rows in enumerate(VECTORS):
                n = sum(count for _, _, count in rows)
                last = dve.tensor_copy(cols[:, b, 0:n], PS[:, b // 4, (b % 4) * P:(b % 4) * P + n])
            last.then_inc(vec_kept, 1)
            splits(4)
            dve.wait_ge(mem_landed, 16)
            scale_rows("mem", xn)
            activations("mem", lambda k: vec("mem_norm", k))
            square_splits(0, 8)

            def ab():
                norm("ab", lambda k: vec("mix_norm", k))
                dve.wait_ge(misc_landed, MISC)
                splits(4)
                dve.wait_ge(ab_gates, 1)
                dve.tensor_scalar(ab_rows[0:4, 0], PS[0:4, 7, 0:T], gbias[0:4, 0:1], 1 / 15, ALU.add, ALU.mult)
                dve.tensor_scalar(ab_rows[0:4, 1], PS[32:36, 7, 0:T], gbias[32:36, 0:1], None, ALU.add).then_inc(ab_f, 1)
                dve.wait_ge(ab_lnf, 1)
                r = ab_rows
                order(dve.scalar_tensor_tensor(r[0:4, 6], r[0:4, 1], 0.0, r[0:4, 5], ALU.min, ALU.subtract))
                order(dve.tensor_tensor_scan(r[0:4, 8], r[0:4, 6], f32(zeros[0:4, 0:T]), 0.0, ALU.add, ALU.add))
                order(dve.scalar_tensor_tensor(r[0:4, 9], r[0:4, 2], 15.0, r[0:4, 8], ALU.mult, ALU.subtract))
                order(dve.tensor_tensor_scan(r[0:4, 10], r[0:4, 9], f32(zeros[0:4, 0:T]), 0.0, ALU.max, ALU.add))
                dve.tensor_scalar(r[0:4, 11], r[0:4, 10], -1.0, None, ALU.mult)
                dve.scalar_tensor_tensor(r[0:4, 12], r[0:4, 8], -1.0, r[0:4, 10], ALU.mult, ALU.subtract).then_inc(ab_rows_done, 1)
                splits(4)
                dve.wait_ge(ab_turned, 1)
                dve.tensor_copy(mcol[:, :, :], PS[:, 6, 8:16].rearrange("p (t h) -> p t h", t=2))
                order(dve.tensor_copy(acol[:, :, :], PS[:, 6, 0:8].rearrange("p (t h) -> p t h", t=2)))
                for h in range(4):
                    o = (h % 2) * T
                    dve.scalar_tensor_tensor(decay[:, h, 0:T], PS[:, 4 + h // 2, o:o + T], acol[:, 0, h:h + 1],
                                             C("causal_min"), ALU.add, ALU.min)
                    last = dve.scalar_tensor_tensor(decay[:, h, T:384], PS[:, 4 + h // 2, o + P:o + T],
                                                    acol[:, 1, h:h + 1], C("causal_min")[:, 0:P], ALU.add, ALU.min)
                last.then_inc(ab_args, 1)
                splits(4)
                dve.wait_ge(ab_scores, 1)
                dve.wait_ge(ab_decayed, 1)
                dve.tensor_tensor(prob[:, :, :], PS[:, 4:8, 0:384], decay[:, :, :], ALU.mult).then_inc(ab_probs, 1)
                splits(4)
                dve.wait_ge(ab_outs, 1)
                o = PS[:, 4:8, :].rearrange("p h (t d) -> p h t d", t=2)
                order(dve.tensor_copy(rden[:, :, :], o[:, :, :, 128]))
                order(dve.scalar_tensor_tensor(rden[:, :, :], rden[:, :, :], -1.0, rden[:, :, :], ALU.mult, ALU.max))
                order(dve.tensor_tensor(rden[:, :, :], rden[:, :, :], emcol[:, :, :].rearrange("p t h -> p h t"), ALU.max))
                order(dve.reciprocal(rden[:, :, :], rden[:, :, :]))
                hm = by_heads(hmix[:, :, 0:512])
                dve.tensor_tensor(hm, o[:, :, :, 0:128], rden[:, :, :].unsqueeze(3).broadcast_to([P, 4, 2, 128]),
                                  ALU.mult).then_inc(ab_norm, 1)
                dve.wait_ge(ab_sq, 1)
                dve.tensor_reduce(ss[:, 0:8], hsq[:, :, :].rearrange("p t (h d) -> p (t h) d", h=4), AX.X,
                                  ALU.add).then_inc(sq_done, 1)
                splits(4)
                dve.wait_ge(sb_z, 1)
                dve.tensor_copy(sb_zs[:, :, :], PS[:, 4:8, 0:384]).then_inc(sb_kept, 1)
                dve.wait_ge(sb_lned, 1)
                order(dve.scalar_tensor_tensor(sb_sp[:, :, :], sb_zs[:, :, :], 0.0, sb_ln[:, :, :], ALU.max, ALU.add))

                def diagonals(v):
                    return v[:, :, :].rearrange("p h (b t) -> p h b t", b=3)[:, :, 0:3:2, :]

                def mask(name):
                    return C(name).unsqueeze(1).unsqueeze(1).broadcast_to([P, 4, 2, P])
                dve.tensor_tensor(diagonals(sb_sp), diagonals(sb_sp), mask("strict"), ALU.mult).then_inc(sb_sped, 1)
                dve.wait_ge(rstd_done, root_at("ab_heads")[1] + 1)
                hv = hmix[:, :, 0:512].rearrange("p t (h d) -> p t h d", h=4)
                order(dve.tensor_tensor(hv, hv, rstd[:, 0:8].rearrange("p (t h) -> p t h", t=2).unsqueeze(3)
                                        .broadcast_to([P, 2, 4, 128]), ALU.mult))
                dve.tensor_tensor(hmix[:, :, 0:512], hmix[:, :, 0:512], ab_og[:, :, :], ALU.mult).then_inc(ab_mixed, 1)
                dve.wait_ge(sb_cum, 1)
                order(dve.tensor_tensor(sb_zs[:, :, :], sb_zs[:, :, :], PS[:, 4:8, 0:384], ALU.subtract))
                dve.tensor_tensor(diagonals(sb_zs), diagonals(sb_zs), mask("strict_min"), ALU.min).then_inc(sb_arg, 1)
                splits(4)
                activations("ab_o", lambda k: vec("ab_head_gain", k) if k < 4 else one_col)
                square_add(UNIT0["ab_o"])

            def cross(l):
                norm(f"xq{l}", lambda k: vec("xa_norm", 8 * l + k))
                square_splits(UNIT0[f"xq{l}"])

                def maxima(h):
                    dve.wait_ge(xa_scores, 4 * l + h + 1)
                    m = slice(2 * h, 2 * h + 2)
                    order(dve.tensor_reduce(xa_m[:, m], PS[:, 4 + h, :].rearrange("p (t s) -> p t s", t=2), AX.X,
                                            ALU.max))
                    dve.tensor_scalar(xa_nm[:, m], xa_m[:, m], -1 / 16, None, ALU.mult).then_inc(xa_max, 1)

                def normalise(h):
                    dve.wait_ge(xa_exp, 8 * l + 2 * h + 2)
                    order(dve.reciprocal(xa_r[:, 2 * h:2 * h + 2], xa_s[:, 2 * h:2 * h + 2]))
                    for t in range(TT):
                        last = dve.tensor_scalar(xa_p[:, h, t], xa_p[:, h, t], xa_r[:, 2 * h + t:2 * h + t + 1], None, ALU.mult)
                    last.then_inc(xa_probs, 1)

                def copy_pt(h):
                    dve.wait_ge(xa_turned, 4 * l + h + 1)
                    dve.tensor_copy(xa_pt[:, h], PS[:, h, :].rearrange("p (m t) -> p m t", m=2)).then_inc(xa_pt_dve, 1)
                maxima(0)
                maxima(1)
                normalise(0)
                maxima(2)
                normalise(1)
                maxima(3)
                normalise(2)
                normalise(3)
                copy_pt(1)
                copy_pt(3)
                activations(f"xo{l}", lambda k: one_col)
                square_add(UNIT0[f"xo{l}"])

            def mlp(l):
                norm(f"mlp{l}", lambda k: vec("mlp_norm", 8 * l + k))
                u0, n, wu = UNIT0[f"mlp{l}"], FF // 512, 4
                h0 = HID0[f"mlp{l}"]

                def hidden(c, q):
                    dve.wait_ge(hid_in, c + (h0 + 1))
                    order(dve.tensor_tensor(relu2[:, q], relu[:, q], relu[:, q], ALU.mult))
                    dve.wait_ge(hid_hi_done, c + (h0 + 1))
                    dve.tensor_tensor(hid_lo[:, q], relu2[:, q], f32(hid_hi[:, q]), ALU.subtract).then_inc(hid_lo_done, 1)

                splits(4)
                hidden(0, 0)
                u1 = nxt[0]
                pairs = (n - 1) // 2
                per = 2 * (4 + wu)
                with dve.Fori(0, pairs) as i:
                    order.loop(i, 2)
                    for q in range(2):
                        for j in range(4 + wu):
                            split(u1 + q * (4 + wu) + j, i, per)
                            if j == wu - 1:
                                hidden(q + 1 + 2 * i, (q + 1) % 2)
                    order.end(pairs)
                nxt[0] = u1 + pairs * per
                splits(4)
                hidden(n - 1, (n - 1) % 2)
                splits(4)
                wide_add(u0 + n * (4 + wu) - 1)

            def glu(l):
                norm(f"ffn{l}", lambda k: ffn_gain[:, l, k:k + 1])
                u0, n, wu = UNIT0[f"ffn{l}"], GLU // 256, 2
                h0, g0 = HID0[f"ffn{l}"], (GLU // 256) * l
                dve.wait_ge(pool_set, POOL_SET[f"ffn{l}"])

                def hidden(c, q, fill):
                    dve.wait_ge(glu_in, c + (g0 + 1))
                    for tap in range(2):
                        for f in range(4):
                            part, k = f // 2, f % 2
                            last = dve.scalar_tensor_tensor(
                                glu_acc[:, q, f], glu_pad[:, q, f, tap:tap + T],
                                vec("ffn_conv_w_2", 132 * l + 44 * tap + 22 * part + k, 2 * c), glu_acc[:, q, f],
                                ALU.mult, ALU.add)
                        if tap == 0:
                            order(last)
                    last.then_inc(glu_conv, 1)
                    fill[0]()
                    dve.wait_ge(glu_silued, c + (g0 + 1))
                    dve.tensor_tensor(glu_prod[:, q], glu_acc[:, q, 0:2], glu_silu[:, q], ALU.mult).then_inc(glu_mult, 1)
                    fill[1]()
                    dve.wait_ge(hid_hi_done, c + (h0 + 1))
                    dve.tensor_tensor(hid_lo[:, q, 0:2], glu_prod[:, q], f32(hid_hi[:, q, 0:2]), ALU.subtract)\
                        .then_inc(hid_lo_done, 1)

                one = lambda: splits(1)
                splits(4)
                hidden(0, 0, (one, one))
                v0 = nxt[0]
                pairs = (n - 3) // 2
                per = 2 * (4 + wu)
                with dve.Fori(0, pairs) as i:
                    order.loop(i, 2)
                    for q in range(2):
                        v = v0 + q * (4 + wu)
                        for j in range(4):
                            split(v + j, i, per)
                        hidden(q + 1 + 2 * i, (q + 1) % 2,
                               (lambda v=v: split(v + 4, i, per), lambda v=v: split(v + 5, i, per)))
                    order.end(pairs)
                nxt[0] = v0 + pairs * per
                splits(4)
                hidden(n - 2, (n - 2) % 2, (one, one))
                splits(2)
                hidden(n - 1, (n - 1) % 2, (lambda: None, lambda: None))
                wide_add(u0 + n * (4 + wu) - 1)

            def gdn():
                norm("gdn", lambda k: vec("mix_norm", 8 + k))
                u0 = UNIT0["gdn_in"]
                dve.wait_ge(pool_set, POOL_SET["gdn"])
                with dve.Fori(0, 3) as i:
                    order.loop(i, 4)
                    for q in range(2):
                        for j in range(3):
                            split(u0 + 4 + 4 * q + j, i, 8)
                        dve.wait_ge(gd_padded, 2 * i + (q + 1))
                        for tap in range(3):
                            for f in range(4):
                                last = dve.scalar_tensor_tensor(
                                    gd_acc[:, q, f], gd_pad[:, q, f, tap:tap + T],
                                    vec("c_conv_w", 24 * tap + 4 * q + f, 8 * i), gd_acc[:, q, f], ALU.mult, ALU.add)
                            if tap < 2:
                                order(last)
                        last.then_inc(gd_conv, 1)
                        split(u0 + 4 + 4 * q + 3, i, 8)
                    order.end(3)
                nxt[0] += 24
                dve.wait_ge(gd_gates_s, 1)
                dve.tensor_scalar(gd_rows[0:8, 1], PS[32:40, 7, 0:T], gbias[32:40, 1:2], None, ALU.add).then_inc(gd_f, 1)
                dve.wait_ge(gd_lnf, 1)
                order(dve.scalar_tensor_tensor(gd_rows[0:8, 5], gd_rows[0:8, 1], 0.0, gd_rows[0:8, 4], ALU.max, ALU.add))
                order(dve.tensor_scalar(gd_rows[0:8, 5], gd_rows[0:8, 5], gd_nea[0:8, 1:2], -1.0, ALU.mult, ALU.mult))
                for c in range(2):
                    s = slice(c * P, c * P + P)
                    last = dve.tensor_tensor_scan(gd_rows[0:8, 6, s], gd_rows[0:8, 5, s], f32(zeros[0:8, 0:P]), 0.0,
                                                  ALU.add, ALU.add)
                last.then_inc(gd_rows_s, 1)
                splits(4)
                for b, scale in ((0, 128 ** -0.5), (1, 1.0)):
                    dve.wait_ge(gd_rooted, b + 1)
                    order(dve.reciprocal(gd_sq[:, :, :], gd_sq[:, :, :]))
                    v = gd_qkv[:, 8 * b:8 * b + 8]
                    dve.scalar_tensor_tensor(v, v, scale, gd_sq[:, :, :], ALU.mult, ALU.mult).then_inc(gd_normed, 1)
                    if b == 0:
                        splits(4)
                dve.wait_ge(gd_colt, 1)
                dve.tensor_copy(gd_bcol[:, :, :], PS[:, 0, 16:32].rearrange("p (c h) -> p c h", c=2))
                order(dve.tensor_copy(gd_gcol[:, :, :], PS[:, 0, 0:16].rearrange("p (c h) -> p c h", c=2)))
                dve.wait_ge(gd_bcast, 1)
                gb = PS[:, 4:8, :].rearrange("p b (k t) -> p (b k) t", k=2)
                dve.tensor_tensor(gd_gl[:, :], gb[:, :, P - 1], gd_gcol[:, 0], ALU.subtract)
                for c in range(2):
                    for h in range(8):
                        o = (h % 2) * T + c * P
                        last = dve.scalar_tensor_tensor(gd_E[:, c, h], PS[:, 4 + h // 2, o:o + P], gd_gcol[:, c, h:h + 1],
                                                        C("causal_min")[:, 0:P], ALU.subtract, ALU.min)
                last.then_inc(gd_args, 1)
                dve.wait_ge(gd_bcast, 2)
                dve.wait_ge(gd_decayed, 1)
                for c in range(2):
                    last = dve.tensor_tensor(gd_U[:, c].rearrange("p (b k) t -> p b k t", k=2),
                                             gd_E[:, c].rearrange("p (b k) t -> p b k t", k=2),
                                             PS[:, 0:4, :].rearrange("p b (k t) -> p b k t", k=2)[:, :, :, c * P:c * P + P],
                                             ALU.mult)
                last.then_inc(gd_bb, 1)
                dve.wait_ge(gd_bb, 1)
                last = dve.tensor_tensor(gd_beg[:, :], gd_eg[:, :], gd_bcol[:, 1], ALU.mult)
                order(last)
                dve.wait_ge(gd_kk, 1)
                allU = gd_U[:, :, :, :].rearrange("p c (b k) t -> p (c b) k t", k=4)
                order(dve.tensor_tensor(allU, allU, PS[:, 4:8, :].rearrange("p b (k t) -> p b k t", k=4), ALU.mult))
                dve.wait_ge(gd_qk, 1)
                allE = gd_E[:, :, :, :].rearrange("p c (b k) t -> p (c b) k t", k=4)
                dve.tensor_tensor(allE, allE, PS[:, 0:4, :].rearrange("p b (k t) -> p b k t", k=4), ALU.mult)\
                    .then_inc(gd_made, 1)
                dve.wait_ge(gd_vt, 1)
                dve.tensor_tensor(gd_bv[:, :, :, :].rearrange("p c (b k) t -> p (c b) k t", k=4),
                                  PS[:, 4:8, :].rearrange("p b (k t) -> p b k t", k=4),
                                  gd_bcol[:, :, :].rearrange("p c (b k) -> p (c b) k", k=4).unsqueeze(3)
                                  .broadcast_to([P, 4, 4, P]), ALU.mult).then_inc(gd_made, 1)
                dve.wait_ge(gd_kt, 1)
                dve.tensor_tensor(gd_kd[:, :, :].rearrange("p (b k) t -> p b k t", k=4),
                                  PS[:, 0:2, :].rearrange("p b (k t) -> p b k t", k=4),
                                  gd_kdc[:, :].rearrange("p (b k) -> p b k", k=4).unsqueeze(3)
                                  .broadcast_to([P, 2, 4, P]), ALU.mult).then_inc(gd_made, 1)

                def wide_mask(name):
                    return C(name).unsqueeze(1).broadcast_to([P, 8, P])

                def banks(g, b):
                    return PS[:, 4 * g + b:4 * g + b + 2, :].rearrange("p b (k t) -> p b k t", k=4)

                def four(v):
                    return v.rearrange("p (b k) t -> p b k t", k=4)
                for g in range(2):
                    dve.tensor_tensor(gd_um[:, g], gd_U[:, g], wide_mask("level0"), ALU.mult).then_inc(gd_masked, 1)
                for g in range(2):
                    dve.wait_ge(gd_masked, 2)
                    dve.tensor_tensor(gd_XT[:, g], wide_mask("ident"), gd_um[:, g], ALU.subtract)
                    dve.wait_ge(gd_xps, g + 1)
                    dve.tensor_tensor(four(gd_X[:, g]), C("ident").unsqueeze(1).unsqueeze(1).broadcast_to([P, 2, 4, P]),
                                      banks(g, 0), ALU.subtract).then_inc(gd_xnew, 1)
                n_level, w_level = CONST_AT["level1"]
                with dve.Fori(0, 5) as i:
                    mask_i = const[:, ds(n_level + i * w_level, w_level)].unsqueeze(1).broadcast_to([P, 8, P])
                    for g in range(2):
                        dve.wait_ge(gd_xnew, 2 * i + (g + 1))
                        dve.tensor_tensor(gd_um[:, g], gd_U[:, g], mask_i, ALU.mult).then_inc(gd_masked, 1)
                    for g in range(2):
                        dve.wait_ge(gd_xps, 2 * i + (g + 3))
                        dve.tensor_tensor(four(gd_X[:, g]), four(gd_X[:, g]), banks(g, 2), ALU.subtract)
                        dve.tensor_tensor(four(gd_XT[:, g]), four(gd_XT[:, g]), banks(g, 0), ALU.subtract).then_inc(gd_xnew, 1)
                for g in range(2):
                    dve.wait_ge(gd_xnew, 11 + g)
                    dve.tensor_tensor(gd_um[:, g], gd_U[:, g], wide_mask("level6"), ALU.mult).then_inc(gd_masked, 1)
                for g in range(2):
                    dve.wait_ge(gd_xps, 13 + g)
                    dve.tensor_tensor(four(gd_XT[:, g]), four(gd_XT[:, g]), banks(g, 0), ALU.subtract).then_inc(gd_xnew, 1)
                dve.wait_ge(gd_fin_pe, 3)
                for h in range(8):
                    last = dve.scalar_tensor_tensor(gd_bv[:, 1, h], PS[:, 6 + h // 4, (h % 4) * P:(h % 4) * P + P],
                                                    gd_beg[:, h:h + 1], gd_bv[:, 1, h], ALU.mult, ALU.subtract, reverse1=True)
                last.then_inc(gd_fin_dve, 1)
                dve.wait_ge(gd_fin_act, 4)
                dve.wait_ge(gd_fin_pe, 5)
                for h in range(8):
                    o = gd_o[:, 1, h * P:(h + 1) * P]
                    last = dve.scalar_tensor_tensor(o, PS[:, 6 + h // 4, (h % 4) * P:(h % 4) * P + P], gd_eg[:, h:h + 1], o,
                                                    ALU.mult, ALU.add)
                last.then_inc(gd_fin_dve, 1)
                dve.wait_ge(gd_osq_s, 1)
                dve.tensor_reduce(ss[:, 0:16], gd_osqt[:, :, :].rearrange("p c (h d) -> p (c h) d", h=8), AX.X,
                                  ALU.add).then_inc(sq_done, 1)
                dve.wait_ge(rstd_done, root_at("gdn_heads")[1] + 1)
                ov = gd_o[:, :, :].rearrange("p c (h d) -> p (c h) d", h=8)
                order(dve.tensor_tensor(ov, ov, rstd[:, 0:16].unsqueeze(2).broadcast_to([P, 16, P]), ALU.mult))
                dve.tensor_tensor(gd_o[:, :, :], gd_o[:, :, :], gd_gate[:, :, :], ALU.mult).then_inc(gd_mixed, 1)
                activations("gdn_o", lambda k: vec("c_head_gain", 0))
                square_add(UNIT0["gdn_o"])

            def pool():
                dve.wait_ge(bc_landed, 64)
                dve.wait_ge(rstd_done, root_at("final1")[1] + 1)
                for t in range(TT):
                    dve.scalar_tensor_tensor(x[:, t], x[:, t], rstd[:, t:t + 1], bc[:, 0], ALU.mult, ALU.mult)\
                        .then_inc(x_updates, 1)
                scale_rows("pool", x)
                activations("pool", lambda k: vec("norm_mix_2", k))
                splits(2)
                for c in range(2):
                    s = slice(512 * c, 512 * c + 512)
                    dve.wait_ge(w_used, UNIT0["pool"] + c + 1)
                    order(dve.tensor_tensor(xn[:, :, s], PS[:, 2 * c:2 * c + 2, :],
                                            bc[:, 2, s].unsqueeze(1).broadcast_to([P, 2, 512]), ALU.add))
                    order(dve.tensor_tensor(xn[:, :, s], xn[:, :, s], bc[:, 3, s].unsqueeze(1).broadcast_to([P, 2, 512]),
                                            ALU.mult))
                    dve.tensor_tensor(x[:, :, s], x[:, :, s], xn[:, :, s], ALU.add).then_inc(x_updates, 1)

            def swa():
                norm("swa", lambda k: vec("norm_mix_2", 8 + k))
                b, n = vec_at("attn_b_qkv_2", 0)
                dve.tensor_scalar(sw_qb[:, :], cols[:, b, n:n + 8], 0.125, None, ALU.mult).then_inc(sw_den, 1)
                u0 = UNIT0["qkv"]
                splits(12)
                dve.wait_ge(w_used, u0 + 12)
                dve.tensor_tensor(sw_v[:, :, :], PS[:, 1, :].rearrange("p (t n) -> p t n", t=2),
                                  vbias[:, :].unsqueeze(1).broadcast_to([P, 2, T]), ALU.add).then_inc(v_kept, 1)
                for grp in range(4):
                    hs = slice(4 * grp, 4 * grp + 4)
                    dve.wait_ge(sw_scores, grp + 1)
                    if grp:
                        dve.wait_ge(sw_turned, grp)
                    for j in range(4):
                        h = 4 * grp + j
                        last = dve.scalar_tensor_tensor(sw_s[:, j], C("dist"), -float(2.0 ** (-8.0 / SWA_HEADS * (h + 1))),
                                                        PS[:, 4 + j, 0:384], ALU.mult, ALU.add)
                    order(last)
                    order(dve.tensor_tensor(sw_s[:, :, :], sw_s[:, :, :],
                                            C("band_add").unsqueeze(1).broadcast_to([P, 4, 384]), ALU.add))
                    dve.tensor_reduce(sw_m[:, 0, hs], sw_s[:, :, 0:128], AX.X, ALU.max)
                    order(dve.tensor_reduce(sw_m[:, 1, hs], sw_s[:, :, 128:384], AX.X, ALU.max))
                    sk = sinks[:, hs].unsqueeze(1).broadcast_to([P, 2, 4])
                    order(dve.tensor_tensor(sw_m[:, :, hs], sw_m[:, :, hs], sk, ALU.max))
                    dve.tensor_scalar(sw_nm[:, :, hs], sw_m[:, :, hs], -1.0, None, ALU.mult)
                    dve.tensor_tensor(sw_es[:, :, hs], sk, sw_m[:, :, hs], ALU.subtract).then_inc(sw_max, 1)
                    dve.wait_ge(sw_exp, 8 * grp + 8)
                    order(dve.tensor_tensor(sw_r[:, :, hs], sw_sum[:, :, hs], sw_es[:, :, hs], ALU.add))
                    order(dve.reciprocal(sw_r[:, :, hs], sw_r[:, :, hs]))
                    for t, s in ((0, slice(0, 128)), (1, slice(128, 384))):
                        last = dve.tensor_tensor(sw_s[:, :, s], sw_s[:, :, s],
                                                 sw_r[:, t, hs].unsqueeze(2).broadcast_to([P, 4, s.stop - s.start]), ALU.mult)
                    last.then_inc(sw_probs, 1)
                activations("swa_o", lambda k: one_col)
                square_add(UNIT0["swa_o"])

            ab()
            cross(0)
            mlp(0)
            gdn()
            cross(1)
            mlp(1)
            pool()
            glu(0)
            swa()
            glu(1)
            dve.wait_ge(rstd_done, root_at("final2")[1] + 1)
            for t in range(TT):
                dve.scalar_tensor_tensor(xn[:, t], x[:, t], rstd[:, t:t + 1], bc[:, 1], ALU.mult, ALU.mult)\
                    .then_inc(xn_ready, 1)

        @block.tensor
        def _(pe):
            mm = pe.matmul

            def kt_pair_wait(turn, j):
                pe.wait_ge(xt_lo, 8 * TURNS.index(turn) + 2 * j + 2)

            def three(dst, ah, al, bh, bl, first, last):
                mm(dst, ah, bh, start=first, stop=False, skip_group_check=True)
                mm(dst, ah, bl, start=False, stop=False, skip_group_check=True)
                return mm(dst, al, bh, start=False, stop=last, skip_group_check=True)

            def token_unit(slot, j, bank, i, cols_=slice(0, 512)):
                n = cols_.stop - cols_.start
                for k in range(2):
                    for t in range(TT):
                        kt = 2 * j + k
                        last = three(PS[:, ds(bank + 2 * i + t, 1), 0:n].rearrange("p a n -> p (a n)") if not isinstance(i, int)
                                     else PS[:, bank + 2 * i + t, 0:n],
                                     XTh[:, kt, t * P:t * P + P], XTl[:, kt, t * P:t * P + P],
                                     w_hi[:, slot, k, cols_], w_lo[:, slot, k, cols_], kt == 0, kt == KT - 1)
                return last

            def feature_unit(slot, j, bank, i, tiles=4):
                for k in range(2):
                    kt = 2 * j + k
                    for f in range(tiles):
                        if isinstance(i, int):
                            dst = PS[:, bank + 2 * i + f // 2, (f % 2) * T:(f % 2) * T + T]
                        else:
                            dst = PS[:, ds(bank + 2 * i + f // 2, 1), (f % 2) * T:(f % 2) * T + T].rearrange("p a n -> p (a n)")
                        s = slice(f * P, f * P + P)
                        last = three(dst, w_hi[:, slot, k, s], w_lo[:, slot, k, s], XTh[:, kt], XTl[:, kt],
                                     kt == 0 and f % 2 == 0, kt == KT - 1)
                return last

            def chunk(u, turn, unit, bank, bank_i=0, i=0, per=0):
                for j in range(4):
                    slot, n, _ = slot_of(u + j, i, per)
                    if turn:
                        kt_pair_wait(turn, j)
                    pe.wait_ge(lo_done, n + 1)
                    unit(slot, j, bank, bank_i).then_inc(w_used, 1)

            def square(u0, turn, unit):
                with pe.Fori(0, 2) as i:
                    chunk(u0, turn, unit, 0, i, i, 4)

            def turn(name):
                for b in range(4):
                    for k in range(2):
                        for t in range(TT):
                            f = 2 * b + k
                            last = pe.transpose(PS[:, 4 + b, k * T + t * P:k * T + t * P + P],
                                                xn[:, t, f:D:KT] if name in ("ffn0", "ffn1") else
                                                xn[:, t, f * P:f * P + P], ident)
                    last.then_inc(turned, 1)

            def norm(name):
                pe.wait_ge(xn_ready, 2 * NORMS.index(name) + 2)
                turn(name)

            def gates(which, width):
                for k in range(KT):
                    mm(PS[0:width, 7, 0:T], gate_w[:, which, k, 0:width], f32(XTh[:, k]), start=k == 0, stop=False)
                    last = mm(PS[0:width, 7, 0:T], gate_w[:, which, k, 0:width], f32(XTl[:, k]), start=False, stop=k == KT - 1)
                return last

            pe.wait_ge(const_landed, 16)
            pe.wait_ge(vec_landed, 16 * sum(len(rows) for rows in VECTORS))
            for b, rows in enumerate(VECTORS):
                n = sum(count for _, _, count in rows)
                last = pe.transpose(PS[:, b // 4, (b % 4) * P:(b % 4) * P + n], vec_rows[0:n, b, :], ident[0:n, 0:n])
            last.then_inc(vec_turned, 1)
            norm("mem")
            pe.wait_ge(pool_set, 2)
            pe.wait_ge(vec_kept, 1)
            for k, unit in enumerate((feature_unit, token_unit, feature_unit, token_unit)):
                if k:
                    pe.wait_ge(evac_act, 2 * k)
                square(8 * k, "mem", unit)

            def ab():
                norm("ab")
                pe.wait_ge(evac_act, EVAC0["ab_in"])
                pe.wait_ge(misc_landed, MISC)
                u, e = UNIT0["ab_in"], EVAC0["ab_in"]
                chunk(u, "ab", feature_unit, 0)
                gates(0, 36).then_inc(ab_gates, 1)
                chunk(u + 4, "ab", token_unit, 2)
                pe.wait_ge(ab_rows_done, 1)
                for t in range(TT):
                    pe.transpose(PS[:, 6, 4 * t:4 * t + 4], ab_rows[0:4, 9, t * P:t * P + P], ident[0:4, 0:4])
                    pe.transpose(PS[:, 6, 8 + 4 * t:12 + 4 * t], ab_rows[0:4, 12, t * P:t * P + P], ident[0:4, 0:4])
                for h in range(4):
                    last = mm(PS[:, 4 + h // 2, (h % 2) * T:(h % 2) * T + T], C(f"select{h}")[0:4, :], ab_rows[0:4, 11],
                              start=True, stop=True)
                last.then_inc(ab_turned, 1)
                pe.wait_ge(evac_act, e + 1)
                chunk(u + 8, "ab", token_unit, 0)
                pe.wait_ge(ab_args, 1)
                for h in range(4):
                    r = slice(64 * (h % 2), 64 * (h % 2) + 64)
                    mm(PS[:, 4 + h, 0:T], ab_qk[r, 2 + h // 2, 0:P], ab_qk[r, h // 2, 0:T], start=True, stop=True)
                    last = mm(PS[:, 4 + h, T:384], ab_qk[r, 2 + h // 2, P:T], ab_qk[r, h // 2, P:T], start=True, stop=True)
                last.then_inc(ab_scores, 1)
                pe.wait_ge(evac_act, e + 2)
                chunk(u + 12, "ab", feature_unit, 2)
                pe.wait_ge(ab_probs, 1)
                pe.wait_ge(pool_set, POOL_SET["ab"])
                for h in range(4):
                    mm(PS[:, 4 + h, 0:129], prob[:, h, 0:P], ab_v[:, 0, h, 0:129], start=True, stop=True)
                    mm(PS[:, 4 + h, T:T + 129], prob[:, h, P:T], ab_v[:, 0, h, 0:129], start=True, stop=False)
                    last = mm(PS[:, 4 + h, T:T + 129], prob[:, h, T:384], ab_v[:, 1, h, 0:129], start=False, stop=True)
                last.then_inc(ab_outs, 1)
                pe.wait_ge(evac_act, e + 3)
                chunk(u + 16, "ab", feature_unit, 0)
                pe.wait_ge(ab_norm, 1)
                pe.wait_ge(evac_act, e + 5)
                for h in range(4):
                    mm(PS[:, 4 + h, 0:T], sb_k[:, h, 0:P], sb_q[:, h, 0:T], start=True, stop=True)
                    last = mm(PS[:, 4 + h, T:384], sb_k[:, h, P:T], sb_q[:, h, P:T], start=True, stop=True)
                last.then_inc(sb_z, 1)
                chunk(u + 20, "ab", token_unit, 2)
                pe.wait_ge(sb_sped, 1)
                for h in range(4):
                    mm(PS[:, 4 + h, 0:T], C("suffix"), sb_sp[:, h, 0:T], start=True, stop=False, skip_group_check=True)
                    mm(PS[:, 4 + h, P:T], ones, sb_sp[:, h, T:384], start=False, stop=True, skip_group_check=True)
                    last = mm(PS[:, 4 + h, T:384], C("suffix"), sb_sp[:, h, T:384], start=True, stop=True, skip_group_check=True)
                last.then_inc(sb_cum, 1)
                pe.wait_ge(sb_w, 1)
                pe.wait_ge(evac_act, e + 6)
                for h in range(4):
                    v = [sb_v[:, s, h * P:h * P + P] for s in range(2)]
                    mm(PS[:, h, 0:P], sb_ln[:, h, 0:P], v[0], start=True, stop=True)
                    mm(PS[:, h, T:T + P], sb_ln[:, h, P:T], v[0], start=True, stop=False)
                    last = mm(PS[:, h, T:T + P], sb_ln[:, h, T:384], v[1], start=False, stop=True)
                last.then_inc(sb_out, 1)
                pe.wait_ge(ab_mixed, 2)
                turn("ab_o")
                square(UNIT0["ab_o"], "ab_o", token_unit)

            def cross(l):
                norm(f"xq{l}")
                square(UNIT0[f"xq{l}"], f"xq{l}", feature_unit)
                pe.wait_ge(evac_act, EVAC0[f"xq{l}"] + 2)
                for h in range(4):
                    for t in range(TT):
                        for d in range(2):
                            last = mm(PS[:, 4 + h, t * T:t * T + T], xa_q[:, 2 * h + d, t * P:t * P + P],
                                      K_of[l][:, 2 * h + d], start=d == 0, stop=d == 1)
                    last.then_inc(xa_scores, 1)
                for h in range(4):
                    pe.wait_ge(xa_probs, 4 * l + h + 1)
                    for m in range(2):
                        for t in range(TT):
                            last = pe.transpose(PS[:, h, m * T + t * P:m * T + t * P + P], xa_p[:, h, t, m * P:m * P + P], ident)
                    last.then_inc(xa_turned, 1)
                for h in range(4):
                    pe.wait_ge((xa_pt_act, xa_pt_dve)[h % 2], 2 * l + h // 2 + 1)
                    for d in range(2):
                        for m in range(2):
                            last = mm(PS[:, 4 + h, d * T:d * T + T], V_of[l][:, m, h * T + d * P:h * T + d * P + P],
                                      xa_pt[:, h, m], start=m == 0, stop=m == 1)
                    last.then_inc(turned, 1)
                square(UNIT0[f"xo{l}"], f"xo{l}", token_unit)

            def wide(name, n, wu):
                u0, h0 = UNIT0[name], HID0[name]

                def second(u, c, q, i, per):
                    pe.wait_ge(hid_lo_done, c + (h0 + 1))
                    for j in range(wu):
                        slot, nn, _ = slot_of(u + j, i, per)
                        pe.wait_ge(lo_done, nn + 1)
                        half = j % 2
                        for k in range(2):
                            f = 2 * (j // 2) + k
                            for t in range(TT):
                                s = slice(t * P, t * P + P)
                                last = three(PS[:, 4 + 2 * t + half, :], hid_hi[:, q, f, s], hid_lo[:, q, f, s],
                                             w_hi[:, slot, k], w_lo[:, slot, k], False, False)
                        last.then_inc(w_used, 1)

                norm(name)
                chunk(u0, name, feature_unit, 0)
                for b in range(4):
                    mm(PS[:, 4 + b, :], zeros[:, 0:P], zeros[:, :], start=True, stop=False, skip_group_check=True)
                pairs = (n - 1) // 2
                per = 2 * (4 + wu)
                with pe.Fori(0, pairs) as i:
                    for q in range(2):
                        u = u0 + 4 + q * (4 + wu)
                        chunk(u, None, feature_unit, 2 * ((q + 1) % 2), 0, i, per)
                        second(u + 4, 2 * i + q, q, i, per)
                for c in range(2 * pairs, n):
                    u = u0 + 4 + c * (4 + wu)
                    if c + 1 < n:
                        chunk(u, None, feature_unit, 2 * ((c + 1) % 2))
                        u += 4
                    second(u, c, c % 2, 0, 0)

            def gdn():
                norm("gdn")
                u0, e = UNIT0["gdn_in"], EVAC0["gdn_in"]
                pe.wait_ge(evac_act, e)
                with pe.Fori(0, 3) as i:
                    for q in range(2):
                        pe.wait_ge(evac_act, e - 1 + q + 2 * i)
                        chunk(u0 + 4 * q, "gdn", feature_unit, 2 * q, 0, i, 8)
                gates(1, 40).then_inc(gd_gates_s, 1)
                pe.wait_ge(evac_act, e + 5)
                chunk(u0 + 24, "gdn", token_unit, 0)
                for b in range(2):
                    pe.wait_ge(gd_sqd, b + 1)
                    if b == 0:
                        pe.wait_ge(gd_rows_s, 1)
                    for h in range(8):
                        last = mm(PS[:, 4 + h // 2, (h % 2) * T:(h % 2) * T + T], ones, gd_sq[:, h], start=True, stop=True)
                    last.then_inc(gd_sums, 1)
                    if b == 0:
                        pe.wait_ge(evac_act, e + 6)
                        chunk(u0 + 28, "gdn", token_unit, 2)
                pe.wait_ge(evac_act, e + 8)
                for c in range(2):
                    pe.transpose(PS[:, 0, 8 * c:8 * c + 8], gd_rows[0:8, 6, c * P:c * P + P], ident[0:8, 0:8])
                    last = pe.transpose(PS[:, 0, 16 + 8 * c:24 + 8 * c], gd_rows[0:8, 0, c * P:c * P + P], ident[0:8, 0:8])
                last.then_inc(gd_colt, 1)
                pe.wait_ge(gd_rooted, 2)
                for h in range(8):
                    last = mm(PS[:, 4 + h // 2, (h % 2) * T:(h % 2) * T + T], C(f"select{h}")[0:8, :], gd_rows[0:8, 6],
                              start=True, stop=True)
                last.then_inc(gd_bcast, 1)
                pe.wait_ge(gd_args, 1)
                for h in range(8):
                    last = mm(PS[:, h // 2, (h % 2) * T:(h % 2) * T + T], C(f"select{h}")[0:8, :], gd_rows[0:8, 0],
                              start=True, stop=True)
                last.then_inc(gd_bcast, 1)

                def system(c, h, base=0):
                    n = 8 * c + h
                    return PS[:, base + n // 4, (n % 4) * P:(n % 4) * P + P]
                pe.wait_ge(gd_normed, 2)
                for c in range(2):
                    for h in range(8):
                        k = gd_qkv[:, 8 + h, c * P:c * P + P]
                        last = mm(system(c, h, 4), k, k, start=True, stop=True)
                last.then_inc(gd_kk, 1)
                pe.wait_ge(gd_bb, 1)
                for c in range(2):
                    for h in range(8):
                        s = slice(c * P, c * P + P)
                        last = mm(system(c, h), gd_qkv[:, 8 + h, s], gd_qkv[:, h, s], start=True, stop=True)
                last.then_inc(gd_qk, 1)
                pe.wait_ge(gd_made, 1)
                for c in range(2):
                    for h in range(8):
                        last = pe.transpose(system(c, h, 4), gd_qkv[:, 16 + h, c * P:c * P + P], ident)
                last.then_inc(gd_vt, 1)
                for h in range(8):
                    last = pe.transpose(system(0, h), gd_qkv[:, 8 + h, 0:P], ident)
                last.then_inc(gd_kt, 1)
                pe.wait_ge(gd_made, 3)

                def group(g, b, h):
                    return PS[:, 4 * g + b + h // 4, (h % 4) * P:(h % 4) * P + P]

                for g in range(2):
                    pe.wait_ge(gd_masked, g + 1)
                    for h in range(8):
                        last = pe.transpose(group(g, 0, h), gd_um[:, g, h], ident)
                    last.then_inc(gd_xps, 1)

                def level(i, last_level=False):
                    for g in range(2):
                        pe.wait_ge(gd_masked, 2 * i + (g + 3))
                        pe.wait_ge(gd_xnew, 2 * i + (g + 1))
                        for h in range(8):
                            last = mm(group(g, 0, h), gd_um[:, g, h], gd_X[:, g, h], start=True, stop=True)
                        last.then_inc(gd_yps, 1)
                    for g in range(2):
                        pe.wait_ge(gd_ysb, 2 * i + (g + 1))
                        for h in range(8):
                            if not last_level:
                                mm(group(g, 2, h), gd_XT[:, g, h], gd_Y[:, g, h], start=True, stop=True)
                            last = mm(group(g, 0, h), gd_Y[:, g, h], gd_XT[:, g, h], start=True, stop=True)
                        last.then_inc(gd_xps, 1)

                with pe.Fori(0, 5) as i:
                    level(i)
                level(5, True)
                pe.wait_ge(gd_xnew, 14)
                for h in range(8):
                    last = mm(group(0, 0, h), gd_XT[:, 0, h], gd_bv[:, 0, h], start=True, stop=True)
                last.then_inc(gd_fin_pe, 1)
                pe.wait_ge(gd_fin_act, 1)
                for h in range(8):
                    mm(group(0, 2, h), gd_E[:, 0, h], gd_vn[:, h], start=True, stop=True)
                    last = mm(group(1, 0, h), gd_kd[:, h], gd_vn[:, h], start=True, stop=True)
                last.then_inc(gd_fin_pe, 1)
                pe.wait_ge(gd_fin_act, 2)
                for h in range(8):
                    last = mm(group(1, 2, h), gd_qkv[:, 8 + h, P:T], gd_S[:, h], start=True, stop=True)
                last.then_inc(gd_fin_pe, 1)
                pe.wait_ge(gd_fin_dve, 1)
                for h in range(8):
                    last = mm(group(0, 0, h), gd_XT[:, 1, h], gd_bv[:, 1, h], start=True, stop=True)
                last.then_inc(gd_fin_pe, 1)
                for h in range(8):
                    mm(group(1, 2, h), gd_qkv[:, h, P:T], gd_S[:, h], start=True, stop=True)
                pe.wait_ge(gd_fin_act, 3)
                for h in range(8):
                    last = mm(group(1, 0, h), gd_E[:, 1, h], gd_vn[:, h], start=True, stop=True)
                last.then_inc(gd_fin_pe, 1)
                pe.wait_ge(gd_mixed, 1)
                turn("gdn_o")
                square(UNIT0["gdn_o"], "gdn_o", token_unit)

            def pool():
                pe.wait_ge(xn_ready, 2 * NORMS.index("pool") + 2)
                for b in range(4):
                    band = C(f"pool{WINDOWS[b]}")
                    for k in range(2):
                        s = slice((2 * b + k) * P, (2 * b + k) * P + P)
                        mm(PS[:, 4 + b, k * T:k * T + T], xn[:, 0, s], band[:, 0:T], start=True, stop=False, skip_group_check=True)
                        last = mm(PS[:, 4 + b, k * T + P:k * T + T], xn[:, 1, s], band[:, T:384], start=False, stop=True,
                                  skip_group_check=True)
                    last.then_inc(turned, 1)
                pe.wait_ge(evac_act, EVAC0["xq1"] + 2)
                for c in range(2):
                    u = UNIT0["pool"] + c
                    pe.wait_ge(lo_done, u + 1)
                    for g in range(2):
                        grp = 2 * c + g
                        kt_pair_wait("pool", grp)
                        for t in range(TT):
                            for k in range(2):
                                ts, ws, ks = slice(t * P, t * P + P), slice(g * T, g * T + T), slice(k * T, k * T + T)
                                last = three(PS[:, 2 * c + t, ws], XTh[:, 2 * grp + k, ts], XTl[:, 2 * grp + k, ts],
                                             w_hi[:, u % RING, g, ks], w_lo[:, u % RING, g, ks], k == 0, k == 1)
                    last.then_inc(w_used, 1)

            def swa():
                norm("swa")
                u0, e = UNIT0["qkv"], EVAC0["qkv"]
                for c in range(2):
                    chunk(u0 + 4 * c, "swa", feature_unit, 2 * c)
                pe.wait_ge(evac_act, e + 1)
                for j in range(4):
                    slot, n, _ = slot_of(u0 + 8 + j, 0, 0)
                    pe.wait_ge(lo_done, n + 1)
                    feature_unit(slot, j, 0, 0, tiles=2)
                    for k in range(2):
                        kt = 2 * j + k
                        for t in range(TT):
                            s = slice(t * P, t * P + P)
                            last = three(PS[:, 1, t * T:t * T + T], XTh[:, kt, s], XTl[:, kt, s], w_hi[:, slot, k, T:512],
                                         w_lo[:, slot, k, T:512], kt == 0 and t == 0, kt == KT - 1)
                    last.then_inc(w_used, 1)
                pe.wait_ge(evac_act, e + 3)

                def scores(grp):
                    if grp:
                        pe.wait_ge(sw_max, grp)
                    for j in range(4):
                        h = 4 * grp + j
                        r = slice(64 * (h % 2), 64 * (h % 2) + 64)
                        q, k = sw_q[r, h // 2], sw_k[r, grp]
                        mm(PS[:, 4 + j, 0:P], q[:, 0:P], k[:, 0:P], start=True, stop=True)
                        last = mm(PS[:, 4 + j, P:384], q[:, P:T], k[:, 0:T], start=True, stop=True)
                    last.then_inc(sw_scores, 1)
                scores(0)
                pe.wait_ge(v_kept, 1)
                for grp in range(4):
                    if grp + 1 < 4:
                        scores(grp + 1)
                    pe.wait_ge(sw_probs, grp + 1)
                    if grp:
                        pe.wait_ge(sw_pted, grp)
                    for j in range(4):
                        for b in range(3):
                            last = pe.transpose(PS[:, j, b * P:b * P + P], sw_s[:, j, b * P:b * P + P], ident)
                    last.then_inc(sw_turned, 1)
                pe.wait_ge(sw_pted, 4)
                for b in range(4):
                    for h in range(4 * b, 4 * b + 4):
                        f, r = h // 2, slice(64 * (h % 2), 64 * (h % 2) + 64)
                        o = (f % 2) * T
                        v = [sw_v[:, s, 64 * (h // 4):64 * (h // 4) + 64] for s in range(2)]
                        mm(PS[r, 4 + b, o:o + P], v[0], sw_pt[:, h, 0:P], start=True, stop=True)
                        mm(PS[r, 4 + b, o + P:o + T], v[0], sw_pt[:, h, P:T], start=True, stop=False)
                        last = mm(PS[r, 4 + b, o + P:o + T], v[1], sw_pt[:, h, T:384], start=False, stop=True)
                    last.then_inc(turned, 1)
                square(UNIT0["swa_o"], "swa_o", token_unit)

            ab()
            cross(0)
            wide("mlp0", FF // 512, 4)
            gdn()
            cross(1)
            wide("mlp1", FF // 512, 4)
            pool()
            wide("ffn0", GLU // 256, 2)
            swa()
            wide("ffn1", GLU // 256, 2)


_INS = ['x', 'mem', 'ab_w_in', 'ab_b_i', 'ab_b_f', 'ab_head_gain', 'ab_w_out', 'c_w_in', 'c_conv_w', 'c_a_log',
        'c_dt_bias', 'c_head_gain', 'c_w_out', 'xa_norm', 'mem_norm', 'mix_norm', 'xa_wq', 'xa_wk', 'xa_wv', 'xa_wo',
        'mlp_norm', 'mlp_w1', 'mlp_w2', 'final_norm', 'pool_w_2', 'pool_b_2', 'pool_scale_2', 'attn_w_qkv_2',
        'attn_b_qkv_2', 'attn_sinks_2', 'attn_w_o_2', 'norm_mix_2', 'norm_ffn_2', 'ffn_w_in_2', 'ffn_conv_w_2',
        'ffn_conv_b_2', 'ffn_w_out_2', 'norm_f_2']


def kernel(**inputs):
    import concourse.bacc as _bacc
    from concourse.bass_utils import run_bass_kernel_spmd as _run

    nc = _bacc.Bacc("TRN2", target_bir_lowering=False, num_devices=1)
    arrays, args = {}, {}
    for name in _INS + ["const"]:
        v = CONST if name == "const" else np.ascontiguousarray(inputs[name])
        arrays[f"in_{name}"] = v
        args[name] = nc.dram_tensor(f"in_{name}", v.shape, mybir.dt.from_np(v.dtype), kind="ExternalInput").ap()
    out = nc.dram_tensor("out_0", (1, T, D), F32, kind="ExternalOutput").ap()
    program(nc, args, out)
    r = _run(nc, [arrays], core_ids=[0])
    return r.results[0]["out_0"]
```

```python
import math

import numpy as np

import concourse.bass as bass
from concourse import mybir
from contextlib import ExitStack

F32 = mybir.dt.float32
F32R = mybir.dt.float32r
ACT = mybir.ActivationFunctionType
ALU = mybir.AluOpType
AX = mybir.AxisListType
ds = bass.ds

P = 128
T = 256
TT = T // P
D = 1024
KT = D // P
RING = 4
NEG = -1e30
EPS = 1e-6
LEVELS = 7
WINDOWS = (2, 4, 8, 16)
SWA_HEADS = 16
FF = 4096
GLU = 2816
HID0 = {"mlp0": 0, "mlp1": FF // 512, "ffn0": 2 * (FF // 512), "ffn1": 2 * (FF // 512) + GLU // 256}
NORMS = ["mem", "ab", "gdn", "pool", "ffn0", "swa", "ffn1"]
XN_LAST = 2 * len(NORMS) + 2
POOL_SET = {"start": 3, "ab": 4, "gdn": 5, "ffn0": 6, "ffn1": 7}
MISC = 16 * 11


def shape_constants():
    i, j = np.arange(P)[:, None], np.arange(P)[None, :]
    parts = {}
    parts["ident"] = i == j
    parts["ones"] = np.ones((P, P))
    parts["suffix"] = i >= j
    parts["causal_min"] = np.concatenate([np.where(i <= j, 0, NEG), np.zeros((P, P))], 1)
    parts["causal_add"] = np.where(i <= j, 0, NEG)
    parts["strict"] = i < j
    parts["strict_min"] = np.where(i < j, 0, NEG)
    for b in range(LEVELS):
        parts[f"level{b}"] = ((i >> (b + 1)) == (j >> (b + 1))) & (((i >> b) & 1) == 0) & (((j >> b) & 1) == 1)
    for h in range(8):
        parts[f"select{h}"] = np.repeat(i == h, P, 1)
    parts["unit_col"] = np.repeat(np.arange(79)[None, :] == 39, P, 0)
    s, t = np.arange(T)[:, None], np.arange(T)[None, :]
    for w in WINDOWS:
        m = ((s <= t) & (s > t - w)) / np.minimum(t + 1, w) - (s == t)
        parts[f"pool{w}"] = np.concatenate([m[:P], m[P:, P:]], 1)
    dist = np.concatenate([i - j, i + P - j, i - j], 1)
    parts["dist"] = dist
    parts["band_add"] = np.where((dist >= 0) & (dist < P), 0, NEG)
    at, arrays, n = {}, [], 0
    for name, v in parts.items():
        at[name] = (n, v.shape[1])
        arrays.append(v.astype(np.float32))
        n += v.shape[1]
    return np.ascontiguousarray(np.concatenate(arrays, 1)), at


CONST, CONST_AT = shape_constants()

VECTORS = [
    [("mem_norm", 0, 8), ("mix_norm", 0, 16), ("xa_norm", 0, 16), ("mlp_norm", 0, 16), ("norm_mix_2", 0, 16),
     ("ab_head_gain", 0, 4), ("c_head_gain", 0, 1), ("attn_b_qkv_2", 0, 12)],
    [("c_conv_w", 0, 96)],
    [("ffn_conv_w_2", 0, 88)],
    [("ffn_conv_w_2", 88, 44), ("ffn_conv_b_2", 0, 44)],
    [("ffn_conv_w_2", 132, 88)],
    [("ffn_conv_w_2", 220, 44), ("ffn_conv_b_2", 44, 44)],
]

STREAM = [("memkv", 32), ("ab_in", 24), ("ab_o", 8), ("xq0", 8), ("xo0", 8), ("mlp0", 64),
          ("gdn_in", 32), ("gdn_o", 8), ("xq1", 8), ("xo1", 8), ("mlp1", 64),
          ("pool", 2), ("ffn0", 66), ("qkv", 12), ("swa_o", 8), ("ffn1", 66)]
UNIT0, UNITS = {}, 0
for _name, _n in STREAM:
    UNIT0[_name] = UNITS
    UNITS += _n

TURNS = ["mem", "ab", "ab_o", "xq0", "xo0", "mlp0", "gdn", "gdn_o", "xq1", "xo1", "mlp1", "pool", "ffn0", "swa",
         "swa_o", "ffn1"]
ROOTS = [("mem", 2, 2, 1 / D), ("ab", 2, 2, 1 / D), ("ab_heads", 1, 8, 1 / 128), ("xq0", 2, 2, 1 / D),
         ("mlp0", 2, 2, 1 / D), ("gdn", 2, 2, 1 / D), ("gdn_heads0", 1, 8, 1 / 128), ("gdn_heads1", 1, 8, 1 / 128), ("xq1", 2, 2, 1 / D),
         ("mlp1", 2, 2, 1 / D), ("final1", 2, 2, 1 / D), ("pool", 2, 2, 1 / D), ("ffn0", 2, 2, 1 / D),
         ("swa", 2, 2, 1 / D), ("ffn1", 2, 2, 1 / D), ("final2", 2, 2, 1 / D)]
X_COUNT = {"ab": 0, "xq0": 2, "mlp0": 4, "gdn": 6, "xq1": 8, "mlp1": 10, "final1": 12, "pool": 14, "ffn0": 16,
           "swa": 18, "ffn1": 20, "final2": 22}
EVACS = [("memkv", 8), ("ab_in", 6), ("xq0", 2), ("gdn_in", 8), ("xq1", 2), ("qkv", 3)]
EVAC0, _n = {}, 0
for _name, _k in EVACS:
    EVAC0[_name] = _n
    _n += _k


def root_at(name):
    n = 0
    for k, (who, signals, _, _) in enumerate(ROOTS):
        n += signals
        if who == name:
            return n, k
    raise KeyError(name)


class Order:

    def __init__(self, eng, sem):
        self.eng, self.sem, self.count, self.turn = eng, sem, 0, 0

    def __call__(self, ins):
        ins.then_inc(self.sem, 1)
        self.count += 1
        self.eng.wait_ge(self.sem, self.turn + self.count)

    def loop(self, i, per):
        self.turn, self.start, self.per = i * per, self.count, per

    def end(self, turns):
        assert self.count - self.start == self.per, (self.count - self.start, self.per)
        self.turn, self.count = 0, self.start + turns * self.per


def program(nc, a, out):
    ctx = ExitStack()
    with ctx:
        first = (nc.sbuf_base + 63) // 64 * 64
        SLAB = 53120
        ctx.enter_context(nc.sbuf_tensor("slab", [P, SLAB], F32))
        place = [0]

        def at(name, shape, word, dt=F32):
            n = int(np.prod(shape))
            assert word + n <= SLAB, (name, word + n)
            return nc.alloc_sbuf_tensor_at(name, [P] + list(shape), dt, offset=first + 4 * word)

        def sb(name, shape, dt=F32):
            t = at(name, shape, place[0], dt)
            place[0] += (int(np.prod(shape)) + 7) // 8 * 8
            return t

        PS = ctx.enter_context(nc.psum_tensor("PS", [P, 8, 512], F32))
        x = sb("x", [TT, D])
        xn_at = place[0]
        xn = sb("xn", [TT, D])
        xt_at = place[0]
        XTh = sb("XTh", [KT, T], F32R)
        XTl = sb("XTl", [KT, T], F32R)
        w_raw = sb("w_raw", [RING, 2, 512])
        w_hi = sb("w_hi", [RING, 2, 512], F32R)
        w_lo = sb("w_lo", [RING, 2, 512], F32R)
        const = sb("const", [CONST.shape[1]])
        cols = sb("cols", [len(VECTORS), P])
        zeros = sb("zeros", [512], F32R)
        gate_w = sb("gate_w", [2, KT, 40])
        ss = sb("ss", [16])
        var = sb("var", [16])
        rstd = sb("rstd", [16])
        inv_ms = sb("inv_ms", [2])
        neghalf = sb("neghalf", [16])
        eps_col = sb("eps_col", [1])
        gbias = sb("gbias", [8])
        ffn_gain = sb("ffn_gain", [2, KT])
        sinks = sb("sinks", [SWA_HEADS])
        vbias = sb("vbias", [256])
        K1 = sb("K1", [KT, T])
        V1 = sb("V1", [TT, D])
        arena_at = place[0]
        shared_at = SLAB - 4096
        K0 = at("K0", [KT, T], shared_at)
        V0 = at("V0", [TT, D], shared_at + 2048)
        bc = at("bc", [4, D], shared_at)
        hid_hi = at("hid_hi", [2, 4, T], shared_at - 4096, F32R)
        hid_lo = at("hid_lo", [2, 4, T], shared_at - 2048, F32R)
        K_of, V_of = [K0, K1], [V0, V1]

        class Arena:

            def __init__(self, tag, start=arena_at, end=shared_at):
                self.tag, self.word, self.end = tag, start, end

            def __call__(self, name, *shape):
                t = at(f"{self.tag}_{name}", list(shape), self.word)
                self.word += (int(np.prod(shape)) + 7) // 8 * 8
                assert self.word <= self.end, (name, self.word - self.end)
                return t

        A = Arena("start")
        vec_rows = A("vec_rows", len(VECTORS), P)

        A = Arena("ab")
        ab_qk = A("qk", 4, T)
        ab_v = A("v", TT, 4, 132)
        ab_og = A("og", TT, 512)
        sb_q, sb_k = A("sq", 4, T), A("sk", 4, T)
        sb_v = A("sv", TT, 512)
        ab_rows = A("rows", 13, T)
        acol = A("acol", 2, 4)
        mcol = A("mcol", 2, 4)
        emcol = A("emcol", 2, 4)
        decay_at = A.word
        decay = A("decay", 4, 384)
        prob = A("prob", 4, 384)
        sb_zs, sb_sp = A("zs", 4, 384), A("sp", 4, 384)
        sb_ln = prob
        rden = A("rden", 4, 2)
        hsq = at("ab_hsq", [TT, 512], decay_at)
        hmix = xn

        A = Arena("xa")
        xa_q = A("q", KT, T)
        xa_p = A("p", 4, TT, T)
        xa_pt = A("pt", 4, 2, T)
        xa_m, xa_nm, xa_s, xa_r, xa_rs = A("m", 8), A("nm", 8), A("s", 8), A("r", 8), A("rs", 4)

        A = Arena("mlp", end=shared_at - 4096)
        relu = A("relu", 2, 4, T)
        relu2 = A("relu2", 2, 4, T)

        A = Arena("glu", end=shared_at - 4096)
        glu_pad = A("pad", 2, 4, 264)
        glu_acc = A("acc", 2, 4, T)
        glu_silu = A("silu", 2, 2, T)
        glu_prod = A("prod", 2, 2, T)

        A = Arena("gd", end=SLAB)
        gd_qkv = A("qkv", 24, T)
        gd_gate = A("gate", TT, D)
        gd_E = A("E", 2, 8, P)
        over = A.word
        gd_U = A("U", 2, 8, P)
        gd_X = A("X", 2, 8, P)
        gd_XT = A("XT", 2, 8, P)
        gd_bv = A("bv", 2, 8, P)
        gd_kd = A("kd", 8, P)
        gd_um = at("gd_um", [2, 8, P], arena_at + 16 * T)
        A = Arena("gdc", start=over, end=SLAB)
        gd_pad = A("pad", 2, 4, 264)
        gd_acc = A("acc", 2, 4, T)
        gd_sq = [at("gd_sqq", [8, T], over - 2048), at("gd_sqk", [8, T], over - 4096)]
        gd_rows = at("gd_rows", [8, T], xn_at)
        gd_Y = at("gd_Y", [2, 8, P], xt_at)
        gd_S = at("gd_S", [8, P], xt_at + 2048)
        gd_vn = at("gd_vn", [8, P], xt_at + 3072)
        gd_o = xn
        gd_osqt = at("gd_osqt", [2, D], over + 2048)
        A = Arena("gds", start=arena_at + 19472, end=SLAB)
        gd_cols = A("cols", 7, 8)
        gd_eg, gd_beg, gd_kdc, gd_gl = A("eg", 8), A("beg", 8), A("kdc", 8), A("gl", 8)
        gd_nea, gd_last = A("nea", 8), A("last", 8)

        A = Arena("swa")
        sw_q = A("q", KT, T)
        sw_k = A("k", 4, T)
        sw_v = A("v", TT, T)
        sw_s = A("s", 4, 384)
        sw_pt = A("pt", 16, 384)
        sw_m, sw_nm, sw_sum = A("m", 2, 16), A("nm", 2, 16), A("sum", 2, 16)
        sw_es, sw_r = A("es", 2, 16), A("r", 2, 16)
        sw_qb = A("qb", 8)

        def C(name):
            n, w = CONST_AT[name]
            return const[:, n:n + w]

        def vec_at(name, k):
            for b, rows in enumerate(VECTORS):
                n = 0
                for who, r0, count in rows:
                    if who == name and r0 <= k < r0 + count:
                        return b, n + k - r0
                    n += count
            raise KeyError(name)

        def vec(name, k, i=0):
            b, n = vec_at(name, k)
            return cols[:, b, ds(n + i, 1)] if not isinstance(i, int) else cols[:, b, n + i:n + i + 1]

        ident, ones = C("ident"), C("ones")
        one_col = ones[:, 0:1]

        def f32(t):
            return t.bitcast(F32)

        def sem(name):
            return ctx.enter_context(nc.semaphore(name))

        raw_landed = [sem(f"raw_landed{s}") for s in range(RING)]
        hi_done, lo_done, w_used = sem("hi_done"), sem("lo_done"), sem("w_used")
        const_landed, vec_landed, x_landed = sem("const_landed"), sem("vec_landed"), sem("x_landed")
        mem_landed, misc_landed, bc_landed = sem("mem_landed"), sem("misc_landed"), sem("bc_landed")
        out_landed, gate_zeroed, pool_set = sem("out_landed"), sem("gate_zeroed"), sem("pool_set")
        vec_turned, vec_kept = sem("vec_turned"), sem("vec_kept")
        x_updates, evac_act, v_kept = sem("x_updates"), sem("evac_act"), sem("v_kept")
        sq_done, rstd_done, xn_ready, squared = sem("sq_done"), sem("rstd_done"), sem("xn_ready"), sem("squared")
        turned, xt_hi, xt_lo = sem("turned"), sem("xt_hi"), sem("xt_lo")
        act_order, dve_order, pool_order = sem("act_order"), sem("dve_order"), sem("pool_order")
        hid_in, hid_hi_done, hid_lo_done = sem("hid_in"), sem("hid_hi_done"), sem("hid_lo_done")
        glu_in, glu_conv, glu_silued, glu_mult = sem("glu_in"), sem("glu_conv"), sem("glu_silued"), sem("glu_mult")
        (ab_gates, ab_f, ab_lnf, ab_rows_done, ab_turned, ab_args, ab_decayed, ab_scores, ab_probs, ab_outs, ab_norm,
         ab_sq, ab_mixed) = [sem(f"ab_{n}_s") for n in (
             "gates", "f", "lnf", "rows", "turned", "args", "decayed", "scores", "probs", "outs", "norm", "sq", "mixed")]
        sb_z, sb_kept, sb_lned, sb_sped, sb_cum, sb_arg, sb_w, sb_out = [
            sem(f"sb_{n}_s") for n in ("z", "kept", "ln", "sp", "cum", "arg", "w", "out")]
        xa_scores, xa_max, xa_exp, xa_probs, xa_turned, xa_pt_act, xa_pt_dve = [
            sem(f"xa_{n}_s") for n in ("scores", "max", "exp", "probs", "turned", "pt_act", "pt_dve")]
        (gd_conv, gd_free, gd_gates_s, gd_f, gd_lnf, gd_rows_s, gd_sqd, gd_sums, gd_rooted, gd_logs, gd_colt,
         gd_colk, gd_exps, gd_bcast, gd_args, gd_decayed, gd_kk, gd_qk, gd_vt, gd_tok, gd_scaled, gd_made, gd_masked,
         gd_yps, gd_ysb, gd_xps, gd_xnew, gd_fin_pe, gd_fin_act, gd_fin_dve, gd_mixed, gd_osq_s) = [
             sem(f"gd_{n}_s") for n in (
                 "conv", "free", "gates", "f", "lnf", "rows", "sqd", "sums", "rooted", "logs", "colt", "colk",
                 "exps", "bcast", "args", "decayed", "kk", "qk", "vt", "tok", "scaled", "made", "masked", "yps", "ysb",
                 "xps", "xnew", "fin_pe", "fin_act", "fin_dve", "mixed", "osq")]
        sw_scores, sw_max, sw_exp, sw_probs, sw_turned, sw_pted, sw_den = [
            sem(f"sw_{n}_s") for n in ("scores", "max", "exp", "probs", "turned", "pted", "den")]

        def group_banks(g, b):
            lo = 4 * (1 - g) + b
            return PS[:, lo:lo + 2, :].rearrange("p b (k t) -> p b k t", k=4)

        def halves(v, size, which):
            return v.rearrange("p h (a w t) -> p h a w t", w=2, t=size)[:, :, :, which, :]

        block = ctx.enter_context(nc.Block())

        def slot_of(u, i, per):
            assert per % RING == 0
            return u % RING, u + per * i, u // RING + (per // RING) * i


        @block.sync
        def _(sp):
            def load(u, src, i=0, per=0, halves=False):
                slot, n, _ = slot_of(u, i, per)
                if u >= RING:
                    sp.wait_ge(lo_done, n - RING + 1)
                dst = w_raw[:, slot].rearrange("p k (h n) -> p (k h) n", h=2) if halves else w_raw[:, slot]
                sp.dma_start(dst, src).then_inc(raw_landed[slot], 16)

            def rows_of(W, k, c):
                return W.rearrange("(k p) n -> p k n", p=P)[:, ds(k, 2), ds(c, 512)]

            def load_chunk(u, W, c, i=0, per=0):
                for j in range(4):
                    load(u + j, rows_of(W, 2 * j, c), i, per)

            def load_square(u, W):
                with sp.Fori(0, 2) as i:
                    load_chunk(u, W, i * 512, i, 4)

            def load_wide(u0, n, wu, load_first, load_second):
                per = 2 * (4 + wu)
                load_first(u0, 0, 0, 0)
                pairs = (n - 1) // 2
                with sp.Fori(0, pairs) as i:
                    for q in range(2):
                        u = u0 + 4 + q * (4 + wu)
                        load_first(u, q + 1 + 2 * i, i, per)
                        load_second(u + 4, q + 2 * i, i, per)
                for c in range(2 * pairs, n):
                    u = u0 + 4 + c * (4 + wu)
                    if c + 1 < n:
                        load_first(u, c + 1, 0, 0)
                        u += 4
                    load_second(u, c, 0, 0)

            def load_mlp(u0, W1, W2):
                load_wide(u0, FF // 512, 4,
                          lambda u, c, i, per: load_chunk(u, W1, c * 512, i, per),
                          lambda u, c, i, per: [load(u + 2 * k + h, rows_of(W2, c * 4 + 2 * k, h * 512), i, per)
                                                for k in range(2) for h in range(2)])

            def load_glu(u0, W1, W2):
                W = W1.rearrange("(p k) (h n) -> p (k h) n", p=P, h=2)

                def first_layer(u, c, i, per):
                    for j in range(4):
                        load(u + j, W[:, 4 * j:4 * j + 4, ds(c * 256, 256)], i, per, halves=True)
                load_wide(u0, GLU // 256, 2, first_layer,
                          lambda u, c, i, per: [load(u + h, rows_of(W2, c * 2, h * 512), i, per) for h in range(2)])

            sp.dma_start(const[:, :], a["const"]).then_inc(const_landed, 16)
            sp.dma_start(xn[:, :, :], a["mem"][0].rearrange("(t p) n -> p t n", p=P)).then_inc(mem_landed, 16)
            for b, rows in enumerate(VECTORS):
                n = 0
                for who, r0, count in rows:
                    src = a[who]
                    if len(src.shape) == 3:
                        src = src.rearrange("a b c -> (a b c)")
                    elif len(src.shape) == 2:
                        src = src.rearrange("a b -> (a b)")
                    src = src.rearrange("(r c) -> r c", c=P)[r0:r0 + count, :]
                    sp.dma_start(vec_rows[n:n + count, b, :], src).then_inc(vec_landed, 16)
                    n += count
            load_chunk(0, a["xa_wk"][0], 0)
            sp.dma_start(x[:, :, :], a["x"][0].rearrange("(t p) n -> p t n", p=P)).then_inc(x_landed, 16)
            sp.wait_ge(gate_zeroed, 1)
            abg = a["ab_w_in"][0].rearrange("(k p) n -> p k n", p=P)
            cg = a["c_w_in"][0].rearrange("(k p) n -> p k n", p=P)
            with nc.allow_non_contiguous_dma("gate columns and per-partition values"):
                for dst, src in (
                        (gate_w[:, 0, :, 0:4], abg[:, :, 1536:1540]), (gate_w[:, 0, :, 32:36], abg[:, :, 1540:1544]),
                        (gate_w[:, 1, :, 0:8], cg[:, :, 4096:4104]), (gate_w[:, 1, :, 32:40], cg[:, :, 4104:4112]),
                        (gbias[0:4, 0:1], a["ab_b_i"].rearrange("a n -> n a")),
                        (gbias[32:36, 0:1], a["ab_b_f"].rearrange("a n -> n a")),
                        (gbias[0:8, 1:2], a["c_a_log"].rearrange("a n -> n a")),
                        (gbias[32:40, 1:2], a["c_dt_bias"].rearrange("a n -> n a")),
                        (ffn_gain[:, :, :], a["norm_ffn_2"].rearrange("l (p k) -> p l k", p=P)),
                        (sinks[:, :], a["attn_sinks_2"].broadcast_to([P, SWA_HEADS])),
                        (vbias[:, :], a["attn_b_qkv_2"][:, 1280:1536].broadcast_to([P, 256]))):
                    sp.dma_start(dst, src).then_inc(misc_landed, 16)
            load_chunk(4, a["xa_wk"][0], 512)
            load_square(8, a["xa_wv"][0])
            load_square(16, a["xa_wk"][1])
            load_square(24, a["xa_wv"][1])

            def ab():
                for k, c in enumerate((0, 512, 1024, 1544, 2056, 2568)):
                    load_chunk(UNIT0["ab_in"] + 4 * k, a["ab_w_in"][0], c)
                load_square(UNIT0["ab_o"], a["ab_w_out"][0])

            def cross(l):
                load_square(UNIT0[f"xq{l}"], a["xa_wq"][l])
                load_square(UNIT0[f"xo{l}"], a["xa_wo"][l])
                if l == 1:
                    sp.wait_ge(x_updates, X_COUNT["xq1"])
                    for k, who in enumerate(("final_norm", "norm_f_2", "pool_b_2", "pool_scale_2")):
                        src = a[who]
                        if len(src.shape) == 3:
                            src = src.rearrange("a b c -> a (b c)")
                        elif len(src.shape) == 1:
                            src = src.rearrange("(a n) -> a n", a=1)
                        sp.dma_start(bc[:, k, :], src.broadcast_to([P, D])).then_inc(bc_landed, 16)

            def gdn():
                with sp.Fori(0, 8) as i:
                    load_chunk(UNIT0["gdn_in"], a["c_w_in"][0], i * 512, i, 4)
                load_square(UNIT0["gdn_o"], a["c_w_out"][0])

            def pool():
                for k in range(2):
                    u = UNIT0["pool"] + k
                    sp.wait_ge(lo_done, u - RING + 1)
                    sp.dma_start(w_raw[:, u % RING].rearrange("p g (k n) -> p (g k) n", k=2),
                                 a["pool_w_2"][0, 2 * k:2 * k + 2].rearrange("g (k p) n -> p (g k) n", p=P))\
                        .then_inc(raw_landed[u % RING], 16)

            def swa():
                with sp.Fori(0, 3) as i:
                    load_chunk(UNIT0["qkv"], a["attn_w_qkv_2"][0], i * 512, i, 4)
                load_square(UNIT0["swa_o"], a["attn_w_o_2"][0])

            ab()
            cross(0)
            load_mlp(UNIT0["mlp0"], a["mlp_w1"][0], a["mlp_w2"][0])
            gdn()
            cross(1)
            load_mlp(UNIT0["mlp1"], a["mlp_w1"][1], a["mlp_w2"][1])
            pool()
            load_glu(UNIT0["ffn0"], a["ffn_w_in_2"][0], a["ffn_w_out_2"][0])
            swa()
            load_glu(UNIT0["ffn1"], a["ffn_w_in_2"][1], a["ffn_w_out_2"][1])
            sp.wait_ge(xn_ready, XN_LAST)
            sp.dma_start(out[0].rearrange("(t p) n -> p t n", p=P), xn[:, :, :]).then_inc(out_landed, 16)
            sp.wait_ge(out_landed, 16)

        @block.gpsimd
        def _(pool):
            order = Order(pool, pool_order)
            pool.memset(gate_w[:, :, :, :], 0.0).then_inc(gate_zeroed, 1)
            pool.memset(f32(zeros[:, :]), 0.0).then_inc(pool_set, 1)
            pool.memset(neghalf[:, :], -0.5).then_inc(pool_set, 1)
            pool.memset(eps_col[:, :], EPS).then_inc(pool_set, 1)
            pool.wait_ge(pool_set, POOL_SET["start"])

            def root(name):
                signals, k = root_at(name)
                _, _, n, scale = ROOTS[k]
                pool.wait_ge(sq_done, signals)
                order(pool.tensor_scalar(var[:, :n], ss[:, :n], scale, EPS, ALU.mult, ALU.add))
                pool.tensor_tensor(rstd[:, :n], var[:, :n], neghalf[:, :n], ALU.pow).then_inc(rstd_done, 1)

            root("mem")
            pool.wait_ge(vec_kept, 1)
            pool.memset(ab_v[:, :, :, 128:129], 1.0).then_inc(pool_set, 1)
            root("ab")
            root("ab_heads")
            root("xq0")
            root("mlp0")
            pool.wait_ge(x_updates, X_COUNT["gdn"])
            pool.memset(gd_pad[:, 0, :, 0:3], 0.0).then_inc(pool_set, 1)
            pool.memset(gd_pad[:, 1, :, 0:3], 0.0).then_inc(gd_free, 2)
            root("gdn")
            pool.wait_ge(gd_tok, 2)
            pool.wait_ge(gd_exps, 1)

            def by_column(v, column):
                return pool.tensor_tensor(v, v, column.unsqueeze(2).broadcast_to([P, 8, P]), ALU.mult)
            by_column(gd_kd[:, :, :], gd_kdc[:, :]).then_inc(gd_scaled, 1)
            for c in range(2):
                by_column(gd_bv[:, c], gd_cols[:, 2 + c]).then_inc(gd_scaled, 1)
            root("gdn_heads0")
            root("gdn_heads1")
            root("xq1")
            root("mlp1")
            root("final1")
            root("pool")
            pool.wait_ge(x_updates, X_COUNT["ffn0"])
            pool.memset(glu_pad[:, :, :, 0:2], 0.0).then_inc(pool_set, 1)
            root("ffn0")
            root("swa")
            pool.wait_ge(x_updates, X_COUNT["ffn1"])
            pool.memset(glu_pad[:, :, :, 0:2], 0.0).then_inc(pool_set, 1)
            root("ffn1")
            root("final2")

        @block.scalar
        def _(act):
            order = Order(act, act_order)
            nxt = [0]

            def split(u, i=0, per=0):
                slot, n, uses = slot_of(u, i, per)
                if u >= RING:
                    act.wait_ge(w_used, n - RING + 1)
                act.wait_ge(raw_landed[slot], 16 * uses + 16)
                act.activation(w_hi[:, slot], w_raw[:, slot], ACT.Copy).then_inc(hi_done, 1)

            def splits(n):
                for _ in range(n):
                    if nxt[0] < UNITS:
                        split(nxt[0])
                    nxt[0] += 1

            def chunk_done(u, i=0, per=0):
                act.wait_ge(w_used, u + per * i + 1)

            def squares(src, dst=None):
                for t in range(TT):
                    act.activation(xn[:, t] if dst is None else dst[:, 4 * t:4 * t + 4].rearrange("p k t -> p (k t)"), src[:, t], ACT.Square,
                                   accum_out=ss[:, t:t + 1]).then_inc(sq_done, 1)

            def activations(turn, gain):
                n = TURNS.index(turn)
                for b in range(4):
                    act.wait_ge(turned, 4 * n + b + 1)
                    for k in (2 * b, 2 * b + 1):
                        act.activation(XTh[:, k], PS[:, 4 + b, (k % 2) * T:(k % 2) * T + T], ACT.Copy,
                                       scale=gain(k)).then_inc(xt_hi, 1)

            def norm(name, gain):
                act.wait_ge(x_updates, X_COUNT[name])
                squares(x)
                activations(name, gain)

            def late_norm(name, gain):
                activations(name, gain)
                act.wait_ge(x_updates, X_COUNT[name])
                squares(x)

            def square_evac(u0, evac, n=2):
                assert nxt[0] == u0 + RING, (nxt[0], u0)
                with act.Fori(0, n) as i:
                    for j in range(3):
                        split(u0 + RING + j, i, 4)
                    chunk_done(u0 + 3, i, 4)
                    evac(i).then_inc(evac_act, 1)
                    split(u0 + RING + 3, i, 4)
                nxt[0] += 4 * n

            def to_features(dst):
                return lambda i: act.activation(dst[:, ds(4 * i, 4), :].rearrange("p (b k) t -> p b k t", b=2),
                                                PS[:, ds(2 * i, 2), :].rearrange("p b (k t) -> p b k t", k=2), ACT.Copy)

            def to_tokens(dst, func=ACT.Copy):
                return lambda i: act.activation(dst[:, :, ds(512 * i, 512)], PS[:, ds(2 * i, 2), :], func)

            splits(4)
            act.wait_ge(mem_landed, 16)
            squares(xn, dst=K0)
            act.wait_ge(vec_kept, 1)
            activations("mem", lambda k: vec("mem_norm", k))
            for k, (dst, kind) in enumerate(((K0, to_features), (V0, to_tokens), (K1, to_features), (V1, to_tokens))):
                square_evac(8 * k, kind(dst))

            def ab():
                act.wait_ge(x_landed, 16)
                norm("ab", lambda k: vec("mix_norm", k))
                u = UNIT0["ab_in"]
                splits(3)
                chunk_done(u + 3)
                act.activation(ab_qk[:, 0:2], PS[:, 0, :].rearrange("p (k t) -> p k t", k=2), ACT.Copy)
                act.activation(ab_qk[:, 2:4], PS[:, 1, :].rearrange("p (k t) -> p k t", k=2), ACT.Copy,
                               scale=64 ** -0.5).then_inc(evac_act, 1)
                splits(1)
                act.wait_ge(ab_f, 1)
                act.activation(ab_rows[0:4, 2], ab_rows[0:4, 0], ACT.Tanh)
                order(act.activation(ab_rows[0:4, 3], ab_rows[0:4, 1], ACT.Abs))
                order(act.activation(ab_rows[0:4, 4], ab_rows[0:4, 3], ACT.Exp, scale=-1.0))
                act.activation(ab_rows[0:4, 5], ab_rows[0:4, 4], ACT.Ln, bias=1.0).then_inc(ab_lnf, 1)
                splits(3)
                chunk_done(u + 7)
                act.activation(ab_v[:, :, :, 0:128], PS[:, 2:4, :].rearrange("p t (h d) -> p t h d", h=4),
                               ACT.Copy).then_inc(evac_act, 1)
                splits(1)
                splits(3)
                chunk_done(u + 11)
                act.activation(ab_og[:, :, :], PS[:, 0:2, :], ACT.Sigmoid).then_inc(evac_act, 1)
                splits(1)
                act.wait_ge(ab_args, 1)
                act.activation(emcol[:, :, :], mcol[:, :, :], ACT.Exp)
                act.activation(decay[:, :, :], decay[:, :, :], ACT.Exp).then_inc(ab_decayed, 1)
                splits(3)
                chunk_done(u + 15)
                act.activation(sb_q[:, :, :].rearrange("p (b k) t -> p b k t", b=2),
                               PS[:, 2:4, :].rearrange("p b (k t) -> p b k t", k=2), ACT.Copy,
                               scale=128 ** -0.5).then_inc(evac_act, 1)
                splits(1)
                act.wait_ge(ab_norm, 1)
                act.activation(hsq[:, :, :], hmix[:, :, 0:512], ACT.Square).then_inc(ab_sq, 1)
                splits(3)
                chunk_done(u + 19)
                act.activation(sb_k[:, :, :].rearrange("p (b k) t -> p b k t", b=2),
                               PS[:, 0:2, :].rearrange("p b (k t) -> p b k t", k=2), ACT.Copy).then_inc(evac_act, 1)
                splits(1)
                act.wait_ge(sb_kept, 1)
                order(act.activation(sb_ln[:, :, :], sb_zs[:, :, :], ACT.Abs))
                order(act.activation(sb_ln[:, :, :], sb_ln[:, :, :], ACT.Exp, scale=-1.0))
                act.activation(sb_ln[:, :, :], sb_ln[:, :, :], ACT.Ln, bias=1.0).then_inc(sb_lned, 1)
                splits(3)
                chunk_done(u + 23)
                act.activation(sb_v[:, :, :], PS[:, 2:4, :], ACT.Copy).then_inc(evac_act, 1)
                act.wait_ge(sb_arg, 1)
                act.activation(sb_ln[:, :, :], sb_zs[:, :, :], ACT.Exp).then_inc(sb_w, 1)
                splits(1)
                act.wait_ge(sb_out, 1)
                act.activation(hmix[:, :, 512:].rearrange("p t (h d) -> p h t d", h=4),
                               PS[:, 0:4, :].rearrange("p h (t d) -> p h t d", t=2)[:, :, :, 0:128],
                               ACT.Copy).then_inc(ab_mixed, 1)
                activations("ab_o", lambda k: vec("ab_head_gain", k) if k < 4 else one_col)
                splits(8)

            def cross(l):
                late_norm(f"xq{l}", lambda k: vec("xa_norm", 8 * l + k))
                square_evac(UNIT0[f"xq{l}"], to_features(xa_q))

                def copy_pt(h):
                    act.wait_ge(xa_turned, 4 * l + h + 1)
                    act.activation(xa_pt[:, h], PS[:, h, :].rearrange("p (m t) -> p m t", m=2),
                                   ACT.Copy).then_inc(xa_pt_act, 1)
                for h in range(4):
                    act.wait_ge(xa_max, 4 * l + h + 1)
                    for t in range(TT):
                        act.activation(xa_p[:, h, t], PS[:, 4 + h, t * T:t * T + T], ACT.Exp, scale=xa_rs[:, t:t + 1],
                                       bias=xa_nm[:, 2 * h + t:2 * h + t + 1],
                                       accum_out=xa_s[:, 2 * h + t:2 * h + t + 1]).then_inc(xa_exp, 1)
                for h in (0, 2):
                    copy_pt(h)
                activations(f"xo{l}", lambda k: one_col)
                splits(8)

            def mlp(l):
                late_norm(f"mlp{l}", lambda k: vec("mlp_norm", 8 * l + k))
                u0, n, wu = UNIT0[f"mlp{l}"], FF // 512, 4
                h0 = HID0[f"mlp{l}"]

                def hidden(c, q, u_last, i, per):
                    chunk_done(u_last, i, per)
                    act.activation(relu[:, q].rearrange("p (b k) t -> p b k t", b=2),
                                   PS[:, 2 * q:2 * q + 2, :].rearrange("p b (k t) -> p b k t", k=2),
                                   ACT.Relu).then_inc(hid_in, 1)
                    act.wait_ge(hid_in, c + (h0 + 1))
                    act.activation(hid_hi[:, q], relu[:, q], ACT.Square).then_inc(hid_hi_done, 1)

                splits(4)
                hidden(0, 0, u0 + 3, 0, 0)
                u1 = nxt[0]
                pairs = (n - 1) // 2
                per = 2 * (4 + wu)
                with act.Fori(0, pairs) as i:
                    for q in range(2):
                        for j in range(4 + wu):
                            split(u1 + q * (4 + wu) + j, i, per)
                            if j == wu - 1:
                                hidden(q + 1 + 2 * i, (q + 1) % 2, u0 + 7 + q * (4 + wu), i, per)
                nxt[0] = u1 + pairs * per
                splits(4)
                hidden(n - 1, (n - 1) % 2, u0 + 3 + 4 + (n - 2) * (4 + wu), 0, 0)
                splits(4)
                splits(4)

            def glu(l):
                norm(f"ffn{l}", lambda k: ffn_gain[:, l, k:k + 1])
                u0, n, wu = UNIT0[f"ffn{l}"], GLU // 256, 2
                h0, g0 = HID0[f"ffn{l}"], (GLU // 256) * l

                def tap(part, c, k):
                    return vec("ffn_conv_w_2", 132 * l + 88 + 22 * part + k, 2 * c)

                def hidden(c, q, u_last, i, per, fill):
                    chunk_done(u_last, i, per)
                    src = PS[:, 2 * q:2 * q + 2, :].rearrange("p b (k t) -> p b k t", k=2)
                    act.activation(glu_pad[:, q, :, 2:2 + T].rearrange("p (b k) t -> p b k t", b=2), src, ACT.Copy)
                    for f in range(4):
                        part, k = f // 2, f % 2
                        last = act.activation(glu_acc[:, q, f], PS[:, 2 * q + f // 2, (f % 2) * T:(f % 2) * T + T],
                                              ACT.Identity, scale=tap(part, c, k),
                                              bias=vec("ffn_conv_b_2", 44 * l + 22 * part + k, 2 * c))
                    last.then_inc(glu_in, 1)
                    fill[0]()
                    act.wait_ge(glu_conv, c + (g0 + 1))
                    act.activation(glu_silu[:, q], glu_acc[:, q, 2:4], ACT.Silu).then_inc(glu_silued, 1)
                    fill[1]()
                    act.wait_ge(glu_mult, c + (g0 + 1))
                    act.activation(hid_hi[:, q, 0:2], glu_prod[:, q], ACT.Copy).then_inc(hid_hi_done, 1)

                splits(4)
                u1 = nxt[0]
                hidden(0, 0, u0 + 3, 0, 0, (lambda: splits(1), lambda: splits(1)))
                assert nxt[0] == u1 + 2
                pairs = (n - 3) // 2
                per = 2 * (4 + wu)
                one = lambda: splits(1)
                with act.Fori(0, pairs) as i:
                    for q in range(2):
                        v = u1 + 2 + q * (4 + wu)
                        for j in range(4):
                            split(v + j, i, per)
                        hidden(q + 1 + 2 * i, (q + 1) % 2, u0 + 7 + q * (4 + wu), i, per,
                               (lambda v=v: split(v + 4, i, per), lambda v=v: split(v + 5, i, per)))
                nxt[0] = u1 + 2 + pairs * per
                splits(4)
                hidden(n - 2, (n - 2) % 2, u0 + 7 + (n - 3) * (4 + wu), 0, 0, (one, one))
                splits(2)
                hidden(n - 1, (n - 1) % 2, u0 + 7 + (n - 2) * (4 + wu), 0, 0, (lambda: None, lambda: None))
                splits(4)

            def gdn():
                norm("gdn", lambda k: vec("mix_norm", 8 + k))
                u0 = UNIT0["gdn_in"]
                act.wait_ge(pool_set, POOL_SET["gdn"])
                with act.Fori(0, 3) as i:
                    for q in range(2):
                        for j in range(3):
                            split(u0 + 4 + 4 * q + j, i, 8)
                        chunk_done(u0 + 4 * q + 3, i, 8)
                        act.activation(gd_pad[:, q, :, 3:3 + T].rearrange("p (b k) t -> p b k t", b=2),
                                       PS[:, 2 * q:2 * q + 2, :].rearrange("p b (k t) -> p b k t", k=2), ACT.Copy)
                        for f in range(4):
                            last = act.activation(gd_acc[:, q, f], PS[:, 2 * q + f // 2, (f % 2) * T:(f % 2) * T + T],
                                                  ACT.Copy, scale=vec("c_conv_w", 72 + 4 * q + f, 8 * i))
                        last.then_inc(gd_free, 1)
                        split(u0 + 4 + 4 * q + 3, i, 8)
                        act.wait_ge(gd_conv, 2 * i + (q + 1))
                        act.activation(gd_qkv[:, ds(8 * i + 4 * q, 4), :], gd_acc[:, q], ACT.Silu).then_inc(evac_act, 1)
                nxt[0] += 24
                for b in range(2):
                    act.activation(gd_sq[b][:, :, :], gd_qkv[:, 8 * b:8 * b + 8], ACT.Square).then_inc(gd_sqd, 1)
                act.wait_ge(gd_f, 1)
                order(act.activation(gd_rows[0:8, 3:5], gd_rows[0:8, 1:3], ACT.Abs))
                order(act.activation(gd_rows[0:8, 3:5], gd_rows[0:8, 3:5], ACT.Exp, scale=-1.0))
                act.activation(gd_nea[0:8, 1:2], gbias[0:8, 1:2], ACT.Exp)
                act.activation(gd_rows[0:8, 3:5], gd_rows[0:8, 3:5], ACT.Ln, bias=1.0).then_inc(gd_lnf, 1)
                act.wait_ge(gd_vt, 1)
                act.activation(gd_kd[:, :, :].rearrange("p (b k) t -> p b k t", b=2),
                               PS[:, 0:2, :].rearrange("p b (k t) -> p b k t", k=4), ACT.Copy).then_inc(gd_tok, 1)
                act.activation(gd_bv[:, :, :, :].rearrange("p c (b k) t -> p (c b) k t", k=4),
                               PS[:, 2:6, :].rearrange("p b (k t) -> p b k t", k=4), ACT.Copy).then_inc(gd_tok, 1)
                act.wait_ge(gd_rows_s, 1)
                act.activation(gd_rows[0:8, 0], gd_rows[0:8, 7], ACT.Exp)
                act.wait_ge(gd_sums, 1)
                act.activation(gd_rows[0:8, 1], PS[0:8, 6, 0:T], ACT.Ln, bias=eps_col[0:8, :])
                act.activation(gd_rows[0:8, 2], PS[32:40, 6, 0:T], ACT.Ln, bias=eps_col[32:40, :]).then_inc(gd_rooted, 1)
                splits(3)
                chunk_done(u0 + 27)
                act.activation(gd_gate[:, :, 0:512], PS[:, 0:2, :], ACT.Silu).then_inc(evac_act, 1)
                splits(1)
                act.wait_ge(gd_colk, 2)
                act.activation(gd_beg[:, :], gd_cols[:, 4], ACT.Exp)
                act.activation(gd_eg[:, :], gd_cols[:, 5], ACT.Exp)
                act.activation(gd_kdc[:, :], gd_gl[:, :], ACT.Exp).then_inc(gd_exps, 1)
                act.wait_ge(gd_args, 1)
                act.activation(gd_U[:, :, :, :], gd_U[:, :, :, :], ACT.Exp).then_inc(gd_decayed, 1)
                splits(2)
                act.wait_ge(gd_args, 2)
                act.activation(gd_E[:, :, :, :], gd_E[:, :, :, :], ACT.Exp).then_inc(gd_decayed, 1)
                splits(1)
                chunk_done(u0 + 31)
                act.activation(gd_gate[:, :, 512:D], PS[:, 2:4, :], ACT.Silu).then_inc(evac_act, 1)
                splits(1)
                with act.Fori(0, LEVELS - 1) as i:
                    for g in range(2):
                        act.wait_ge(gd_yps, 2 * i + (g + 1))
                        act.activation(gd_Y[:, g].rearrange("p (b k) t -> p b k t", b=2), group_banks(g, 0),
                                       ACT.Copy).then_inc(gd_ysb, 1)
                for n, (dst, bank) in enumerate(((gd_vn, 0), (gd_S, 4), (gd_vn, 0))):
                    act.wait_ge(gd_fin_pe, n + 1 if n < 2 else 4)
                    act.activation(dst[:, :, :].rearrange("p (b k) t -> p b k t", b=2),
                                   PS[:, bank:bank + 2, :].rearrange("p b (k t) -> p b k t", k=4),
                                   ACT.Copy).then_inc(gd_fin_act, 1)
                    if n == 1:
                        order(act.activation(gd_o[:, 0].rearrange("p (b n) -> p b n", b=2), PS[:, 2:4, :], ACT.Copy))
                        act.activation(gd_osqt[:, 0], gd_o[:, 0], ACT.Square).then_inc(gd_osq_s, 1)
                act.wait_ge(gd_fin_pe, 5)
                act.activation(gd_o[:, 1].rearrange("p (b n) -> p b n", b=2), PS[:, 4:6, :], ACT.Copy).then_inc(gd_fin_act, 1)
                act.wait_ge(gd_fin_dve, 2)
                act.activation(gd_osqt[:, 1], gd_o[:, 1], ACT.Square).then_inc(gd_osq_s, 1)
                activations("gdn_o", lambda k: vec("c_head_gain", 0))
                splits(8)

            def pool():
                act.wait_ge(x_updates, X_COUNT["final1"])
                squares(x)
                norm("pool", lambda k: vec("norm_mix_2", k))
                splits(2)

            def swa():
                norm("swa", lambda k: vec("norm_mix_2", 8 + k))
                u0 = UNIT0["qkv"]
                act.wait_ge(sw_den, 1)
                for c in range(2):
                    splits(3)
                    chunk_done(u0 + 4 * c + 3)
                    for f in range(4):
                        last = act.activation(sw_q[:, 4 * c + f], PS[:, 2 * (c % 2) + f // 2, (f % 2) * T:(f % 2) * T + T],
                                              ACT.Identity, scale=0.125, bias=sw_qb[:, 4 * c + f:4 * c + f + 1])
                    last.then_inc(evac_act, 1)
                    splits(1)
                splits(3)
                chunk_done(u0 + 11)
                for g in range(4):
                    r = slice(64 * (g % 2), 64 * (g % 2) + 64)
                    b, n = vec_at("attn_b_qkv_2", 8 + g // 2)
                    for half in range(2):
                        last = act.activation(sw_k[64 * half:64 * half + 64, g], PS[r, 0, (g // 2) * T:(g // 2) * T + T],
                                              ACT.Identity, bias=cols[r, b, n:n + 1])
                last.then_inc(evac_act, 1)
                splits(1)
                for grp in range(4):
                    act.wait_ge(sw_max, grp + 1)
                    for t in range(2):
                        act.activation(sw_es[:, t, 4 * grp:4 * grp + 4], sw_es[:, t, 4 * grp:4 * grp + 4], ACT.Exp)
                        for j in range(4):
                            h = 4 * grp + j
                            v = sw_s[:, j, 0:128] if t == 0 else sw_s[:, j, 128:384]
                            act.activation(v, v, ACT.Exp, bias=sw_nm[:, t, h:h + 1],
                                           accum_out=sw_sum[:, t, h:h + 1]).then_inc(sw_exp, 1)
                    act.wait_ge(sw_turned, grp + 1)
                    act.activation(sw_pt[:, 4 * grp:4 * grp + 4], PS[:, 0:4, 0:384], ACT.Copy).then_inc(sw_pted, 1)
                activations("swa_o", lambda k: one_col)
                splits(8)

            ab()
            cross(0)
            mlp(0)
            gdn()
            cross(1)
            mlp(1)
            pool()
            glu(0)
            swa()
            glu(1)
            act.wait_ge(x_updates, X_COUNT["final2"])
            squares(x)

        @block.vector
        def _(dve):
            order = Order(dve, dve_order)
            nxt = [0]

            def split(u, i=0, per=0):
                slot, n, _ = slot_of(u, i, per)
                dve.wait_ge(hi_done, n + 1)
                dve.tensor_tensor(w_lo[:, slot], w_raw[:, slot], f32(w_hi[:, slot]), ALU.subtract).then_inc(lo_done, 1)

            def splits(n):
                for _ in range(n):
                    if nxt[0] < UNITS:
                        split(nxt[0])
                    nxt[0] += 1

            def activations(turn, gain):
                n = TURNS.index(turn)
                for k in range(KT):
                    dve.wait_ge(xt_hi, 8 * n + 2 * (k // 2) + 2)
                    dve.scalar_tensor_tensor(XTl[:, k], PS[:, 4 + k // 2, (k % 2) * T:(k % 2) * T + T], gain(k),
                                             f32(XTh[:, k]), ALU.mult, ALU.subtract).then_inc(xt_lo, 1)

            def scale_rows(name, src):
                dve.wait_ge(rstd_done, root_at(name)[1] + 1)
                for t in range(TT):
                    dve.tensor_scalar(xn[:, t], src[:, t], rstd[:, t:t + 1], None, ALU.mult).then_inc(xn_ready, 1)

            def norm(name, gain):
                scale_rows(name, x)
                activations(name, gain)

            def late_norm(name, gain):
                activations(name, gain)

            def square_splits(u0, n=2):
                with dve.Fori(0, n) as i:
                    for j in range(4):
                        split(u0 + RING + j, i, 4)
                nxt[0] += 4 * n

            def square_add(u0):
                with dve.Fori(0, 2) as i:
                    for j in range(3):
                        split(u0 + RING + j, i, 4)
                    dve.wait_ge(w_used, u0 + 4 + 4 * i)
                    xs = x[:, :, ds(512 * i, 512)]
                    dve.tensor_tensor(xs, PS[:, ds(2 * i, 2), :], xs, ALU.add).then_inc(x_updates, 1)
                    split(u0 + RING + 3, i, 4)
                nxt[0] += 8

            def wide_add(u_last, late=None):
                if late:
                    dve.wait_ge(rstd_done, root_at(late)[1] + 1)
                    dve.tensor_tensor(inv_ms[:, :], rstd[:, 0:2], rstd[:, 0:2], ALU.mult).then_inc(squared, 1)
                    dve.wait_ge(squared, 1 if late == "mlp0" else 2)
                splits(3)
                dve.wait_ge(w_used, u_last + 1)
                for t in range(TT):
                    xs = x[:, t].rearrange("p (b n) -> p b n", b=2)
                    y = PS[:, 4 + 2 * t:6 + 2 * t, :]
                    if late:
                        add = dve.scalar_tensor_tensor(xs, y, inv_ms[:, t:t + 1], xs, ALU.mult, ALU.add)
                    else:
                        add = dve.tensor_tensor(xs, y, xs, ALU.add)
                    add.then_inc(x_updates, 1)
                splits(1)

            def by_heads(v):
                return v.rearrange("p t (h d) -> p h t d", h=4)

            dve.wait_ge(vec_turned, 1)
            for b, rows in enumerate(VECTORS):
                n = sum(count for _, _, count in rows)
                last = dve.tensor_copy(cols[:, b, 0:n], PS[:, b // 4, (b % 4) * P:(b % 4) * P + n])
            last.then_inc(vec_kept, 1)
            splits(4)
            dve.wait_ge(mem_landed, 16)
            scale_rows("mem", xn)
            activations("mem", lambda k: vec("mem_norm", k))
            square_splits(0, 8)

            def ab():
                norm("ab", lambda k: vec("mix_norm", k))
                dve.wait_ge(misc_landed, MISC)
                splits(4)
                dve.wait_ge(ab_gates, 1)
                dve.tensor_scalar(ab_rows[0:4, 0], PS[0:4, 7, 0:T], gbias[0:4, 0:1], 1 / 15, ALU.add, ALU.mult)
                dve.tensor_scalar(ab_rows[0:4, 1], PS[32:36, 7, 0:T], gbias[32:36, 0:1], None, ALU.add).then_inc(ab_f, 1)
                dve.wait_ge(ab_lnf, 1)
                r = ab_rows
                order(dve.scalar_tensor_tensor(r[0:4, 6], r[0:4, 1], 0.0, r[0:4, 5], ALU.min, ALU.subtract))
                order(dve.tensor_tensor_scan(r[0:4, 8], r[0:4, 6], f32(zeros[0:4, 0:T]), 0.0, ALU.add, ALU.add))
                order(dve.scalar_tensor_tensor(r[0:4, 9], r[0:4, 2], 15.0, r[0:4, 8], ALU.mult, ALU.subtract))
                order(dve.tensor_tensor_scan(r[0:4, 10], r[0:4, 9], f32(zeros[0:4, 0:T]), 0.0, ALU.max, ALU.add))
                dve.tensor_scalar(r[0:4, 11], r[0:4, 10], -1.0, None, ALU.mult)
                dve.scalar_tensor_tensor(r[0:4, 12], r[0:4, 8], -1.0, r[0:4, 10], ALU.mult, ALU.subtract).then_inc(ab_rows_done, 1)
                splits(4)
                dve.wait_ge(ab_turned, 1)
                dve.tensor_copy(mcol[:, :, :], PS[:, 6, 8:16].rearrange("p (t h) -> p t h", t=2))
                order(dve.tensor_copy(acol[:, :, :], PS[:, 6, 0:8].rearrange("p (t h) -> p t h", t=2)))
                for h in range(4):
                    o = (h % 2) * T
                    dve.scalar_tensor_tensor(decay[:, h, 0:T], PS[:, 4 + h // 2, o:o + T], acol[:, 0, h:h + 1],
                                             C("causal_min"), ALU.add, ALU.min)
                    last = dve.scalar_tensor_tensor(decay[:, h, T:384], PS[:, 4 + h // 2, o + P:o + T],
                                                    acol[:, 1, h:h + 1], C("causal_min")[:, 0:P], ALU.add, ALU.min)
                last.then_inc(ab_args, 1)
                splits(4)
                dve.wait_ge(ab_scores, 1)
                dve.wait_ge(ab_decayed, 1)
                dve.tensor_tensor(prob[:, :, :], PS[:, 4:8, 0:384], decay[:, :, :], ALU.mult).then_inc(ab_probs, 1)
                splits(4)
                dve.wait_ge(ab_outs, 1)
                o = PS[:, 4:8, :].rearrange("p h (t d) -> p h t d", t=2)
                order(dve.tensor_copy(rden[:, :, :], o[:, :, :, 128]))
                order(dve.scalar_tensor_tensor(rden[:, :, :], rden[:, :, :], -1.0, rden[:, :, :], ALU.mult, ALU.max))
                order(dve.tensor_tensor(rden[:, :, :], rden[:, :, :], emcol[:, :, :].rearrange("p t h -> p h t"), ALU.max))
                order(dve.reciprocal(rden[:, :, :], rden[:, :, :]))
                hm = by_heads(hmix[:, :, 0:512])
                dve.tensor_tensor(hm, o[:, :, :, 0:128], rden[:, :, :].unsqueeze(3).broadcast_to([P, 4, 2, 128]),
                                  ALU.mult).then_inc(ab_norm, 1)
                dve.wait_ge(ab_sq, 1)
                dve.tensor_reduce(ss[:, 0:8], hsq[:, :, :].rearrange("p t (h d) -> p (t h) d", h=4), AX.X,
                                  ALU.add).then_inc(sq_done, 1)
                splits(4)
                dve.wait_ge(sb_z, 1)
                dve.tensor_copy(sb_zs[:, :, :], PS[:, 4:8, 0:384]).then_inc(sb_kept, 1)
                dve.wait_ge(sb_lned, 1)
                order(dve.scalar_tensor_tensor(sb_sp[:, :, :], sb_zs[:, :, :], 0.0, sb_ln[:, :, :], ALU.max, ALU.add))

                def diagonals(v):
                    return v[:, :, :].rearrange("p h (b t) -> p h b t", b=3)[:, :, 0:3:2, :]

                def mask(name):
                    return C(name).unsqueeze(1).unsqueeze(1).broadcast_to([P, 4, 2, P])
                dve.tensor_tensor(diagonals(sb_sp), diagonals(sb_sp), mask("strict"), ALU.mult).then_inc(sb_sped, 1)
                dve.wait_ge(rstd_done, root_at("ab_heads")[1] + 1)
                hv = hmix[:, :, 0:512].rearrange("p t (h d) -> p t h d", h=4)
                order(dve.tensor_tensor(hv, hv, rstd[:, 0:8].rearrange("p (t h) -> p t h", t=2).unsqueeze(3)
                                        .broadcast_to([P, 2, 4, 128]), ALU.mult))
                dve.tensor_tensor(hmix[:, :, 0:512], hmix[:, :, 0:512], ab_og[:, :, :], ALU.mult).then_inc(ab_mixed, 1)
                dve.wait_ge(sb_cum, 1)
                order(dve.tensor_tensor(sb_zs[:, :, :], sb_zs[:, :, :], PS[:, 4:8, 0:384], ALU.subtract))
                dve.tensor_tensor(diagonals(sb_zs), diagonals(sb_zs), mask("strict_min"), ALU.min).then_inc(sb_arg, 1)
                splits(4)
                activations("ab_o", lambda k: vec("ab_head_gain", k) if k < 4 else one_col)
                square_add(UNIT0["ab_o"])

            def cross(l):
                late_norm(f"xq{l}", lambda k: vec("xa_norm", 8 * l + k))
                square_splits(UNIT0[f"xq{l}"])
                dve.wait_ge(rstd_done, root_at(f"xq{l}")[1] + 1)
                dve.tensor_scalar(xa_rs[:, 0:2], rstd[:, 0:2], 1 / 16, None, ALU.mult)
                order(dve.tensor_scalar(xa_rs[:, 2:4], rstd[:, 0:2], -1 / 16, None, ALU.mult))

                def maxima(h):
                    dve.wait_ge(xa_scores, 4 * l + h + 1)
                    m = slice(2 * h, 2 * h + 2)
                    order(dve.tensor_reduce(xa_m[:, m], PS[:, 4 + h, :].rearrange("p (t s) -> p t s", t=2), AX.X,
                                            ALU.max))
                    dve.tensor_tensor(xa_nm[:, m], xa_m[:, m], xa_rs[:, 2:4], ALU.mult).then_inc(xa_max, 1)

                def normalise(h):
                    dve.wait_ge(xa_exp, 8 * l + 2 * h + 2)
                    order(dve.reciprocal(xa_r[:, 2 * h:2 * h + 2], xa_s[:, 2 * h:2 * h + 2]))
                    for t in range(TT):
                        last = dve.tensor_scalar(xa_p[:, h, t], xa_p[:, h, t], xa_r[:, 2 * h + t:2 * h + t + 1], None, ALU.mult)
                    last.then_inc(xa_probs, 1)

                def copy_pt(h):
                    dve.wait_ge(xa_turned, 4 * l + h + 1)
                    dve.tensor_copy(xa_pt[:, h], PS[:, h, :].rearrange("p (m t) -> p m t", m=2)).then_inc(xa_pt_dve, 1)
                maxima(0)
                maxima(1)
                normalise(0)
                maxima(2)
                normalise(1)
                maxima(3)
                normalise(2)
                normalise(3)
                copy_pt(1)
                copy_pt(3)
                activations(f"xo{l}", lambda k: one_col)
                square_add(UNIT0[f"xo{l}"])

            def mlp(l):
                late_norm(f"mlp{l}", lambda k: vec("mlp_norm", 8 * l + k))
                u0, n, wu = UNIT0[f"mlp{l}"], FF // 512, 4
                h0 = HID0[f"mlp{l}"]

                def hidden(c, q):
                    dve.wait_ge(hid_in, c + (h0 + 1))
                    order(dve.tensor_tensor(relu2[:, q], relu[:, q], relu[:, q], ALU.mult))
                    dve.wait_ge(hid_hi_done, c + (h0 + 1))
                    dve.tensor_tensor(hid_lo[:, q], relu2[:, q], f32(hid_hi[:, q]), ALU.subtract).then_inc(hid_lo_done, 1)

                splits(4)
                hidden(0, 0)
                u1 = nxt[0]
                pairs = (n - 1) // 2
                per = 2 * (4 + wu)
                with dve.Fori(0, pairs) as i:
                    order.loop(i, 2)
                    for q in range(2):
                        for j in range(4 + wu):
                            split(u1 + q * (4 + wu) + j, i, per)
                            if j == wu - 1:
                                hidden(q + 1 + 2 * i, (q + 1) % 2)
                    order.end(pairs)
                nxt[0] = u1 + pairs * per
                splits(4)
                hidden(n - 1, (n - 1) % 2)
                splits(4)
                wide_add(u0 + n * (4 + wu) - 1, late=f"mlp{l}")

            def glu(l):
                norm(f"ffn{l}", lambda k: ffn_gain[:, l, k:k + 1])
                u0, n, wu = UNIT0[f"ffn{l}"], GLU // 256, 2
                h0, g0 = HID0[f"ffn{l}"], (GLU // 256) * l
                dve.wait_ge(pool_set, POOL_SET[f"ffn{l}"])

                def hidden(c, q, fill):
                    dve.wait_ge(glu_in, c + (g0 + 1))
                    for tap in range(2):
                        for f in range(4):
                            part, k = f // 2, f % 2
                            last = dve.scalar_tensor_tensor(
                                glu_acc[:, q, f], glu_pad[:, q, f, tap:tap + T],
                                vec("ffn_conv_w_2", 132 * l + 44 * tap + 22 * part + k, 2 * c), glu_acc[:, q, f],
                                ALU.mult, ALU.add)
                        if tap == 0:
                            order(last)
                    last.then_inc(glu_conv, 1)
                    fill[0]()
                    dve.wait_ge(glu_silued, c + (g0 + 1))
                    dve.tensor_tensor(glu_prod[:, q], glu_acc[:, q, 0:2], glu_silu[:, q], ALU.mult).then_inc(glu_mult, 1)
                    fill[1]()
                    dve.wait_ge(hid_hi_done, c + (h0 + 1))
                    dve.tensor_tensor(hid_lo[:, q, 0:2], glu_prod[:, q], f32(hid_hi[:, q, 0:2]), ALU.subtract)\
                        .then_inc(hid_lo_done, 1)

                one = lambda: splits(1)
                splits(4)
                hidden(0, 0, (one, one))
                v0 = nxt[0]
                pairs = (n - 3) // 2
                per = 2 * (4 + wu)
                with dve.Fori(0, pairs) as i:
                    order.loop(i, 2)
                    for q in range(2):
                        v = v0 + q * (4 + wu)
                        for j in range(4):
                            split(v + j, i, per)
                        hidden(q + 1 + 2 * i, (q + 1) % 2,
                               (lambda v=v: split(v + 4, i, per), lambda v=v: split(v + 5, i, per)))
                    order.end(pairs)
                nxt[0] = v0 + pairs * per
                splits(4)
                hidden(n - 2, (n - 2) % 2, (one, one))
                splits(2)
                hidden(n - 1, (n - 1) % 2, (lambda: None, lambda: None))
                wide_add(u0 + n * (4 + wu) - 1)

            def gdn():
                norm("gdn", lambda k: vec("mix_norm", 8 + k))
                u0 = UNIT0["gdn_in"]
                dve.wait_ge(pool_set, POOL_SET["gdn"])
                with dve.Fori(0, 3) as i:
                    order.loop(i, 4)
                    for q in range(2):
                        for j in range(3):
                            split(u0 + 4 + 4 * q + j, i, 8)
                        dve.wait_ge(gd_free, 2 * i + (q + 3))
                        for tap in range(3):
                            for f in range(4):
                                last = dve.scalar_tensor_tensor(
                                    gd_acc[:, q, f], gd_pad[:, q, f, tap:tap + T],
                                    vec("c_conv_w", 24 * tap + 4 * q + f, 8 * i), gd_acc[:, q, f], ALU.mult, ALU.add)
                            if tap < 2:
                                order(last)
                        last.then_inc(gd_conv, 1)
                        split(u0 + 4 + 4 * q + 3, i, 8)
                    order.end(3)
                nxt[0] += 24
                R = gd_rows
                dve.wait_ge(gd_gates_s, 1)
                dve.tensor_scalar(R[0:8, 1], PS[32:40, 7, 0:T], gbias[32:40, 1:2], None, ALU.add)
                dve.tensor_copy(R[0:8, 2], PS[0:8, 7, 0:T]).then_inc(gd_f, 1)
                dve.wait_ge(gd_lnf, 1)
                dve.scalar_tensor_tensor(R[0:8, 7], R[0:8, 2], 0.0, R[0:8, 4], ALU.min, ALU.subtract)
                order(dve.scalar_tensor_tensor(R[0:8, 5], R[0:8, 1], 0.0, R[0:8, 3], ALU.max, ALU.add))
                order(dve.tensor_scalar(R[0:8, 5], R[0:8, 5], gd_nea[0:8, 1:2], -1.0, ALU.mult, ALU.mult))
                for c in range(2):
                    s = slice(c * P, c * P + P)
                    last = dve.tensor_tensor_scan(R[0:8, 6, s], R[0:8, 5, s], f32(zeros[0:8, 0:P]), 0.0, ALU.add, ALU.add)
                last.then_inc(gd_rows_s, 1)
                dve.wait_ge(gd_rows_s, 1)
                dve.wait_ge(gd_rooted, 1)
                order(dve.tensor_tensor(R[0:8, 7], R[0:8, 7], R[0:8, 6], ALU.add))
                dve.scalar_tensor_tensor(R[0:8, 3], R[0:8, 2], -0.5, R[0:8, 7], ALU.mult, ALU.add)
                order(dve.tensor_scalar(R[0:8, 1], R[0:8, 1], -0.5, -0.5 * math.log(128), ALU.mult, ALU.add))
                dve.tensor_tensor(R[0:8, 4], R[0:8, 1], R[0:8, 6], ALU.add)
                dve.tensor_scalar(gd_last[0:8, :], ident[0:8, 0:8], R[0:8, 6, P - 1:P], None, ALU.mult)
                dve.scalar_tensor_tensor(R[0:8, 5], R[0:8, 2], 0.5, R[0:8, 6], ALU.mult, ALU.add).then_inc(gd_logs, 1)
                splits(3)
                dve.wait_ge(gd_colt, 1)
                dve.tensor_copy(gd_cols[:, :, :], PS[:, 6, 0:56].rearrange("p (k h) -> p k h", h=8)).then_inc(gd_colk, 1)
                dve.wait_ge(gd_colk, 1)
                dve.tensor_tensor(gd_gl[:, :], gd_cols[:, 6], gd_cols[:, 0], ALU.subtract).then_inc(gd_colk, 1)
                splits(1)

                def decay_args(dst):
                    for c in range(2):
                        for h in range(8):
                            o = (h % 2) * T + c * P
                            last = dve.scalar_tensor_tensor(dst[:, c, h], PS[:, 4 + h // 2, o:o + P], gd_cols[:, c, h:h + 1],
                                                            C("causal_add"), ALU.subtract, ALU.add)
                    last.then_inc(gd_args, 1)
                dve.wait_ge(gd_bcast, 1)
                decay_args(gd_U)
                splits(2)
                dve.wait_ge(gd_bcast, 2)
                decay_args(gd_E)
                splits(2)
                dve.wait_ge(gd_kk, 1)
                dve.wait_ge(gd_decayed, 1)
                for g in range(2):
                    u = gd_U[:, g].rearrange("p (b k) t -> p b k t", k=4)
                    order(dve.tensor_tensor(u, u, PS[:, 4 + 2 * g:6 + 2 * g, :].rearrange("p b (k t) -> p b k t", k=4),
                                            ALU.mult))

                def wide_mask(name):
                    return C(name).unsqueeze(1).broadcast_to([P, 8, P])

                def masked(g, level):
                    return dve.tensor_tensor(gd_um[:, g], gd_U[:, g], wide_mask(f"level{level}"), ALU.mult)\
                        .then_inc(gd_masked, 1)

                def four(v):
                    return v.rearrange("p (b k) t -> p b k t", k=4)
                masked(0, 0)
                masked(1, 0)
                dve.wait_ge(gd_qk, 1)
                dve.wait_ge(gd_decayed, 2)
                allE = gd_E[:, :, :, :].rearrange("p c (b k) t -> p (c b) k t", k=4)
                dve.tensor_tensor(allE, allE, PS[:, 0:4, :].rearrange("p b (k t) -> p b k t", k=4), ALU.mult)\
                    .then_inc(gd_made, 1)
                dve.wait_ge(gd_masked, 2)
                for g in range(2):
                    dve.tensor_tensor(gd_XT[:, g], wide_mask("ident"), gd_um[:, g], ALU.subtract)
                    dve.wait_ge(gd_xps, g + 1)
                    dve.tensor_tensor(four(gd_X[:, g]), C("ident").unsqueeze(1).unsqueeze(1).broadcast_to([P, 2, 4, P]),
                                      group_banks(g, 0), ALU.subtract).then_inc(gd_xnew, 1)
                    dve.wait_ge(gd_xnew, g + 1)
                    masked(g, 1)
                for level in range(1, LEVELS):
                    size = 2 ** level
                    if level + 1 < LEVELS:
                        for g in range(2):
                            dve.wait_ge(gd_yps, 2 * level + g - 1)
                            masked(g, level + 1)
                    for g in range(2):
                        dve.wait_ge(gd_xps, 2 * level + g + 1)
                        for dst, b, which in ((gd_X, 2, 0), (gd_XT, 0, 1)):
                            if dst is gd_XT or level + 1 < LEVELS:
                                v = halves(dst[:, g], size, which).rearrange("p h a t -> p (h a) t")
                                lo = 4 * (1 - g) + b
                                y = PS[:, lo, :].rearrange("p (n t) -> p n t", t=size)
                                last = dve.tensor_tensor(v, v, y, ALU.subtract)
                        last.then_inc(gd_xnew, 1)
                dve.wait_ge(gd_fin_pe, 3)
                dve.wait_ge(gd_scaled, 3)
                for h in range(8):
                    last = dve.scalar_tensor_tensor(gd_bv[:, 1, h], PS[:, 6 + h // 4, (h % 4) * P:(h % 4) * P + P],
                                                    gd_beg[:, h:h + 1], gd_bv[:, 1, h], ALU.mult, ALU.subtract, reverse1=True)
                last.then_inc(gd_fin_dve, 1)
                def mixed(c):
                    gate = gd_gate[:, c]
                    order(dve.tensor_tensor(gate, gd_o[:, c], gate, ALU.mult))
                    dve.wait_ge(gd_osq_s, c + 1)
                    dve.tensor_reduce(ss[:, 0:8], gd_osqt[:, c].rearrange("p (h d) -> p h d", h=8), AX.X,
                                      ALU.add).then_inc(sq_done, 1)
                    dve.wait_ge(rstd_done, root_at(f"gdn_heads{c}")[1] + 1)
                    dve.tensor_tensor(gd_o[:, c].rearrange("p (h d) -> p h d", h=8), gate.rearrange("p (h d) -> p h d", h=8),
                                      rstd[:, 0:8].unsqueeze(2).broadcast_to([P, 8, P]), ALU.mult).then_inc(gd_mixed, 1)
                dve.wait_ge(gd_osq_s, 1)
                mixed(0)
                dve.wait_ge(gd_fin_act, 4)
                dve.wait_ge(gd_fin_pe, 5)
                for h in range(8):
                    o = gd_o[:, 1, h * P:(h + 1) * P]
                    last = dve.scalar_tensor_tensor(o, PS[:, 6 + h // 4, (h % 4) * P:(h % 4) * P + P], gd_eg[:, h:h + 1], o,
                                                    ALU.mult, ALU.add)
                last.then_inc(gd_fin_dve, 1)
                dve.wait_ge(gd_fin_dve, 2)
                mixed(1)
                activations("gdn_o", lambda k: vec("c_head_gain", 0))
                square_add(UNIT0["gdn_o"])

            def pool():
                dve.wait_ge(bc_landed, 64)
                dve.wait_ge(rstd_done, root_at("final1")[1] + 1)
                for t in range(TT):
                    dve.scalar_tensor_tensor(x[:, t], x[:, t], rstd[:, t:t + 1], bc[:, 0], ALU.mult, ALU.mult)\
                        .then_inc(x_updates, 1)
                scale_rows("pool", x)
                activations("pool", lambda k: vec("norm_mix_2", k))
                splits(2)
                for c in range(2):
                    s = slice(512 * c, 512 * c + 512)
                    dve.wait_ge(w_used, UNIT0["pool"] + c + 1)
                    order(dve.tensor_tensor(xn[:, :, s], PS[:, 2 * c:2 * c + 2, :],
                                            bc[:, 2, s].unsqueeze(1).broadcast_to([P, 2, 512]), ALU.add))
                    order(dve.tensor_tensor(xn[:, :, s], xn[:, :, s], bc[:, 3, s].unsqueeze(1).broadcast_to([P, 2, 512]),
                                            ALU.mult))
                    dve.tensor_tensor(x[:, :, s], x[:, :, s], xn[:, :, s], ALU.add).then_inc(x_updates, 1)

            def swa():
                norm("swa", lambda k: vec("norm_mix_2", 8 + k))
                b, n = vec_at("attn_b_qkv_2", 0)
                dve.tensor_scalar(sw_qb[:, :], cols[:, b, n:n + 8], 0.125, None, ALU.mult).then_inc(sw_den, 1)
                u0 = UNIT0["qkv"]
                splits(12)
                dve.wait_ge(w_used, u0 + 12)
                dve.tensor_tensor(sw_v[:, :, :], PS[:, 1, :].rearrange("p (t n) -> p t n", t=2),
                                  vbias[:, :].unsqueeze(1).broadcast_to([P, 2, T]), ALU.add).then_inc(v_kept, 1)
                for grp in range(4):
                    hs = slice(4 * grp, 4 * grp + 4)
                    dve.wait_ge(sw_scores, grp + 1)
                    if grp:
                        dve.wait_ge(sw_turned, grp)
                    for j in range(4):
                        h = 4 * grp + j
                        last = dve.scalar_tensor_tensor(sw_s[:, j], C("dist"), -float(2.0 ** (-8.0 / SWA_HEADS * (h + 1))),
                                                        PS[:, 4 + j, 0:384], ALU.mult, ALU.add)
                    order(last)
                    order(dve.tensor_tensor(sw_s[:, :, :], sw_s[:, :, :],
                                            C("band_add").unsqueeze(1).broadcast_to([P, 4, 384]), ALU.add))
                    dve.tensor_reduce(sw_m[:, 0, hs], sw_s[:, :, 0:128], AX.X, ALU.max)
                    order(dve.tensor_reduce(sw_m[:, 1, hs], sw_s[:, :, 128:384], AX.X, ALU.max))
                    sk = sinks[:, hs].unsqueeze(1).broadcast_to([P, 2, 4])
                    order(dve.tensor_tensor(sw_m[:, :, hs], sw_m[:, :, hs], sk, ALU.max))
                    dve.tensor_scalar(sw_nm[:, :, hs], sw_m[:, :, hs], -1.0, None, ALU.mult)
                    dve.tensor_tensor(sw_es[:, :, hs], sk, sw_m[:, :, hs], ALU.subtract).then_inc(sw_max, 1)
                    dve.wait_ge(sw_exp, 8 * grp + 8)
                    order(dve.tensor_tensor(sw_r[:, :, hs], sw_sum[:, :, hs], sw_es[:, :, hs], ALU.add))
                    order(dve.reciprocal(sw_r[:, :, hs], sw_r[:, :, hs]))
                    for t, s in ((0, slice(0, 128)), (1, slice(128, 384))):
                        last = dve.tensor_tensor(sw_s[:, :, s], sw_s[:, :, s],
                                                 sw_r[:, t, hs].unsqueeze(2).broadcast_to([P, 4, s.stop - s.start]), ALU.mult)
                    last.then_inc(sw_probs, 1)
                activations("swa_o", lambda k: one_col)
                square_add(UNIT0["swa_o"])

            ab()
            cross(0)
            mlp(0)
            gdn()
            cross(1)
            mlp(1)
            pool()
            glu(0)
            swa()
            glu(1)
            dve.wait_ge(rstd_done, root_at("final2")[1] + 1)
            for t in range(TT):
                dve.scalar_tensor_tensor(xn[:, t], x[:, t], rstd[:, t:t + 1], bc[:, 1], ALU.mult, ALU.mult)\
                    .then_inc(xn_ready, 1)

        @block.tensor
        def _(pe):
            mm = pe.matmul

            def kt_pair_wait(turn, j):
                pe.wait_ge(xt_lo, 8 * TURNS.index(turn) + 2 * j + 2)

            def three(dst, ah, al, bh, bl, first, last):
                mm(dst, ah, bh, start=first, stop=False, skip_group_check=True)
                mm(dst, ah, bl, start=False, stop=False, skip_group_check=True)
                return mm(dst, al, bh, start=False, stop=last, skip_group_check=True)

            def token_unit(slot, j, bank, i, cols_=slice(0, 512)):
                n = cols_.stop - cols_.start
                for k in range(2):
                    for t in range(TT):
                        kt = 2 * j + k
                        last = three(PS[:, ds(bank + 2 * i + t, 1), 0:n].rearrange("p a n -> p (a n)") if not isinstance(i, int)
                                     else PS[:, bank + 2 * i + t, 0:n],
                                     XTh[:, kt, t * P:t * P + P], XTl[:, kt, t * P:t * P + P],
                                     w_hi[:, slot, k, cols_], w_lo[:, slot, k, cols_], kt == 0, kt == KT - 1)
                return last

            def feature_unit(slot, j, bank, i, tiles=4):
                for k in range(2):
                    kt = 2 * j + k
                    for f in range(tiles):
                        if isinstance(i, int):
                            dst = PS[:, bank + 2 * i + f // 2, (f % 2) * T:(f % 2) * T + T]
                        else:
                            dst = PS[:, ds(bank + 2 * i + f // 2, 1), (f % 2) * T:(f % 2) * T + T].rearrange("p a n -> p (a n)")
                        s = slice(f * P, f * P + P)
                        last = three(dst, w_hi[:, slot, k, s], w_lo[:, slot, k, s], XTh[:, kt], XTl[:, kt],
                                     kt == 0 and f % 2 == 0, kt == KT - 1)
                return last

            def chunk(u, turn, unit, bank, bank_i=0, i=0, per=0):
                for j in range(4):
                    slot, n, _ = slot_of(u + j, i, per)
                    if turn:
                        kt_pair_wait(turn, j)
                    pe.wait_ge(lo_done, n + 1)
                    unit(slot, j, bank, bank_i).then_inc(w_used, 1)

            def square(u0, turn, unit):
                with pe.Fori(0, 2) as i:
                    chunk(u0, turn, unit, 0, i, i, 4)

            def turn(name, src=xn, wait=lambda b: None):
                for b in range(4):
                    wait(b)
                    for k in range(2):
                        for t in range(TT):
                            f = 2 * b + k
                            last = pe.transpose(PS[:, 4 + b, k * T + t * P:k * T + t * P + P],
                                                src[:, t, f:D:KT] if name in ("ffn0", "ffn1") else
                                                src[:, t, f * P:f * P + P], ident)
                    last.then_inc(turned, 1)

            def norm(name):
                if name in NORMS:
                    pe.wait_ge(xn_ready, 2 * NORMS.index(name) + 2)
                    turn(name)
                else:
                    turn(name, x, lambda b: pe.wait_ge(x_updates, X_COUNT[name] - 1 + b // 2))

            def gates(which, width):
                for k in range(KT):
                    mm(PS[0:width, 7, 0:T], gate_w[:, which, k, 0:width], f32(XTh[:, k]), start=k == 0, stop=False)
                    last = mm(PS[0:width, 7, 0:T], gate_w[:, which, k, 0:width], f32(XTl[:, k]), start=False, stop=k == KT - 1)
                return last

            pe.wait_ge(const_landed, 16)
            pe.wait_ge(vec_landed, 16 * sum(len(rows) for rows in VECTORS))
            for b, rows in enumerate(VECTORS):
                n = sum(count for _, _, count in rows)
                last = pe.transpose(PS[:, b // 4, (b % 4) * P:(b % 4) * P + n], vec_rows[0:n, b, :], ident[0:n, 0:n])
            last.then_inc(vec_turned, 1)
            norm("mem")
            pe.wait_ge(pool_set, 2)
            pe.wait_ge(vec_kept, 1)
            for k, unit in enumerate((feature_unit, token_unit, feature_unit, token_unit)):
                with pe.Fori(0, 2) as i:
                    if k:
                        pe.wait_ge(evac_act, i + (2 * k - 1))
                    chunk(8 * k, "mem", unit, 0, i, i, 4)

            def ab():
                norm("ab")
                pe.wait_ge(evac_act, EVAC0["ab_in"])
                pe.wait_ge(misc_landed, MISC)
                u, e = UNIT0["ab_in"], EVAC0["ab_in"]
                chunk(u, "ab", feature_unit, 0)
                gates(0, 36).then_inc(ab_gates, 1)
                chunk(u + 4, "ab", token_unit, 2)
                pe.wait_ge(ab_rows_done, 1)
                for t in range(TT):
                    pe.transpose(PS[:, 6, 4 * t:4 * t + 4], ab_rows[0:4, 9, t * P:t * P + P], ident[0:4, 0:4])
                    pe.transpose(PS[:, 6, 8 + 4 * t:12 + 4 * t], ab_rows[0:4, 12, t * P:t * P + P], ident[0:4, 0:4])
                for h in range(4):
                    last = mm(PS[:, 4 + h // 2, (h % 2) * T:(h % 2) * T + T], C(f"select{h}")[0:4, :], ab_rows[0:4, 11],
                              start=True, stop=True)
                last.then_inc(ab_turned, 1)
                pe.wait_ge(evac_act, e + 1)
                chunk(u + 8, "ab", token_unit, 0)
                pe.wait_ge(ab_args, 1)
                for h in range(4):
                    r = slice(64 * (h % 2), 64 * (h % 2) + 64)
                    mm(PS[:, 4 + h, 0:T], ab_qk[r, 2 + h // 2, 0:P], ab_qk[r, h // 2, 0:T], start=True, stop=True)
                    last = mm(PS[:, 4 + h, T:384], ab_qk[r, 2 + h // 2, P:T], ab_qk[r, h // 2, P:T], start=True, stop=True)
                last.then_inc(ab_scores, 1)
                pe.wait_ge(evac_act, e + 2)
                chunk(u + 12, "ab", feature_unit, 2)
                pe.wait_ge(ab_probs, 1)
                pe.wait_ge(pool_set, POOL_SET["ab"])
                for h in range(4):
                    mm(PS[:, 4 + h, 0:129], prob[:, h, 0:P], ab_v[:, 0, h, 0:129], start=True, stop=True)
                    mm(PS[:, 4 + h, T:T + 129], prob[:, h, P:T], ab_v[:, 0, h, 0:129], start=True, stop=False)
                    last = mm(PS[:, 4 + h, T:T + 129], prob[:, h, T:384], ab_v[:, 1, h, 0:129], start=False, stop=True)
                last.then_inc(ab_outs, 1)
                pe.wait_ge(evac_act, e + 3)
                chunk(u + 16, "ab", feature_unit, 0)
                pe.wait_ge(ab_norm, 1)
                pe.wait_ge(evac_act, e + 5)
                for h in range(4):
                    mm(PS[:, 4 + h, 0:T], sb_k[:, h, 0:P], sb_q[:, h, 0:T], start=True, stop=True)
                    last = mm(PS[:, 4 + h, T:384], sb_k[:, h, P:T], sb_q[:, h, P:T], start=True, stop=True)
                last.then_inc(sb_z, 1)
                chunk(u + 20, "ab", token_unit, 2)
                pe.wait_ge(sb_sped, 1)
                for h in range(4):
                    mm(PS[:, 4 + h, 0:T], C("suffix"), sb_sp[:, h, 0:T], start=True, stop=False, skip_group_check=True)
                    mm(PS[:, 4 + h, P:T], ones, sb_sp[:, h, T:384], start=False, stop=True, skip_group_check=True)
                    last = mm(PS[:, 4 + h, T:384], C("suffix"), sb_sp[:, h, T:384], start=True, stop=True, skip_group_check=True)
                last.then_inc(sb_cum, 1)
                pe.wait_ge(sb_w, 1)
                pe.wait_ge(evac_act, e + 6)
                for h in range(4):
                    v = [sb_v[:, s, h * P:h * P + P] for s in range(2)]
                    mm(PS[:, h, 0:P], sb_ln[:, h, 0:P], v[0], start=True, stop=True)
                    mm(PS[:, h, T:T + P], sb_ln[:, h, P:T], v[0], start=True, stop=False)
                    last = mm(PS[:, h, T:T + P], sb_ln[:, h, T:384], v[1], start=False, stop=True)
                last.then_inc(sb_out, 1)
                pe.wait_ge(ab_mixed, 2)
                turn("ab_o")
                square(UNIT0["ab_o"], "ab_o", token_unit)

            def cross(l):
                norm(f"xq{l}")
                square(UNIT0[f"xq{l}"], f"xq{l}", feature_unit)
                pe.wait_ge(evac_act, EVAC0[f"xq{l}"] + 2)
                for h in range(4):
                    for t in range(TT):
                        for d in range(2):
                            last = mm(PS[:, 4 + h, t * T:t * T + T], xa_q[:, 2 * h + d, t * P:t * P + P],
                                      K_of[l][:, 2 * h + d], start=d == 0, stop=d == 1)
                    last.then_inc(xa_scores, 1)
                for h in range(4):
                    pe.wait_ge(xa_probs, 4 * l + h + 1)
                    for m in range(2):
                        for t in range(TT):
                            last = pe.transpose(PS[:, h, m * T + t * P:m * T + t * P + P], xa_p[:, h, t, m * P:m * P + P], ident)
                    last.then_inc(xa_turned, 1)
                for h in range(4):
                    pe.wait_ge((xa_pt_act, xa_pt_dve)[h % 2], 2 * l + h // 2 + 1)
                    for d in range(2):
                        for m in range(2):
                            last = mm(PS[:, 4 + h, d * T:d * T + T], V_of[l][:, m, h * T + d * P:h * T + d * P + P],
                                      xa_pt[:, h, m], start=m == 0, stop=m == 1)
                    last.then_inc(turned, 1)
                square(UNIT0[f"xo{l}"], f"xo{l}", token_unit)

            def wide(name, n, wu):
                u0, h0 = UNIT0[name], HID0[name]

                def second(u, c, q, i, per):
                    pe.wait_ge(hid_lo_done, c + (h0 + 1))
                    for j in range(wu):
                        slot, nn, _ = slot_of(u + j, i, per)
                        pe.wait_ge(lo_done, nn + 1)
                        half = j % 2
                        for k in range(2):
                            f = 2 * (j // 2) + k
                            for t in range(TT):
                                s = slice(t * P, t * P + P)
                                last = three(PS[:, 4 + 2 * t + half, :], hid_hi[:, q, f, s], hid_lo[:, q, f, s],
                                             w_hi[:, slot, k], w_lo[:, slot, k], False, False)
                        last.then_inc(w_used, 1)

                norm(name)
                chunk(u0, name, feature_unit, 0)
                for b in range(4):
                    mm(PS[:, 4 + b, :], zeros[:, 0:P], zeros[:, :], start=True, stop=False, skip_group_check=True)
                pairs = (n - 1) // 2
                per = 2 * (4 + wu)
                with pe.Fori(0, pairs) as i:
                    for q in range(2):
                        u = u0 + 4 + q * (4 + wu)
                        chunk(u, None, feature_unit, 2 * ((q + 1) % 2), 0, i, per)
                        second(u + 4, 2 * i + q, q, i, per)
                for c in range(2 * pairs, n):
                    u = u0 + 4 + c * (4 + wu)
                    if c + 1 < n:
                        chunk(u, None, feature_unit, 2 * ((c + 1) % 2))
                        u += 4
                    second(u, c, c % 2, 0, 0)

            def gdn():
                norm("gdn")
                u0, e = UNIT0["gdn_in"], EVAC0["gdn_in"]
                pe.wait_ge(evac_act, e)
                with pe.Fori(0, 3) as i:
                    for q in range(2):
                        pe.wait_ge(gd_free, q + 1 + 2 * i)
                        chunk(u0 + 4 * q, "gdn", feature_unit, 2 * q, 0, i, 8)
                gates(1, 40).then_inc(gd_gates_s, 1)
                pe.wait_ge(evac_act, e + 6)
                for h in range(8):
                    pe.transpose(PS[:, h // 4, (h % 4) * P:(h % 4) * P + P], gd_qkv[:, 8 + h, 0:P], ident)
                for c in range(2):
                    for h in range(8):
                        n = 8 * c + h
                        last = pe.transpose(PS[:, 2 + n // 4, (n % 4) * P:(n % 4) * P + P],
                                            gd_qkv[:, 16 + h, c * P:c * P + P], ident)
                last.then_inc(gd_vt, 1)
                for b in range(2):
                    pe.wait_ge(gd_sqd, b + 1)
                    for h in range(8):
                        o = 39 - (32 * b + h)
                        last = mm(PS[0:40, 6, 0:T], C("unit_col")[:, o:o + 40], gd_sq[b][:, h], start=b == 0 and h == 0,
                                  stop=b == 1 and h == 7)
                last.then_inc(gd_sums, 1)
                pe.wait_ge(gd_tok, 1)
                chunk(u0 + 24, "gdn", token_unit, 0)
                pe.wait_ge(gd_logs, 1)
                for n, (row, c) in enumerate(((5, 0), (5, 1), (0, 0), (0, 1), (3, 1), (4, 1))):
                    pe.transpose(PS[:, 6, 8 * n:8 * n + 8], gd_rows[0:8, row, c * P:c * P + P], ident[0:8, 0:8])
                mm(PS[:, 6, 48:56], ones[0:8, :], gd_last[0:8, :], start=True, stop=True).then_inc(gd_colt, 1)

                def to_all(row):
                    for h in range(8):
                        last = mm(PS[:, 4 + h // 2, (h % 2) * T:(h % 2) * T + T], C(f"select{h}")[0:8, :], gd_rows[0:8, row],
                                  start=True, stop=True)
                    last.then_inc(gd_bcast, 1)
                pe.wait_ge(gd_colk, 1)
                pe.wait_ge(gd_tok, 2)
                to_all(3)

                def gate_unit(j):
                    slot, n, _ = slot_of(u0 + 28 + j, 0, 0)
                    pe.wait_ge(lo_done, n + 1)
                    token_unit(slot, j, 2, 0).then_inc(w_used, 1)
                gate_unit(0)
                gate_unit(1)
                pe.wait_ge(gd_args, 1)
                to_all(4)
                gate_unit(2)
                gate_unit(3)

                def system(c, h, base=0):
                    n = 8 * c + h
                    return PS[:, base + n // 4, (n % 4) * P:(n % 4) * P + P]
                pe.wait_ge(gd_args, 2)
                for c in range(2):
                    for h in range(8):
                        k = gd_qkv[:, 8 + h, c * P:c * P + P]
                        last = mm(system(c, h, 4), k, k, start=True, stop=True)
                last.then_inc(gd_kk, 1)
                pe.wait_ge(evac_act, e + 8)
                for c in range(2):
                    for h in range(8):
                        s = slice(c * P, c * P + P)
                        last = mm(system(c, h), gd_qkv[:, 8 + h, s], gd_qkv[:, h, s], start=True, stop=True)
                last.then_inc(gd_qk, 1)

                def group(g, b, h):
                    return PS[:, 4 * (1 - g) + b + h // 4, (h % 4) * P:(h % 4) * P + P]

                for g in range(2):
                    pe.wait_ge(gd_masked, 2)
                    if g == 1:
                        pe.wait_ge(gd_made, 1)
                    for h in range(8):
                        last = pe.transpose(group(g, 0, h), gd_um[:, g, h], ident)
                    last.then_inc(gd_xps, 1)

                for level in range(1, LEVELS):
                    size = 2 ** level
                    for g in range(2):
                        pe.wait_ge(gd_masked, 2 * level + g + 1)
                        pe.wait_ge(gd_xnew, 2 * level + g - 1)
                        for h in range(8):
                            last = mm(group(g, 0, h), gd_um[:, g, h], gd_X[:, g, h], start=True, stop=True)
                        last.then_inc(gd_yps, 1)
                    for g in range(2):
                        pe.wait_ge(gd_ysb, 2 * level + g - 1)
                        lo = 4 * (1 - g)
                        for h in range(8):
                            if level + 1 < LEVELS:
                                mm(PS[:, lo + 2, 64 * h:64 * h + 64].rearrange("p (a t) -> p a t", t=size), gd_XT[:, g, h], halves(gd_Y[:, g, h:h + 1], size, 0)[:, 0],
                                   start=True, stop=True)
                            last = mm(PS[:, lo, 64 * h:64 * h + 64].rearrange("p (a t) -> p a t", t=size), gd_Y[:, g, h], halves(gd_XT[:, g, h:h + 1], size, 1)[:, 0],
                                      start=True, stop=True)
                        last.then_inc(gd_xps, 1)
                pe.wait_ge(gd_xnew, 14)
                pe.wait_ge(gd_scaled, 3)
                def bank_of(b0, b, h):
                    return PS[:, b0 + b + h // 4, (h % 4) * P:(h % 4) * P + P]
                for h in range(8):
                    last = mm(bank_of(0, 0, h), gd_XT[:, 0, h], gd_bv[:, 0, h], start=True, stop=True)
                last.then_inc(gd_fin_pe, 1)
                pe.wait_ge(gd_fin_act, 1)
                for h in range(8):
                    mm(bank_of(0, 2, h), gd_E[:, 0, h], gd_vn[:, h], start=True, stop=True)
                    last = mm(bank_of(4, 0, h), gd_kd[:, h], gd_vn[:, h], start=True, stop=True)
                last.then_inc(gd_fin_pe, 1)
                pe.wait_ge(gd_fin_act, 2)
                for h in range(8):
                    last = mm(bank_of(4, 2, h), gd_qkv[:, 8 + h, P:T], gd_S[:, h], start=True, stop=True)
                last.then_inc(gd_fin_pe, 1)
                pe.wait_ge(gd_fin_dve, 1)
                for h in range(8):
                    last = mm(bank_of(0, 0, h), gd_XT[:, 1, h], gd_bv[:, 1, h], start=True, stop=True)
                last.then_inc(gd_fin_pe, 1)
                for h in range(8):
                    mm(bank_of(4, 2, h), gd_qkv[:, h, P:T], gd_S[:, h], start=True, stop=True)
                pe.wait_ge(gd_fin_act, 3)
                for h in range(8):
                    last = mm(bank_of(4, 0, h), gd_E[:, 1, h], gd_vn[:, h], start=True, stop=True)
                last.then_inc(gd_fin_pe, 1)
                pe.wait_ge(gd_mixed, 2)
                turn("gdn_o")
                square(UNIT0["gdn_o"], "gdn_o", token_unit)

            def pool():
                pe.wait_ge(xn_ready, 2 * NORMS.index("pool") + 2)
                for b in range(4):
                    band = C(f"pool{WINDOWS[b]}")
                    for k in range(2):
                        s = slice((2 * b + k) * P, (2 * b + k) * P + P)
                        mm(PS[:, 4 + b, k * T:k * T + T], xn[:, 0, s], band[:, 0:T], start=True, stop=False, skip_group_check=True)
                        last = mm(PS[:, 4 + b, k * T + P:k * T + T], xn[:, 1, s], band[:, T:384], start=False, stop=True,
                                  skip_group_check=True)
                    last.then_inc(turned, 1)
                pe.wait_ge(evac_act, EVAC0["xq1"] + 2)
                for c in range(2):
                    u = UNIT0["pool"] + c
                    pe.wait_ge(lo_done, u + 1)
                    for g in range(2):
                        grp = 2 * c + g
                        kt_pair_wait("pool", grp)
                        for t in range(TT):
                            for k in range(2):
                                ts, ws, ks = slice(t * P, t * P + P), slice(g * T, g * T + T), slice(k * T, k * T + T)
                                last = three(PS[:, 2 * c + t, ws], XTh[:, 2 * grp + k, ts], XTl[:, 2 * grp + k, ts],
                                             w_hi[:, u % RING, g, ks], w_lo[:, u % RING, g, ks], k == 0, k == 1)
                    last.then_inc(w_used, 1)

            def swa():
                norm("swa")
                u0, e = UNIT0["qkv"], EVAC0["qkv"]
                for c in range(2):
                    chunk(u0 + 4 * c, "swa", feature_unit, 2 * c)
                pe.wait_ge(evac_act, e + 1)
                for j in range(4):
                    slot, n, _ = slot_of(u0 + 8 + j, 0, 0)
                    pe.wait_ge(lo_done, n + 1)
                    feature_unit(slot, j, 0, 0, tiles=2)
                    for k in range(2):
                        kt = 2 * j + k
                        for t in range(TT):
                            s = slice(t * P, t * P + P)
                            last = three(PS[:, 1, t * T:t * T + T], XTh[:, kt, s], XTl[:, kt, s], w_hi[:, slot, k, T:512],
                                         w_lo[:, slot, k, T:512], kt == 0 and t == 0, kt == KT - 1)
                    last.then_inc(w_used, 1)
                pe.wait_ge(evac_act, e + 3)

                def scores(grp):
                    if grp:
                        pe.wait_ge(sw_max, grp)
                    for j in range(4):
                        h = 4 * grp + j
                        r = slice(64 * (h % 2), 64 * (h % 2) + 64)
                        q, k = sw_q[r, h // 2], sw_k[r, grp]
                        mm(PS[:, 4 + j, 0:P], q[:, 0:P], k[:, 0:P], start=True, stop=True)
                        last = mm(PS[:, 4 + j, P:384], q[:, P:T], k[:, 0:T], start=True, stop=True)
                    last.then_inc(sw_scores, 1)
                scores(0)
                pe.wait_ge(v_kept, 1)
                for grp in range(4):
                    if grp + 1 < 4:
                        scores(grp + 1)
                    pe.wait_ge(sw_probs, grp + 1)
                    if grp:
                        pe.wait_ge(sw_pted, grp)
                    for j in range(4):
                        for b in range(3):
                            last = pe.transpose(PS[:, j, b * P:b * P + P], sw_s[:, j, b * P:b * P + P], ident)
                    last.then_inc(sw_turned, 1)
                pe.wait_ge(sw_pted, 4)
                for b in range(4):
                    for h in range(4 * b, 4 * b + 4):
                        f, r = h // 2, slice(64 * (h % 2), 64 * (h % 2) + 64)
                        o = (f % 2) * T
                        v = [sw_v[:, s, 64 * (h // 4):64 * (h // 4) + 64] for s in range(2)]
                        mm(PS[r, 4 + b, o:o + P], v[0], sw_pt[:, h, 0:P], start=True, stop=True)
                        mm(PS[r, 4 + b, o + P:o + T], v[0], sw_pt[:, h, P:T], start=True, stop=False)
                        last = mm(PS[r, 4 + b, o + P:o + T], v[1], sw_pt[:, h, T:384], start=False, stop=True)
                    last.then_inc(turned, 1)
                square(UNIT0["swa_o"], "swa_o", token_unit)

            ab()
            cross(0)
            wide("mlp0", FF // 512, 4)
            gdn()
            cross(1)
            wide("mlp1", FF // 512, 4)
            pool()
            wide("ffn0", GLU // 256, 2)
            swa()
            wide("ffn1", GLU // 256, 2)


_INS = ['x', 'mem', 'ab_w_in', 'ab_b_i', 'ab_b_f', 'ab_head_gain', 'ab_w_out', 'c_w_in', 'c_conv_w', 'c_a_log',
        'c_dt_bias', 'c_head_gain', 'c_w_out', 'xa_norm', 'mem_norm', 'mix_norm', 'xa_wq', 'xa_wk', 'xa_wv', 'xa_wo',
        'mlp_norm', 'mlp_w1', 'mlp_w2', 'final_norm', 'pool_w_2', 'pool_b_2', 'pool_scale_2', 'attn_w_qkv_2',
        'attn_b_qkv_2', 'attn_sinks_2', 'attn_w_o_2', 'norm_mix_2', 'norm_ffn_2', 'ffn_w_in_2', 'ffn_conv_w_2',
        'ffn_conv_b_2', 'ffn_w_out_2', 'norm_f_2']


def kernel(**inputs):
    import concourse.bacc as _bacc
    from concourse.bass_utils import run_bass_kernel_spmd as _run

    nc = _bacc.Bacc("TRN2", target_bir_lowering=False, num_devices=1)
    arrays, args = {}, {}
    for name in _INS + ["const"]:
        v = CONST if name == "const" else np.ascontiguousarray(inputs[name])
        arrays[f"in_{name}"] = v
        args[name] = nc.dram_tensor(f"in_{name}", v.shape, mybir.dt.from_np(v.dtype), kind="ExternalInput").ap()
    out = nc.dram_tensor("out_0", (1, T, D), F32, kind="ExternalOutput").ap()
    program(nc, args, out)
    r = _run(nc, [arrays], core_ids=[0])
    return r.results[0]["out_0"]
```

```python
import math

import numpy as np

import concourse.bass as bass
from concourse import mybir
from contextlib import ExitStack

F32 = mybir.dt.float32
F32R = mybir.dt.float32r
ACT = mybir.ActivationFunctionType
ALU = mybir.AluOpType
AX = mybir.AxisListType
ds = bass.ds

P = 128
T = 256
TT = T // P
D = 1024
KT = D // P
RING = 4
NEG = -1e30
EPS = 1e-6
LEVELS = 7
WINDOWS = (2, 4, 8, 16)
SWA_HEADS = 16
FF = 4096
GLU = 2816
HID0 = {"mlp0": 0, "mlp1": FF // 512, "ffn0": 2 * (FF // 512), "ffn1": 2 * (FF // 512) + GLU // 256}
NORMS = ["mem", "ab", "gdn", "pool", "ffn0", "swa", "ffn1"]
WIDE = ["mlp0", "mlp1", "ffn0", "ffn1"]
NORMS_ACT = [name for name in NORMS if name != "pool"]
XN_LAST = 2 * len(NORMS) + 2
POOL_SET = {"start": 3, "ab": 4, "gdn": 5, "ffn0": 6, "ffn1": 7}
MISC = 16 * 13


def shape_constants():
    i, j = np.arange(P)[:, None], np.arange(P)[None, :]
    parts = {}
    parts["ident"] = i == j
    parts["ones"] = np.ones((P, P))
    parts["suffix"] = i >= j
    parts["causal_min"] = np.concatenate([np.where(i <= j, 0, NEG), np.zeros((P, P))], 1)
    parts["causal_add"] = np.where(i <= j, 0, NEG)
    parts["strict"] = i < j
    parts["strict_min"] = np.where(i < j, 0, NEG)
    for b in range(LEVELS):
        parts[f"level{b}"] = ((i >> (b + 1)) == (j >> (b + 1))) & (((i >> b) & 1) == 0) & (((j >> b) & 1) == 1)
    for h in range(8):
        parts[f"select{h}"] = np.repeat(i == h, P, 1)
    parts["unit_col"] = np.repeat(np.arange(79)[None, :] == 39, P, 0)
    s, t = np.arange(T)[:, None], np.arange(T)[None, :]
    for w in WINDOWS:
        m = ((s <= t) & (s > t - w)) / np.minimum(t + 1, w) - (s == t)
        parts[f"pool{w}"] = np.concatenate([m[:P], m[P:, P:]], 1)
    dist = np.concatenate([i - j, i + P - j, i - j], 1)
    parts["dist"] = np.where((dist >= 0) & (dist < P), dist, -NEG)
    at, arrays, n = {}, [], 0
    for name, v in parts.items():
        at[name] = (n, v.shape[1])
        arrays.append(v.astype(np.float32))
        n += v.shape[1]
    return np.ascontiguousarray(np.concatenate(arrays, 1)), at


CONST, CONST_AT = shape_constants()
CONST_HALF = CONST.shape[1] // 2

VECTORS = [
    [("mem_norm", 0, 8), ("mix_norm", 0, 16), ("xa_norm", 0, 16), ("mlp_norm", 0, 16), ("norm_mix_2", 0, 16),
     ("ab_head_gain", 0, 4), ("c_head_gain", 0, 1), ("attn_b_qkv_2", 0, 12)],
    [("c_conv_w", 0, 96)],
    [("ffn_conv_w_2", 0, 88)],
    [("ffn_conv_w_2", 88, 44), ("ffn_conv_b_2", 0, 44)],
    [("ffn_conv_w_2", 132, 88)],
    [("ffn_conv_w_2", 220, 44), ("ffn_conv_b_2", 44, 44)],
]

STREAM = [("memkv", 32), ("ab_in", 24), ("ab_o", 8), ("xq0", 8), ("xo0", 8), ("mlp0", 64),
          ("gdn_in", 32), ("gdn_o", 8), ("xq1", 8), ("xo1", 8), ("mlp1", 64),
          ("pool", 2), ("ffn0", 66), ("qkv", 12), ("swa_o", 8), ("ffn1", 66)]
UNIT0, UNITS = {}, 0
for _name, _n in STREAM:
    UNIT0[_name] = UNITS
    UNITS += _n

TURNS = ["mem", "ab", "ab_o", "xq0", "xo0", "mlp0", "gdn", "gdn_o", "xq1", "xo1", "mlp1", "pool", "ffn0", "swa",
         "swa_o", "ffn1"]
ROOTS = [("mem", 2, 2, 1 / D), ("ab", 2, 2, 1 / D), ("ab_heads", 1, 8, 1 / 128), ("xq0", 2, 2, 1 / D),
         ("mlp0", 2, 2, 1 / D), ("gdn", 2, 2, 1 / D), ("gdn_heads0", 1, 8, 1 / 128), ("gdn_heads1", 1, 8, 1 / 128), ("xq1", 2, 2, 1 / D),
         ("mlp1", 2, 2, 1 / D), ("final1", 4, 2, 1 / D), ("ffn0", 2, 2, 1 / D),
         ("swa", 2, 2, 1 / D), ("ffn1", 2, 2, 1 / D), ("final2", 2, 2, 1 / D)]
X_COUNT = {"ab": 0, "xq0": 2, "mlp0": 4, "gdn": 6, "xq1": 8, "mlp1": 10, "final1": 12, "pool": 14, "ffn0": 16,
           "swa": 18, "ffn1": 20, "final2": 22}
EVACS = [("memkv", 8), ("ab_in", 6), ("xq0", 2), ("gdn_in", 8), ("xq1", 2), ("qkv", 3)]
EVAC0, _n = {}, 0
for _name, _k in EVACS:
    EVAC0[_name] = _n
    _n += _k


def root_at(name):
    n = 0
    for k, (who, signals, _, _) in enumerate(ROOTS):
        n += signals
        if who == name:
            return n, k
    raise KeyError(name)


class Order:

    def __init__(self, eng, sem):
        self.eng, self.sem, self.count, self.turn = eng, sem, 0, 0

    def __call__(self, ins):
        ins.then_inc(self.sem, 1)
        self.count += 1
        self.eng.wait_ge(self.sem, self.turn + self.count)

    def loop(self, i, per):
        self.turn, self.start, self.per = i * per, self.count, per

    def end(self, turns):
        assert self.count - self.start == self.per, (self.count - self.start, self.per)
        self.turn, self.count = 0, self.start + turns * self.per


def program(nc, a, out):
    ctx = ExitStack()
    with ctx:
        first = (nc.sbuf_base + 63) // 64 * 64
        SLAB = 53120
        ctx.enter_context(nc.sbuf_tensor("slab", [P, SLAB], F32))
        place = [0]

        def at(name, shape, word, dt=F32):
            n = int(np.prod(shape))
            assert word + n <= SLAB, (name, word + n)
            return nc.alloc_sbuf_tensor_at(name, [P] + list(shape), dt, offset=first + 4 * word)

        def sb(name, shape, dt=F32):
            t = at(name, shape, place[0], dt)
            place[0] += (int(np.prod(shape)) + 7) // 8 * 8
            return t

        PS = ctx.enter_context(nc.psum_tensor("PS", [P, 8, 512], F32))
        x = sb("x", [TT, D])
        xn_at = place[0]
        xn = sb("xn", [TT, D])
        xt_at = place[0]
        XTh = sb("XTh", [KT, T], F32R)
        XTl = sb("XTl", [KT, T], F32R)
        w_raw = sb("w_raw", [RING, 2, 512])
        w_hi = sb("w_hi", [RING, 2, 512], F32R)
        w_lo = sb("w_lo", [RING, 2, 512], F32R)
        const = sb("const", [CONST.shape[1]])
        cols = sb("cols", [len(VECTORS), P])
        zeros = sb("zeros", [512], F32R)
        gate_w = sb("gate_w", [2, KT, 40])
        gate_hi = sb("gate_hi", [2, KT, 40], F32R)
        gate_lo = sb("gate_lo", [2, KT, 40], F32R)
        ss = sb("ss", [16])
        var = sb("var", [16])
        rstd = sb("rstd", [16])
        inv_ms = sb("inv_ms", [2])
        neghalf = sb("neghalf", [16])
        eps_col = sb("eps_col", [1])
        gbias = sb("gbias", [8])
        ffn_gain = sb("ffn_gain", [2, KT])
        sinks = sb("sinks", [SWA_HEADS])
        vbias = sb("vbias", [256])
        K1 = sb("K1", [KT, T])
        V1 = sb("V1", [TT, D])
        arena_at = place[0]
        shared_at = SLAB - 4096
        K0 = at("K0", [KT, T], shared_at)
        V0 = at("V0", [TT, D], shared_at + 2048)
        bc = at("bc", [4, D], shared_at)
        hid_hi = at("hid_hi", [2, 4, T], shared_at - 4096, F32R)
        hid_lo = at("hid_lo", [2, 4, T], shared_at - 2048, F32R)
        sq_junk = at("sq_junk", [2 * KT, T], xt_at)
        K_of, V_of = [K0, K1], [V0, V1]

        class Arena:

            def __init__(self, tag, start=arena_at, end=shared_at):
                self.tag, self.word, self.end = tag, start, end

            def __call__(self, name, *shape):
                t = at(f"{self.tag}_{name}", list(shape), self.word)
                self.word += (int(np.prod(shape)) + 7) // 8 * 8
                assert self.word <= self.end, (name, self.word - self.end)
                return t

        A = Arena("start")
        vec_rows = A("vec_rows", len(VECTORS), P)

        A = Arena("ab")
        ab_qk = A("qk", 4, T)
        ab_v = A("v", TT, 4, 132)
        ab_og = A("og", TT, 512)
        sb_q, sb_k = A("sq", 4, T), A("sk", 4, T)
        sb_v = A("sv", TT, 512)
        ab_rows = A("rows", 13, T)
        acol = A("acol", 2, 4)
        mcol = A("mcol", 2, 4)
        emcol = A("emcol", 2, 4)
        decay_at = A.word
        decay = A("decay", 4, 384)
        prob = A("prob", 4, 384)
        sb_zs, sb_sp = A("zs", 4, 384), A("sp", 4, 384)
        sb_ln = prob
        rden = A("rden", 4, 2)
        hsq = at("ab_hsq", [TT, 512], decay_at)
        hmix = xn
        ab_junk = at("ab_junk", [KT, T], decay_at)

        A = Arena("xa")
        xa_q = A("q", KT, T)
        xa_p = A("p", 4, TT, T)
        xa_pt = A("pt", 4, 2, T)
        xa_m, xa_nm, xa_s, xa_r, xa_rs = A("m", 8), A("nm", 8), A("s", 8), A("r", 8), A("rs", 4)

        A = Arena("mlp", end=shared_at - 4096)
        relu = A("relu", 2, 4, T)
        relu2 = A("relu2", 2, 4, T)

        A = Arena("glu", end=shared_at - 4096)
        glu_pad = A("pad", 2, 4, 264)
        glu_acc = A("acc", 2, 4, T)
        glu_silu = A("silu", 2, 2, T)
        glu_prod = A("prod", 2, 2, T)

        A = Arena("gd", end=SLAB)
        gd_qkv = A("qkv", 24, T)
        gd_gate = A("gate", TT, D)
        gd_E = A("E", 2, 8, P)
        over = A.word
        gd_U = A("U", 2, 8, P)
        gd_X = A("X", 2, 8, P)
        gd_XT = A("XT", 2, 8, P)
        gd_bv = A("bv", 2, 8, P)
        gd_kd = A("kd", 8, P)
        gd_um = at("gd_um", [2, 8, P], arena_at + 16 * T)
        A = Arena("gdc", start=over, end=SLAB)
        gd_pad = A("pad", 2, 4, 264)
        gd_acc = A("acc", 2, 4, T)
        gd_sq = [at("gd_sqq", [8, T], over - 2048), at("gd_sqk", [8, T], over - 4096)]
        gd_rows = at("gd_rows", [8, T], xn_at)
        gd_Y = at("gd_Y", [2, 8, P], xt_at)
        gd_S = at("gd_S", [8, P], xt_at + 2048)
        gd_vn = at("gd_vn", [8, P], xt_at + 3072)
        gd_o = xn
        gd_osqt = at("gd_osqt", [2, D], over + 2048)
        A = Arena("gds", start=arena_at + 19472, end=SLAB)
        gd_cols = A("cols", 7, 8)
        gd_eg, gd_beg, gd_kdc, gd_gl = A("eg", 8), A("beg", 8), A("kdc", 8), A("gl", 8)
        gd_nea, gd_last = A("nea", 8), A("last", 8)

        A = Arena("swa")
        sw_q = A("q", KT, T)
        sw_k = A("k", 4, T)
        sw_v = A("v", TT, T)
        sw_s = A("s", 3, 4, 384)
        sw_pt = A("pt", 16, 384)
        sw_m, sw_nm, sw_sum = A("m", 2, 16), A("nm", 2, 16), A("sum", 2, 16)
        sw_es, sw_r = A("es", 2, 16), A("r", 2, 16)
        sw_qb = A("qb", 8)

        def C(name):
            n, w = CONST_AT[name]
            return const[:, n:n + w]

        def vec_at(name, k):
            for b, rows in enumerate(VECTORS):
                n = 0
                for who, r0, count in rows:
                    if who == name and r0 <= k < r0 + count:
                        return b, n + k - r0
                    n += count
            raise KeyError(name)

        def vec(name, k, i=0):
            b, n = vec_at(name, k)
            return cols[:, b, ds(n + i, 1)] if not isinstance(i, int) else cols[:, b, n + i:n + i + 1]

        ident, ones = C("ident"), C("ones")
        one_col = ones[:, 0:1]

        def f32(t):
            return t.bitcast(F32)

        def sem(name):
            return ctx.enter_context(nc.semaphore(name))

        raw_landed = [sem(f"raw_landed{s}") for s in range(RING)]
        hi_done, lo_done, w_used = sem("hi_done"), sem("lo_done"), sem("w_used")
        const_landed, x_landed = sem("const_landed"), sem("x_landed")
        vec_landed = [sem("vec_landed_first"), sem("vec_landed_rest")]
        mem_landed, misc_landed, bc_landed = sem("mem_landed"), sem("misc_landed"), sem("bc_landed")
        out_landed, gate_zeroed, pool_set = sem("out_landed"), sem("gate_zeroed"), sem("pool_set")
        vec_turned, vec_kept = sem("vec_turned"), sem("vec_kept")
        x_updates, evac_act, v_kept = sem("x_updates"), sem("evac_act"), sem("v_kept")
        sq_done, rstd_done, xn_ready, squared, gained = sem("sq_done"), sem("rstd_done"), sem("xn_ready"), sem("squared"), sem("gained")
        xn_ready_act, gates_hi, gates_lo, tile_done = sem("xn_ready_act"), sem("gates_hi"), sem("gates_lo"), sem("tile_done")
        turned, xt_hi, xt_lo = sem("turned"), sem("xt_hi"), sem("xt_lo")
        act_order, dve_order, pool_order = sem("act_order"), sem("dve_order"), sem("pool_order")
        hid_in, hid_hi_done, hid_lo_done = sem("hid_in"), sem("hid_hi_done"), sem("hid_lo_done")
        glu_in, glu_conv, glu_silued, glu_mult = sem("glu_in"), sem("glu_conv"), sem("glu_silued"), sem("glu_mult")
        (ab_gates, ab_f, ab_lnf, ab_rows_done, ab_turned, ab_args, ab_decayed, ab_scores, ab_probs, ab_outs, ab_norm,
         ab_sq, ab_mixed) = [sem(f"ab_{n}_s") for n in (
             "gates", "f", "lnf", "rows", "turned", "args", "decayed", "scores", "probs", "outs", "norm", "sq", "mixed")]
        sb_z, sb_kept, sb_lned, sb_sped, sb_cum, sb_arg, sb_w, sb_out = [
            sem(f"sb_{n}_s") for n in ("z", "kept", "ln", "sp", "cum", "arg", "w", "out")]
        xa_scores, xa_max, xa_exp, xa_probs, xa_turned, xa_pt_act, xa_pt_dve = [
            sem(f"xa_{n}_s") for n in ("scores", "max", "exp", "probs", "turned", "pt_act", "pt_dve")]
        (gd_conv, gd_free, gd_gates_s, gd_f, gd_lnf, gd_rows_s, gd_sqd, gd_sums, gd_rooted, gd_logs, gd_colt,
         gd_colk, gd_exps, gd_bcast, gd_args, gd_decayed, gd_kk, gd_qk, gd_vt, gd_tok, gd_scaled, gd_made, gd_masked,
         gd_yps, gd_ysb, gd_xps, gd_xnew, gd_fin_pe, gd_fin_act, gd_fin_dve, gd_mixed, gd_osq_s) = [
             sem(f"gd_{n}_s") for n in (
                 "conv", "free", "gates", "f", "lnf", "rows", "sqd", "sums", "rooted", "logs", "colt", "colk",
                 "exps", "bcast", "args", "decayed", "kk", "qk", "vt", "tok", "scaled", "made", "masked", "yps", "ysb",
                 "xps", "xnew", "fin_pe", "fin_act", "fin_dve", "mixed", "osq")]
        sw_scores, sw_max, sw_exp, sw_probs, sw_turned, sw_pted, sw_den, sw_kept = [
            sem(f"sw_{n}_s") for n in ("scores", "max", "exp", "probs", "turned", "pted", "den", "kept")]

        def group_banks(g, b):
            lo = 4 * (1 - g) + b
            return PS[:, lo:lo + 2, :].rearrange("p b (k t) -> p b k t", k=4)

        def halves(v, size, which):
            return v.rearrange("p h (a w t) -> p h a w t", w=2, t=size)[:, :, :, which, :]

        block = ctx.enter_context(nc.Block())

        def slot_of(u, i, per):
            assert per % RING == 0
            return u % RING, u + per * i, u // RING + (per // RING) * i


        @block.sync
        def _(sp):
            def load(u, src, i=0, per=0, halves=False):
                slot, n, _ = slot_of(u, i, per)
                if u >= RING:
                    sp.wait_ge(lo_done, n - RING + 1)
                dst = w_raw[:, slot].rearrange("p k (h n) -> p (k h) n", h=2) if halves else w_raw[:, slot]
                sp.dma_start(dst, src).then_inc(raw_landed[slot], 16)

            def rows_of(W, k, c):
                return W.rearrange("(k p) n -> p k n", p=P)[:, ds(k, 2), ds(c, 512)]

            def load_chunk(u, W, c, i=0, per=0):
                for j in range(4):
                    load(u + j, rows_of(W, 2 * j, c), i, per)

            def load_square(u, W):
                with sp.Fori(0, 2) as i:
                    load_chunk(u, W, i * 512, i, 4)

            def load_wide(u0, n, wu, load_first, load_second):
                per = 2 * (4 + wu)
                load_first(u0, 0, 0, 0)
                pairs = (n - 1) // 2
                with sp.Fori(0, pairs) as i:
                    for q in range(2):
                        u = u0 + 4 + q * (4 + wu)
                        load_first(u, q + 1 + 2 * i, i, per)
                        load_second(u + 4, q + 2 * i, i, per)
                for c in range(2 * pairs, n):
                    u = u0 + 4 + c * (4 + wu)
                    if c + 1 < n:
                        load_first(u, c + 1, 0, 0)
                        u += 4
                    load_second(u, c, 0, 0)

            def load_mlp(u0, W1, W2):
                load_wide(u0, FF // 512, 4,
                          lambda u, c, i, per: load_chunk(u, W1, c * 512, i, per),
                          lambda u, c, i, per: [load(u + 2 * k + h, rows_of(W2, c * 4 + 2 * k, h * 512), i, per)
                                                for k in range(2) for h in range(2)])

            def load_glu(u0, W1, W2):
                W = W1.rearrange("(p k) (h n) -> p (k h) n", p=P, h=2)

                def first_layer(u, c, i, per):
                    for j in range(4):
                        load(u + j, W[:, 4 * j:4 * j + 4, ds(c * 256, 256)], i, per, halves=True)
                load_wide(u0, GLU // 256, 2, first_layer,
                          lambda u, c, i, per: [load(u + h, rows_of(W2, c * 2, h * 512), i, per) for h in range(2)])

            sp.dma_start(const[:, 0:2 * P], a["const"][:, 0:2 * P]).then_inc(const_landed, 16)
            sp.dma_start(xn[:, :, :], a["mem"][0].rearrange("(t p) n -> p t n", p=P)).then_inc(mem_landed, 16)
            for b, rows in enumerate(VECTORS):
                if b == 1:
                    load(0, rows_of(a["xa_wk"][0], 0, 0))
                n = 0
                for who, r0, count in rows:
                    src = a[who]
                    if len(src.shape) == 3:
                        src = src.rearrange("a b c -> (a b c)")
                    elif len(src.shape) == 2:
                        src = src.rearrange("a b -> (a b)")
                    src = src.rearrange("(r c) -> r c", c=P)[r0:r0 + count, :]
                    sp.dma_start(vec_rows[n:n + count, b, :], src).then_inc(vec_landed[min(b, 1)], 16)
                    n += count
            for j in range(1, 4):
                load(j, rows_of(a["xa_wk"][0], 2 * j, 0))
            load_chunk(4, a["xa_wk"][0], 512)
            sp.dma_start(x[:, :, :], a["x"][0].rearrange("(t p) n -> p t n", p=P)).then_inc(x_landed, 16)
            load_square(8, a["xa_wv"][0])
            sp.wait_ge(gate_zeroed, 1)
            abg = a["ab_w_in"][0].rearrange("(k p) n -> p k n", p=P)
            cg = a["c_w_in"][0].rearrange("(k p) n -> p k n", p=P)
            with nc.allow_non_contiguous_dma("gate columns and per-partition values"):
                for dst, src in (
                        (gate_w[:, 0, :, 0:4], abg[:, :, 1536:1540]), (gate_w[:, 0, :, 32:36], abg[:, :, 1540:1544]),
                        (gate_w[:, 1, :, 0:8], cg[:, :, 4096:4104]), (gate_w[:, 1, :, 32:40], cg[:, :, 4104:4112]),
                        (gbias[0:4, 0:1], a["ab_b_i"].rearrange("a n -> n a")),
                        (gbias[32:36, 0:1], a["ab_b_f"].rearrange("a n -> n a")),
                        (gbias[0:8, 1:2], a["c_a_log"].rearrange("a n -> n a")),
                        (gbias[32:40, 1:2], a["c_dt_bias"].rearrange("a n -> n a")),
                        (ffn_gain[:, :, :], a["norm_ffn_2"].rearrange("l (p k) -> p l k", p=P)),
                        (sinks[:, :], a["attn_sinks_2"].broadcast_to([P, SWA_HEADS])),
                        (vbias[:, :], a["attn_b_qkv_2"][:, 1280:1536].broadcast_to([P, 256]))):
                    sp.dma_start(dst, src).then_inc(misc_landed, 16)
            sp.dma_start(const[:, 2 * P:CONST_HALF], a["const"][:, 2 * P:CONST_HALF]).then_inc(misc_landed, 16)
            load_square(16, a["xa_wk"][1])
            sp.dma_start(const[:, CONST_HALF:], a["const"][:, CONST_HALF:]).then_inc(misc_landed, 16)
            load_square(24, a["xa_wv"][1])


            def ab():
                for k, c in enumerate((0, 512, 1024, 1544, 2056, 2568)):
                    load_chunk(UNIT0["ab_in"] + 4 * k, a["ab_w_in"][0], c)
                load_square(UNIT0["ab_o"], a["ab_w_out"][0])

            def cross(l):
                load_square(UNIT0[f"xq{l}"], a["xa_wq"][l])
                load_square(UNIT0[f"xo{l}"], a["xa_wo"][l])
                if l == 1:
                    sp.wait_ge(x_updates, X_COUNT["xq1"])
                    for k, who in enumerate(("final_norm", "norm_f_2", "pool_b_2", "pool_scale_2")):
                        src = a[who]
                        if len(src.shape) == 3:
                            src = src.rearrange("a b c -> a (b c)")
                        elif len(src.shape) == 1:
                            src = src.rearrange("(a n) -> a n", a=1)
                        sp.dma_start(bc[:, k, :], src.broadcast_to([P, D])).then_inc(bc_landed, 16)

            def gdn():
                with sp.Fori(0, 8) as i:
                    load_chunk(UNIT0["gdn_in"], a["c_w_in"][0], i * 512, i, 4)
                load_square(UNIT0["gdn_o"], a["c_w_out"][0])

            def pool():
                for k in range(2):
                    u = UNIT0["pool"] + k
                    sp.wait_ge(lo_done, u - RING + 1)
                    sp.dma_start(w_raw[:, u % RING].rearrange("p g (k n) -> p (g k) n", k=2),
                                 a["pool_w_2"][0, 2 * k:2 * k + 2].rearrange("g (k p) n -> p (g k) n", p=P))\
                        .then_inc(raw_landed[u % RING], 16)

            def swa():
                for k, c in enumerate((1024, 0, 512)):
                    load_chunk(UNIT0["qkv"] + 4 * k, a["attn_w_qkv_2"][0], c)
                load_square(UNIT0["swa_o"], a["attn_w_o_2"][0])

            ab()
            cross(0)
            load_mlp(UNIT0["mlp0"], a["mlp_w1"][0], a["mlp_w2"][0])
            gdn()
            cross(1)
            load_mlp(UNIT0["mlp1"], a["mlp_w1"][1], a["mlp_w2"][1])
            pool()
            load_glu(UNIT0["ffn0"], a["ffn_w_in_2"][0], a["ffn_w_out_2"][0])
            swa()
            load_glu(UNIT0["ffn1"], a["ffn_w_in_2"][1], a["ffn_w_out_2"][1])
            for t in range(TT):
                sp.wait_ge(xn_ready, XN_LAST - 1 + t)
                sp.dma_start(out[0, t * P:t * P + P, :], xn[:, t, :]).then_inc(out_landed, 16)
            sp.wait_ge(out_landed, 16 * TT)

        @block.gpsimd
        def _(pool):
            order = Order(pool, pool_order)
            pool.memset(gate_w[:, :, :, :], 0.0).then_inc(gate_zeroed, 1)
            pool.memset(f32(zeros[:, :]), 0.0).then_inc(pool_set, 1)
            pool.memset(neghalf[:, :], -0.5).then_inc(pool_set, 1)
            pool.memset(eps_col[:, :], EPS).then_inc(pool_set, 1)
            pool.wait_ge(pool_set, POOL_SET["start"])

            def root(name, last=True):
                signals, k = root_at(name)
                _, _, n, scale = ROOTS[k]
                pool.wait_ge(sq_done, signals)
                order(pool.tensor_scalar(var[:, :n], ss[:, :n], scale, EPS, ALU.mult, ALU.add))
                power = pool.tensor_tensor(rstd[:, :n], var[:, :n], neghalf[:, :n], ALU.pow)
                if last:
                    power.then_inc(rstd_done, 1)
                else:
                    order(power)

            root("mem")
            pool.wait_ge(vec_kept, 2)
            pool.memset(ab_v[:, :, :, 128:129], 1.0).then_inc(pool_set, 1)
            root("ab")
            root("ab_heads")
            root("xq0")
            root("mlp0")
            pool.wait_ge(x_updates, X_COUNT["gdn"])
            pool.memset(gd_pad[:, 0, :, 0:3], 0.0).then_inc(pool_set, 1)
            pool.memset(gd_pad[:, 1, :, 0:3], 0.0).then_inc(gd_free, 2)
            root("gdn")
            pool.wait_ge(gd_exps, 1)
            pool.wait_ge(gd_tok, 1)

            def by_column(v, column):
                return pool.tensor_tensor(v, v, column.unsqueeze(2).broadcast_to([P, 8, P]), ALU.mult)
            for c in range(2):
                by_column(gd_bv[:, c], gd_cols[:, 2 + c]).then_inc(gd_scaled, 1)
            pool.wait_ge(gd_tok, 2)
            by_column(gd_kd[:, :, :], gd_kdc[:, :]).then_inc(gd_scaled, 1)
            root("gdn_heads0")
            root("gdn_heads1")
            root("xq1")
            root("mlp1")
            root("final1", last=False)
            order(pool.tensor_tensor(var[:, 2:4], rstd[:, 0:2], rstd[:, 0:2], ALU.mult))
            order(pool.tensor_tensor(var[:, 2:4], var[:, 2:4], ss[:, 2:4], ALU.mult))
            order(pool.tensor_scalar(var[:, 2:4], var[:, 2:4], 1 / D, EPS, ALU.mult, ALU.add))
            order(pool.tensor_tensor(rstd[:, 2:4], var[:, 2:4], neghalf[:, 2:4], ALU.pow))
            pool.tensor_tensor(rstd[:, 4:6], rstd[:, 2:4], rstd[:, 0:2], ALU.mult).then_inc(rstd_done, 1)
            pool.wait_ge(x_updates, X_COUNT["ffn0"])
            pool.memset(glu_pad[:, :, :, 0:2], 0.0).then_inc(pool_set, 1)
            root("ffn0")
            root("swa")
            pool.wait_ge(x_updates, X_COUNT["ffn1"])
            pool.memset(glu_pad[:, :, :, 0:2], 0.0).then_inc(pool_set, 1)
            root("ffn1")
            root("final2")

        @block.scalar
        def _(act):
            order = Order(act, act_order)
            nxt = [0]

            def split(u, i=0, per=0):
                slot, n, uses = slot_of(u, i, per)
                if u >= RING:
                    act.wait_ge(w_used, n - RING + 1)
                act.wait_ge(raw_landed[slot], 16 * uses + 16)
                act.activation(w_hi[:, slot], w_raw[:, slot], ACT.Copy).then_inc(hi_done, 1)

            def splits(n):
                for _ in range(n):
                    if nxt[0] < UNITS:
                        split(nxt[0])
                    nxt[0] += 1

            def chunk_done(u, i=0, per=0):
                act.wait_ge(w_used, u + per * i + 1)

            def squares(src, dst=None, after_wide=None):
                for t in range(TT):
                    if after_wide:
                        act.wait_ge(x_updates, X_COUNT[after_wide] - 1 + t)
                    unused = xn[:, t] if dst is None else dst[:, 4 * t:4 * t + 4].rearrange("p k t -> p (k t)")
                    act.activation(unused, src[:, t], ACT.Square,
                                   accum_out=ss[:, t:t + 1]).then_inc(sq_done, 1)
                    if after_wide in ("gdn", "final1") and t == 0:
                        splits(2)

            def activations(turn, gain):
                n = TURNS.index(turn)
                for b in range(4):
                    act.wait_ge(turned, 4 * n + b + 1)
                    for k in (2 * b, 2 * b + 1):
                        act.activation(XTh[:, k], PS[:, 4 + b, (k % 2) * T:(k % 2) * T + T], ACT.Copy,
                                       scale=gain(k)).then_inc(xt_hi, 1)

            def scale_rows(name, src):
                act.wait_ge(rstd_done, root_at(name)[1] + 1)
                for half in range(2):
                    s = slice(512 * half, 512 * half + 512)
                    act.activation(xn[:, 1, s], src[:, 1, s], ACT.Copy, scale=rstd[:, 1:2]).then_inc(xn_ready_act, 1)

            def norm(name, gain):
                if name in ("gdn", "swa"):
                    squares(x, after_wide=name)
                else:
                    act.wait_ge(x_updates, X_COUNT[name])
                    squares(x)
                splits(1)
                scale_rows(name, x)
                activations(name, gain)
                if name in ("gdn", "swa"):
                    splits(1)

            def late_norm(name, gain):
                activations(name, gain)
                splits(1)
                act.wait_ge(x_updates, X_COUNT[name])
                squares(x)

            def square_evac(u0, evac, n=2):
                assert nxt[0] == u0 + RING, (nxt[0], u0)
                with act.Fori(0, n) as i:
                    for j in range(3):
                        split(u0 + RING + j, i, 4)
                    chunk_done(u0 + 3, i, 4)
                    evac(i).then_inc(evac_act, 1)
                    split(u0 + RING + 3, i, 4)
                nxt[0] += 4 * n

            def to_features(dst):
                return lambda i: act.activation(dst[:, ds(4 * i, 4), :].rearrange("p (b k) t -> p b k t", b=2),
                                                PS[:, ds(2 * i, 2), :].rearrange("p b (k t) -> p b k t", k=2), ACT.Copy)

            def to_tokens(dst, func=ACT.Copy):
                return lambda i: act.activation(dst[:, :, ds(512 * i, 512)], PS[:, ds(2 * i, 2), :], func)

            act.wait_ge(mem_landed, 16)
            squares(xn, dst=K0)
            splits(1)
            scale_rows("mem", xn)
            act.wait_ge(vec_kept, 1)
            activations("mem", lambda k: vec("mem_norm", k))
            splits(3)
            for k, (dst, kind) in enumerate(((K0, to_features), (V0, to_tokens), (K1, to_features), (V1, to_tokens))):
                square_evac(8 * k, kind(dst))
                if k == 0:
                    act.wait_ge(x_landed, 16)
                    squares(x, dst=ab_junk)
                    scale_rows("ab", x)
                if k == 2:
                    act.wait_ge(misc_landed, MISC)
                    act.activation(gate_hi[:, :, :, :], gate_w[:, :, :, :], ACT.Copy).then_inc(gates_hi, 1)

            def ab():
                activations("ab", lambda k: vec("mix_norm", k))
                u = UNIT0["ab_in"]
                splits(3)
                chunk_done(u + 3)
                act.activation(ab_qk[:, 0:2], PS[:, 0, :].rearrange("p (k t) -> p k t", k=2), ACT.Copy)
                act.activation(ab_qk[:, 2:4], PS[:, 1, :].rearrange("p (k t) -> p k t", k=2), ACT.Copy,
                               scale=64 ** -0.5).then_inc(evac_act, 1)
                splits(1)
                act.wait_ge(ab_f, 1)
                act.activation(ab_rows[0:4, 2], ab_rows[0:4, 0], ACT.Tanh)
                order(act.activation(ab_rows[0:4, 3], ab_rows[0:4, 1], ACT.Abs))
                order(act.activation(ab_rows[0:4, 4], ab_rows[0:4, 3], ACT.Exp, scale=-1.0))
                act.activation(ab_rows[0:4, 5], ab_rows[0:4, 4], ACT.Ln, bias=1.0).then_inc(ab_lnf, 1)
                splits(3)
                chunk_done(u + 7)
                act.activation(ab_v[:, :, :, 0:128], PS[:, 2:4, :].rearrange("p t (h d) -> p t h d", h=4),
                               ACT.Copy).then_inc(evac_act, 1)
                splits(1)
                splits(3)
                chunk_done(u + 11)
                act.activation(ab_og[:, :, :], PS[:, 0:2, :], ACT.Sigmoid).then_inc(evac_act, 1)
                splits(1)
                act.wait_ge(ab_args, 1)
                act.activation(emcol[:, :, :], mcol[:, :, :], ACT.Exp)
                act.activation(decay[:, :, :], decay[:, :, :], ACT.Exp).then_inc(ab_decayed, 1)
                splits(3)
                chunk_done(u + 15)
                act.activation(sb_q[:, :, :].rearrange("p (b k) t -> p b k t", b=2),
                               PS[:, 2:4, :].rearrange("p b (k t) -> p b k t", k=2), ACT.Copy,
                               scale=128 ** -0.5).then_inc(evac_act, 1)
                splits(1)
                act.wait_ge(ab_norm, 1)
                act.activation(hsq[:, :, :], hmix[:, :, 0:512], ACT.Square).then_inc(ab_sq, 1)
                splits(3)
                chunk_done(u + 19)
                act.activation(sb_k[:, :, :].rearrange("p (b k) t -> p b k t", b=2),
                               PS[:, 0:2, :].rearrange("p b (k t) -> p b k t", k=2), ACT.Copy).then_inc(evac_act, 1)
                splits(1)
                act.wait_ge(sb_kept, 1)
                order(act.activation(sb_ln[:, :, :], sb_zs[:, :, :], ACT.Abs))
                order(act.activation(sb_ln[:, :, :], sb_ln[:, :, :], ACT.Exp, scale=-1.0))
                act.activation(sb_ln[:, :, :], sb_ln[:, :, :], ACT.Ln, bias=1.0).then_inc(sb_lned, 1)
                splits(3)
                chunk_done(u + 23)
                act.activation(sb_v[:, :, :], PS[:, 2:4, :], ACT.Copy).then_inc(evac_act, 1)
                for h in (0, 2):
                    act.wait_ge(sb_arg, h // 2 + 1)
                    act.activation(sb_ln[:, h:h + 2], sb_zs[:, h:h + 2], ACT.Exp).then_inc(sb_w, 1)
                splits(1)
                act.wait_ge(sb_out, 1)
                act.activation(hmix[:, :, 512:].rearrange("p t (h d) -> p h t d", h=4),
                               PS[:, 0:4, :].rearrange("p h (t d) -> p h t d", t=2)[:, :, :, 0:128],
                               ACT.Copy).then_inc(ab_mixed, 1)
                activations("ab_o", lambda k: vec("ab_head_gain", k) if k < 4 else one_col)
                splits(7)

            def cross(l):
                late_norm(f"xq{l}", lambda k: vec("xa_norm", 8 * l + k))
                square_evac(UNIT0[f"xq{l}"], to_features(xa_q))

                def copy_pt(h):
                    act.wait_ge(xa_turned, 4 * l + h + 1)
                    act.activation(xa_pt[:, h], PS[:, h, :].rearrange("p (m t) -> p m t", m=2),
                                   ACT.Copy).then_inc(xa_pt_act, 1)
                for h in range(4):
                    act.wait_ge(xa_max, 4 * l + h + 1)
                    for t in range(TT):
                        act.activation(xa_p[:, h, t], PS[:, 4 + h, t * T:t * T + T], ACT.Exp, scale=xa_rs[:, t:t + 1],
                                       bias=xa_nm[:, 2 * h + t:2 * h + t + 1],
                                       accum_out=xa_s[:, 2 * h + t:2 * h + t + 1]).then_inc(xa_exp, 1)
                for h in (0, 2):
                    copy_pt(h)
                activations(f"xo{l}", lambda k: one_col)
                splits(7)

            def mlp(l):
                late_norm(f"mlp{l}", lambda k: vec("mlp_norm", 8 * l + k))
                u0, n, wu = UNIT0[f"mlp{l}"], FF // 512, 4
                h0 = HID0[f"mlp{l}"]

                def hidden(c, q, u_last, i, per):
                    chunk_done(u_last, i, per)
                    act.activation(relu[:, q].rearrange("p (b k) t -> p b k t", b=2),
                                   PS[:, 2 * q:2 * q + 2, :].rearrange("p b (k t) -> p b k t", k=2),
                                   ACT.Relu).then_inc(hid_in, 1)
                    act.wait_ge(hid_in, c + (h0 + 1))
                    act.activation(hid_hi[:, q], relu[:, q], ACT.Square).then_inc(hid_hi_done, 1)

                splits(4)
                hidden(0, 0, u0 + 3, 0, 0)
                u1 = nxt[0]
                pairs = (n - 1) // 2
                per = 2 * (4 + wu)
                with act.Fori(0, pairs) as i:
                    for q in range(2):
                        for j in range(4 + wu):
                            split(u1 + q * (4 + wu) + j, i, per)
                            if j == wu - 1:
                                hidden(q + 1 + 2 * i, (q + 1) % 2, u0 + 7 + q * (4 + wu), i, per)
                nxt[0] = u1 + pairs * per
                splits(4)
                hidden(n - 1, (n - 1) % 2, u0 + 3 + 4 + (n - 2) * (4 + wu), 0, 0)
                splits(4)

            def glu(l):
                norm(f"ffn{l}", lambda k: ffn_gain[:, l, k:k + 1])
                u0, n, wu = UNIT0[f"ffn{l}"], GLU // 256, 2
                h0, g0 = HID0[f"ffn{l}"], (GLU // 256) * l

                def tap(part, c, k):
                    return vec("ffn_conv_w_2", 132 * l + 88 + 22 * part + k, 2 * c)

                def hidden(c, q, u_last, i, per, fill):
                    chunk_done(u_last, i, per)
                    src = PS[:, 2 * q:2 * q + 2, :].rearrange("p b (k t) -> p b k t", k=2)
                    act.activation(glu_pad[:, q, :, 2:2 + T].rearrange("p (b k) t -> p b k t", b=2), src, ACT.Copy)
                    for f in range(4):
                        part, k = f // 2, f % 2
                        last = act.activation(glu_acc[:, q, f], PS[:, 2 * q + f // 2, (f % 2) * T:(f % 2) * T + T],
                                              ACT.Identity, scale=tap(part, c, k),
                                              bias=vec("ffn_conv_b_2", 44 * l + 22 * part + k, 2 * c))
                    last.then_inc(glu_in, 1)
                    fill[0]()
                    act.wait_ge(glu_conv, c + (g0 + 1))
                    act.activation(glu_silu[:, q], glu_acc[:, q, 2:4], ACT.Silu).then_inc(glu_silued, 1)
                    fill[1]()
                    act.wait_ge(glu_mult, c + (g0 + 1))
                    act.activation(hid_hi[:, q, 0:2], glu_prod[:, q], ACT.Copy).then_inc(hid_hi_done, 1)

                splits(4)
                u1 = nxt[0]
                hidden(0, 0, u0 + 3, 0, 0, (lambda: splits(1), lambda: splits(1)))
                assert nxt[0] == u1 + 2
                pairs = (n - 3) // 2
                per = 2 * (4 + wu)
                one = lambda: splits(1)
                with act.Fori(0, pairs) as i:
                    for q in range(2):
                        v = u1 + 2 + q * (4 + wu)
                        for j in range(4):
                            split(v + j, i, per)
                        hidden(q + 1 + 2 * i, (q + 1) % 2, u0 + 7 + q * (4 + wu), i, per,
                               (lambda v=v: split(v + 4, i, per), lambda v=v: split(v + 5, i, per)))
                nxt[0] = u1 + 2 + pairs * per
                splits(4)
                hidden(n - 2, (n - 2) % 2, u0 + 7 + (n - 3) * (4 + wu), 0, 0, (one, one))
                splits(2)
                hidden(n - 1, (n - 1) % 2, u0 + 7 + (n - 2) * (4 + wu), 0, 0, (lambda: None, lambda: None))
                splits(2)

            def gdn():
                norm("gdn", lambda k: vec("mix_norm", 8 + k))
                u0 = UNIT0["gdn_in"]
                act.wait_ge(pool_set, POOL_SET["gdn"])

                def chunk_in(c, i=0, per=0):
                    for j in range(3):
                        split(u0 + 4 + 4 * c + j, i, per)
                    chunk_done(u0 + 4 * c + 3, i, per)
                    q = c % 2
                    act.wait_ge(evac_act, 2 * i + (EVAC0["gdn_in"] + c - 1))
                    act.activation(gd_pad[:, q, :, 3:3 + T].rearrange("p (b k) t -> p b k t", b=2),
                                   PS[:, 2 * q:2 * q + 2, :].rearrange("p b (k t) -> p b k t", k=2), ACT.Copy)
                    for f in range(4):
                        last = act.activation(gd_acc[:, q, f], PS[:, 2 * q + f // 2, (f % 2) * T:(f % 2) * T + T],
                                              ACT.Copy, scale=vec("c_conv_w", 72 + 4 * c + f, per * i))
                    last.then_inc(gd_free, 1)
                    split(u0 + 4 + 4 * c + 3, i, per)

                def silu(c, i=0, per=0):
                    act.wait_ge(gd_conv, 2 * i + (c + 1))
                    act.activation(gd_qkv[:, ds(per * i + 4 * c, 4), :], gd_acc[:, c % 2], ACT.Silu).then_inc(evac_act, 1)
                chunk_in(0)
                with act.Fori(0, 2) as i:
                    for c in range(2):
                        chunk_in(c + 1, i, 8)
                        silu(c, i, 8)
                chunk_in(5)
                silu(4)
                silu(5)
                nxt[0] += 24
                splits(1)
                for b in range(2):
                    act.activation(gd_sq[b][:, :, :], gd_qkv[:, 8 * b:8 * b + 8], ACT.Square).then_inc(gd_sqd, 1)
                act.wait_ge(gd_f, 1)
                order(act.activation(gd_rows[0:8, 3:5], gd_rows[0:8, 1:3], ACT.Abs))
                order(act.activation(gd_rows[0:8, 3:5], gd_rows[0:8, 3:5], ACT.Exp, scale=-1.0))
                act.activation(gd_nea[0:8, 1:2], gbias[0:8, 1:2], ACT.Exp)
                act.activation(gd_rows[0:8, 3:5], gd_rows[0:8, 3:5], ACT.Ln, bias=1.0).then_inc(gd_lnf, 1)
                act.wait_ge(gd_vt, 1)
                act.activation(gd_bv[:, :, :, :].rearrange("p c (b k) t -> p (c b) k t", k=4),
                               PS[:, 2:6, :].rearrange("p b (k t) -> p b k t", k=4), ACT.Copy).then_inc(gd_tok, 1)
                act.wait_ge(gd_rows_s, 1)
                act.activation(gd_rows[0:8, 0], gd_rows[0:8, 7], ACT.Exp)
                act.wait_ge(gd_sums, 1)
                act.activation(gd_rows[0:8, 1], PS[0:8, 6, 0:T], ACT.Ln, bias=eps_col[0:8, :])
                act.activation(gd_rows[0:8, 2], PS[32:40, 6, 0:T], ACT.Ln, bias=eps_col[32:40, :]).then_inc(gd_rooted, 1)
                splits(2)
                chunk_done(u0 + 27)
                act.activation(gd_gate[:, :, 0:512], PS[:, 0:2, :], ACT.Silu).then_inc(evac_act, 1)
                splits(1)
                act.wait_ge(gd_colk, 2)
                act.activation(gd_beg[:, :], gd_cols[:, 4], ACT.Exp)
                act.activation(gd_eg[:, :], gd_cols[:, 5], ACT.Exp)
                act.activation(gd_kdc[:, :], gd_gl[:, :], ACT.Exp).then_inc(gd_exps, 1)
                act.wait_ge(gd_args, 1)
                act.activation(gd_U[:, :, :, :], gd_U[:, :, :, :], ACT.Exp).then_inc(gd_decayed, 1)
                splits(2)
                act.wait_ge(gd_vt, 2)
                act.activation(gd_kd[:, :, :].rearrange("p (b k) t -> p b k t", b=2),
                               PS[:, 0:2, :].rearrange("p b (k t) -> p b k t", k=4), ACT.Copy).then_inc(gd_tok, 1)
                act.wait_ge(gd_args, 2)
                act.activation(gd_E[:, :, :, :], gd_E[:, :, :, :], ACT.Exp).then_inc(gd_decayed, 1)
                splits(1)
                chunk_done(u0 + 31)
                act.activation(gd_gate[:, :, 512:D], PS[:, 2:4, :], ACT.Silu).then_inc(evac_act, 1)
                splits(1)
                with act.Fori(0, LEVELS - 1) as i:
                    for g in range(2):
                        act.wait_ge(gd_yps, 2 * i + (g + 1))
                        act.activation(gd_Y[:, g].rearrange("p (b k) t -> p b k t", b=2), group_banks(g, 0),
                                       ACT.Copy).then_inc(gd_ysb, 1)
                for n, (dst, bank) in enumerate(((gd_vn, 0), (gd_S, 4), (gd_vn, 0))):
                    act.wait_ge(gd_fin_pe, n + 1 if n < 2 else 4)
                    act.activation(dst[:, :, :].rearrange("p (b k) t -> p b k t", b=2),
                                   PS[:, bank:bank + 2, :].rearrange("p b (k t) -> p b k t", k=4),
                                   ACT.Copy).then_inc(gd_fin_act, 1)
                    if n == 1:
                        order(act.activation(gd_o[:, 0].rearrange("p (b n) -> p b n", b=2), PS[:, 2:4, :], ACT.Copy))
                        act.activation(gd_osqt[:, 0], gd_o[:, 0], ACT.Square).then_inc(gd_osq_s, 1)
                act.wait_ge(gd_fin_pe, 5)
                act.activation(gd_o[:, 1].rearrange("p (b n) -> p b n", b=2), PS[:, 4:6, :], ACT.Copy).then_inc(gd_fin_act, 1)
                act.wait_ge(gd_fin_dve, 2)
                act.activation(gd_osqt[:, 1], gd_o[:, 1], ACT.Square).then_inc(gd_osq_s, 1)
                activations("gdn_o", lambda k: vec("c_head_gain", 0))
                splits(7)

            def pool():
                squares(x, dst=sq_junk, after_wide="final1")
                splits(1)
                for t in range(TT):
                    act.wait_ge(gained, t + 1)
                    act.activation(sq_junk[:, 8 + 4 * t:12 + 4 * t].rearrange("p k t -> p (k t)"), xn[:, t], ACT.Square,
                                   accum_out=ss[:, 2 + t:3 + t]).then_inc(sq_done, 1)
                activations("pool", lambda k: vec("norm_mix_2", k))
                splits(2)

            def swa():
                norm("swa", lambda k: vec("norm_mix_2", 8 + k))
                u0 = UNIT0["qkv"]
                splits(3)
                chunk_done(u0 + 3)
                for g in range(4):
                    r = slice(64 * (g % 2), 64 * (g % 2) + 64)
                    b, n = vec_at("attn_b_qkv_2", 8 + g // 2)
                    for half in range(2):
                        last = act.activation(sw_k[64 * half:64 * half + 64, g], PS[r, 0, (g // 2) * T:(g // 2) * T + T],
                                              ACT.Identity, bias=cols[r, b, n:n + 1])
                last.then_inc(evac_act, 1)
                splits(1)
                act.wait_ge(sw_den, 1)

                def queries(c):
                    chunk_done(u0 + 4 * c + 7)
                    for f in range(4):
                        last = act.activation(sw_q[:, 4 * c + f],
                                              PS[:, 2 * (1 - c) + f // 2, (f % 2) * T:(f % 2) * T + T],
                                              ACT.Identity, scale=0.125, bias=sw_qb[:, 4 * c + f:4 * c + f + 1])
                    last.then_inc(evac_act, 1)

                def exps(grp):
                    act.wait_ge(sw_max, grp + 1)
                    es = sw_es[:, :, 4 * grp:4 * grp + 4]
                    act.activation(es, es, ACT.Exp)
                    for t, s in ((0, slice(0, P)), (1, slice(P, 384))):
                        for j in range(4):
                            h = 4 * grp + j
                            v = sw_s[:, grp % 3, j, s]
                            act.activation(v, v, ACT.Exp, bias=sw_nm[:, t, h:h + 1],
                                           accum_out=sw_sum[:, t, h:h + 1]).then_inc(sw_exp, 1)

                def copy_out(grp):
                    act.wait_ge(sw_turned, grp + 1)
                    act.activation(sw_pt[:, 4 * grp:4 * grp + 4], PS[:, 0:4, 0:384], ACT.Copy).then_inc(sw_pted, 1)
                splits(3)
                queries(0)
                splits(2)
                exps(0)
                splits(2)
                queries(1)
                splits(1)
                for grp in range(1, 4):
                    exps(grp)
                    copy_out(grp - 1)
                copy_out(3)
                activations("swa_o", lambda k: one_col)
                splits(7)

            ab()
            cross(0)
            mlp(0)
            gdn()
            cross(1)
            mlp(1)
            pool()
            glu(0)
            swa()
            glu(1)
            squares(x, after_wide="final2")

        @block.vector
        def _(dve):
            order = Order(dve, dve_order)
            nxt = [0]

            def split(u, i=0, per=0):
                slot, n, _ = slot_of(u, i, per)
                dve.wait_ge(hi_done, n + 1)
                dve.tensor_tensor(w_lo[:, slot], w_raw[:, slot], f32(w_hi[:, slot]), ALU.subtract).then_inc(lo_done, 1)

            def splits(n):
                for _ in range(n):
                    if nxt[0] < UNITS:
                        split(nxt[0])
                    nxt[0] += 1

            def activations(turn, gain):
                n = TURNS.index(turn)
                for k in range(KT):
                    dve.wait_ge(xt_hi, 8 * n + 2 * (k // 2) + 2)
                    dve.scalar_tensor_tensor(XTl[:, k], PS[:, 4 + k // 2, (k % 2) * T:(k % 2) * T + T], gain(k),
                                             f32(XTh[:, k]), ALU.mult, ALU.subtract).then_inc(xt_lo, 1)

            def scale_rows(name, src):
                dve.wait_ge(rstd_done, root_at(name)[1] + 1)
                for half in range(2):
                    s = slice(512 * half, 512 * half + 512)
                    dve.tensor_scalar(xn[:, 0, s], src[:, 0, s], rstd[:, 0:1], None, ALU.mult).then_inc(xn_ready, 1)

            def norm(name, gain):
                splits(1)
                scale_rows(name, x)
                activations(name, gain)
                if name in ("gdn", "swa"):
                    splits(1)

            def late_norm(name, gain):
                activations(name, gain)
                splits(1)

            def square_splits(u0, n=2):
                with dve.Fori(0, n) as i:
                    for j in range(4):
                        split(u0 + RING + j, i, 4)
                nxt[0] += 4 * n

            def square_add(u0):
                for c in range(2):
                    splits(3 + c)
                    dve.wait_ge(w_used, u0 + 4 + 4 * c)
                    xs = x[:, :, 512 * c:512 * c + 512]
                    dve.tensor_tensor(xs, PS[:, 2 * c:2 * c + 2, :], xs, ALU.add).then_inc(x_updates, 1)

            def wide_add(name, u_last, late=None):
                if late:
                    dve.wait_ge(rstd_done, root_at(late)[1] + 1)
                    dve.tensor_tensor(inv_ms[:, :], rstd[:, 0:2], rstd[:, 0:2], ALU.mult).then_inc(squared, 1)
                    dve.wait_ge(squared, 1 if late == "mlp0" else 2)
                if not late:
                    splits(2)
                dve.wait_ge(tile_done, WIDE.index(name) + 1)
                for t in range(TT):
                    if t == 1:
                        if late:
                            splits(2)
                        dve.wait_ge(w_used, u_last + 1)
                    xs = x[:, t].rearrange("p (b n) -> p b n", b=2)
                    y = PS[:, 4 + 2 * t:6 + 2 * t, :]
                    if late:
                        add = dve.scalar_tensor_tensor(xs, y, inv_ms[:, t:t + 1], xs, ALU.mult, ALU.add)
                    else:
                        add = dve.tensor_tensor(xs, y, xs, ALU.add)
                    add.then_inc(x_updates, 1)

            def by_heads(v):
                return v.rearrange("p t (h d) -> p h t d", h=4)

            def keep(blocks, bank):
                for b in blocks:
                    n, o = sum(count for _, _, count in VECTORS[b]), b - blocks[0]
                    last = dve.tensor_copy(cols[:, b, 0:n], PS[:, bank + o // 4, (o % 4) * P:(o % 4) * P + n])
                last.then_inc(vec_kept, 1)
            dve.wait_ge(vec_turned, 1)
            keep([0], 0)
            splits(1)
            dve.wait_ge(mem_landed, 16)
            scale_rows("mem", xn)
            activations("mem", lambda k: vec("mem_norm", k))
            splits(3)
            square_splits(0)
            dve.wait_ge(vec_turned, 2)
            keep([1, 2, 3, 4, 5], 4)
            dve.wait_ge(x_landed, 16)
            scale_rows("ab", x)
            square_splits(8, 4)
            dve.wait_ge(gates_hi, 1)
            dve.tensor_tensor(gate_lo[:, :, :, :], gate_w[:, :, :, :], f32(gate_hi[:, :, :, :]), ALU.subtract)\
                .then_inc(gates_lo, 1)
            square_splits(24, 2)

            def ab():
                activations("ab", lambda k: vec("mix_norm", k))
                dve.wait_ge(misc_landed, MISC)
                splits(4)
                dve.wait_ge(ab_gates, 1)
                dve.tensor_scalar(ab_rows[0:4, 0], PS[0:4, 7, 0:T], gbias[0:4, 0:1], 1 / 15, ALU.add, ALU.mult)
                dve.tensor_scalar(ab_rows[0:4, 1], PS[32:36, 7, 0:T], gbias[32:36, 0:1], None, ALU.add).then_inc(ab_f, 1)
                dve.wait_ge(ab_lnf, 1)
                r = ab_rows
                order(dve.scalar_tensor_tensor(r[0:4, 6], r[0:4, 1], 0.0, r[0:4, 5], ALU.min, ALU.subtract))
                order(dve.tensor_tensor_scan(r[0:4, 8], r[0:4, 6], f32(zeros[0:4, 0:T]), 0.0, ALU.add, ALU.add))
                order(dve.scalar_tensor_tensor(r[0:4, 9], r[0:4, 2], 15.0, r[0:4, 8], ALU.mult, ALU.subtract))
                order(dve.tensor_tensor_scan(r[0:4, 10], r[0:4, 9], f32(zeros[0:4, 0:T]), 0.0, ALU.max, ALU.add))
                dve.tensor_scalar(r[0:4, 11], r[0:4, 10], -1.0, None, ALU.mult)
                dve.scalar_tensor_tensor(r[0:4, 12], r[0:4, 8], -1.0, r[0:4, 10], ALU.mult, ALU.subtract).then_inc(ab_rows_done, 1)
                splits(4)
                dve.wait_ge(ab_turned, 1)
                dve.tensor_copy(mcol[:, :, :], PS[:, 6, 8:16].rearrange("p (t h) -> p t h", t=2))
                order(dve.tensor_copy(acol[:, :, :], PS[:, 6, 0:8].rearrange("p (t h) -> p t h", t=2)))
                for h in range(4):
                    o = (h % 2) * T
                    dve.scalar_tensor_tensor(decay[:, h, 0:T], PS[:, 4 + h // 2, o:o + T], acol[:, 0, h:h + 1],
                                             C("causal_min"), ALU.add, ALU.min)
                    last = dve.scalar_tensor_tensor(decay[:, h, T:384], PS[:, 4 + h // 2, o + P:o + T],
                                                    acol[:, 1, h:h + 1], C("causal_min")[:, 0:P], ALU.add, ALU.min)
                last.then_inc(ab_args, 1)
                splits(4)
                dve.wait_ge(ab_scores, 1)
                dve.wait_ge(ab_decayed, 1)
                dve.tensor_tensor(prob[:, :, :], PS[:, 4:8, 0:384], decay[:, :, :], ALU.mult).then_inc(ab_probs, 1)
                splits(4)
                dve.wait_ge(ab_outs, 1)
                o = PS[:, 4:8, :].rearrange("p h (t d) -> p h t d", t=2)
                order(dve.tensor_copy(rden[:, :, :], o[:, :, :, 128]))
                order(dve.scalar_tensor_tensor(rden[:, :, :], rden[:, :, :], -1.0, rden[:, :, :], ALU.mult, ALU.max))
                order(dve.tensor_tensor(rden[:, :, :], rden[:, :, :], emcol[:, :, :].rearrange("p t h -> p h t"), ALU.max))
                order(dve.reciprocal(rden[:, :, :], rden[:, :, :]))
                hm = by_heads(hmix[:, :, 0:512])
                dve.tensor_tensor(hm, o[:, :, :, 0:128], rden[:, :, :].unsqueeze(3).broadcast_to([P, 4, 2, 128]),
                                  ALU.mult).then_inc(ab_norm, 1)
                dve.wait_ge(ab_sq, 1)
                dve.tensor_reduce(ss[:, 0:8], hsq[:, :, :].rearrange("p t (h d) -> p (t h) d", h=4), AX.X,
                                  ALU.add).then_inc(sq_done, 1)
                splits(4)
                dve.wait_ge(sb_z, 1)
                dve.tensor_copy(sb_zs[:, :, :], PS[:, 4:8, 0:384]).then_inc(sb_kept, 1)
                dve.wait_ge(sb_lned, 1)
                order(dve.scalar_tensor_tensor(sb_sp[:, :, :], sb_zs[:, :, :], 0.0, sb_ln[:, :, :], ALU.max, ALU.add))

                def diagonals(v):
                    return v[:, :, :].rearrange("p h (b t) -> p h b t", b=3)[:, :, 0:3:2, :]

                def mask(name):
                    return C(name).unsqueeze(1).unsqueeze(1).broadcast_to([P, 4, 2, P])
                dve.tensor_tensor(diagonals(sb_sp), diagonals(sb_sp), mask("strict"), ALU.mult).then_inc(sb_sped, 1)
                dve.wait_ge(rstd_done, root_at("ab_heads")[1] + 1)
                hv = hmix[:, :, 0:512].rearrange("p t (h d) -> p t h d", h=4)
                order(dve.tensor_tensor(hv, hv, rstd[:, 0:8].rearrange("p (t h) -> p t h", t=2).unsqueeze(3)
                                        .broadcast_to([P, 2, 4, 128]), ALU.mult))
                dve.tensor_tensor(hmix[:, :, 0:512], hmix[:, :, 0:512], ab_og[:, :, :], ALU.mult).then_inc(ab_mixed, 1)
                dve.wait_ge(sb_cum, 1)
                for h in (0, 2):
                    order(dve.tensor_tensor(sb_zs[:, h:h + 2], sb_zs[:, h:h + 2], PS[:, 4 + h:6 + h, 0:384], ALU.subtract))
                    v = diagonals(sb_zs)[:, h:h + 2]
                    dve.tensor_tensor(v, v, C("strict_min").unsqueeze(1).unsqueeze(1).broadcast_to([P, 2, 2, P]),
                                      ALU.min).then_inc(sb_arg, 1)
                splits(4)
                activations("ab_o", lambda k: vec("ab_head_gain", k) if k < 4 else one_col)
                square_add(UNIT0["ab_o"])

            def cross(l):
                late_norm(f"xq{l}", lambda k: vec("xa_norm", 8 * l + k))
                square_splits(UNIT0[f"xq{l}"])
                dve.wait_ge(rstd_done, root_at(f"xq{l}")[1] + 1)
                dve.tensor_scalar(xa_rs[:, 0:2], rstd[:, 0:2], 1 / 16, None, ALU.mult)
                order(dve.tensor_scalar(xa_rs[:, 2:4], rstd[:, 0:2], -1 / 16, None, ALU.mult))

                def maxima(h):
                    dve.wait_ge(xa_scores, 4 * l + h + 1)
                    m = slice(2 * h, 2 * h + 2)
                    order(dve.tensor_reduce(xa_m[:, m], PS[:, 4 + h, :].rearrange("p (t s) -> p t s", t=2), AX.X,
                                            ALU.max))
                    dve.tensor_tensor(xa_nm[:, m], xa_m[:, m], xa_rs[:, 2:4], ALU.mult).then_inc(xa_max, 1)

                def normalise(h):
                    dve.wait_ge(xa_exp, 8 * l + 2 * h + 2)
                    order(dve.reciprocal(xa_r[:, 2 * h:2 * h + 2], xa_s[:, 2 * h:2 * h + 2]))
                    for t in range(TT):
                        last = dve.tensor_scalar(xa_p[:, h, t], xa_p[:, h, t], xa_r[:, 2 * h + t:2 * h + t + 1], None, ALU.mult)
                    last.then_inc(xa_probs, 1)

                def copy_pt(h):
                    dve.wait_ge(xa_turned, 4 * l + h + 1)
                    dve.tensor_copy(xa_pt[:, h], PS[:, h, :].rearrange("p (m t) -> p m t", m=2)).then_inc(xa_pt_dve, 1)
                maxima(0)
                maxima(1)
                normalise(0)
                maxima(2)
                normalise(1)
                maxima(3)
                normalise(2)
                normalise(3)
                copy_pt(1)
                copy_pt(3)
                activations(f"xo{l}", lambda k: one_col)
                square_add(UNIT0[f"xo{l}"])

            def mlp(l):
                late_norm(f"mlp{l}", lambda k: vec("mlp_norm", 8 * l + k))
                u0, n, wu = UNIT0[f"mlp{l}"], FF // 512, 4
                h0 = HID0[f"mlp{l}"]

                def hidden(c, q):
                    dve.wait_ge(hid_in, c + (h0 + 1))
                    order(dve.tensor_tensor(relu2[:, q], relu[:, q], relu[:, q], ALU.mult))
                    dve.wait_ge(hid_hi_done, c + (h0 + 1))
                    dve.tensor_tensor(hid_lo[:, q], relu2[:, q], f32(hid_hi[:, q]), ALU.subtract).then_inc(hid_lo_done, 1)

                splits(4)
                hidden(0, 0)
                u1 = nxt[0]
                pairs = (n - 1) // 2
                per = 2 * (4 + wu)
                with dve.Fori(0, pairs) as i:
                    order.loop(i, 2)
                    for q in range(2):
                        for j in range(4 + wu):
                            split(u1 + q * (4 + wu) + j, i, per)
                            if j == wu - 1:
                                hidden(q + 1 + 2 * i, (q + 1) % 2)
                    order.end(pairs)
                nxt[0] = u1 + pairs * per
                splits(4)
                hidden(n - 1, (n - 1) % 2)
                splits(4)
                wide_add(f"mlp{l}", u0 + n * (4 + wu) - 1, late=f"mlp{l}")

            def glu(l):
                norm(f"ffn{l}", lambda k: ffn_gain[:, l, k:k + 1])
                u0, n, wu = UNIT0[f"ffn{l}"], GLU // 256, 2
                h0, g0 = HID0[f"ffn{l}"], (GLU // 256) * l
                dve.wait_ge(pool_set, POOL_SET[f"ffn{l}"])

                def hidden(c, q, fill):
                    dve.wait_ge(glu_in, c + (g0 + 1))
                    for tap in range(2):
                        for f in range(4):
                            part, k = f // 2, f % 2
                            last = dve.scalar_tensor_tensor(
                                glu_acc[:, q, f], glu_pad[:, q, f, tap:tap + T],
                                vec("ffn_conv_w_2", 132 * l + 44 * tap + 22 * part + k, 2 * c), glu_acc[:, q, f],
                                ALU.mult, ALU.add)
                        if tap == 0:
                            order(last)
                    last.then_inc(glu_conv, 1)
                    fill[0]()
                    dve.wait_ge(glu_silued, c + (g0 + 1))
                    dve.tensor_tensor(glu_prod[:, q], glu_acc[:, q, 0:2], glu_silu[:, q], ALU.mult).then_inc(glu_mult, 1)
                    fill[1]()
                    dve.wait_ge(hid_hi_done, c + (h0 + 1))
                    dve.tensor_tensor(hid_lo[:, q, 0:2], glu_prod[:, q], f32(hid_hi[:, q, 0:2]), ALU.subtract)\
                        .then_inc(hid_lo_done, 1)

                one = lambda: splits(1)
                splits(4)
                hidden(0, 0, (one, one))
                v0 = nxt[0]
                pairs = (n - 3) // 2
                per = 2 * (4 + wu)
                with dve.Fori(0, pairs) as i:
                    order.loop(i, 2)
                    for q in range(2):
                        v = v0 + q * (4 + wu)
                        for j in range(4):
                            split(v + j, i, per)
                        hidden(q + 1 + 2 * i, (q + 1) % 2,
                               (lambda v=v: split(v + 4, i, per), lambda v=v: split(v + 5, i, per)))
                    order.end(pairs)
                nxt[0] = v0 + pairs * per
                splits(4)
                hidden(n - 2, (n - 2) % 2, (one, one))
                splits(2)
                hidden(n - 1, (n - 1) % 2, (lambda: None, lambda: None))
                wide_add(f"ffn{l}", u0 + n * (4 + wu) - 1)

            def gdn():
                norm("gdn", lambda k: vec("mix_norm", 8 + k))
                u0 = UNIT0["gdn_in"]
                dve.wait_ge(pool_set, POOL_SET["gdn"])
                with dve.Fori(0, 3) as i:
                    order.loop(i, 4)
                    for q in range(2):
                        for j in range(3):
                            split(u0 + 4 + 4 * q + j, i, 8)
                        dve.wait_ge(gd_free, 2 * i + (q + 3))
                        for tap in range(3):
                            for f in range(4):
                                last = dve.scalar_tensor_tensor(
                                    gd_acc[:, q, f], gd_pad[:, q, f, tap:tap + T],
                                    vec("c_conv_w", 24 * tap + 4 * q + f, 8 * i), gd_acc[:, q, f], ALU.mult, ALU.add)
                            if tap < 2:
                                order(last)
                            if tap == 0:
                                split(u0 + 4 + 4 * q + 3, i, 8)
                        last.then_inc(gd_conv, 1)
                    order.end(3)
                nxt[0] += 24
                splits(1)
                R = gd_rows
                dve.wait_ge(gd_gates_s, 1)
                dve.tensor_scalar(R[0:8, 1], PS[32:40, 7, 0:T], gbias[32:40, 1:2], None, ALU.add)
                dve.tensor_copy(R[0:8, 2], PS[0:8, 7, 0:T]).then_inc(gd_f, 1)
                dve.wait_ge(gd_lnf, 1)
                dve.scalar_tensor_tensor(R[0:8, 7], R[0:8, 2], 0.0, R[0:8, 4], ALU.min, ALU.subtract)
                order(dve.scalar_tensor_tensor(R[0:8, 5], R[0:8, 1], 0.0, R[0:8, 3], ALU.max, ALU.add))
                order(dve.tensor_scalar(R[0:8, 5], R[0:8, 5], gd_nea[0:8, 1:2], -1.0, ALU.mult, ALU.mult))
                for c in range(2):
                    s = slice(c * P, c * P + P)
                    last = dve.tensor_tensor_scan(R[0:8, 6, s], R[0:8, 5, s], f32(zeros[0:8, 0:P]), 0.0, ALU.add, ALU.add)
                last.then_inc(gd_rows_s, 1)
                dve.wait_ge(gd_rows_s, 1)
                dve.wait_ge(gd_rooted, 1)
                order(dve.tensor_tensor(R[0:8, 7], R[0:8, 7], R[0:8, 6], ALU.add))
                dve.scalar_tensor_tensor(R[0:8, 3], R[0:8, 2], -0.5, R[0:8, 7], ALU.mult, ALU.add)
                order(dve.tensor_scalar(R[0:8, 1], R[0:8, 1], -0.5, -0.5 * math.log(128), ALU.mult, ALU.add))
                dve.tensor_tensor(R[0:8, 4], R[0:8, 1], R[0:8, 6], ALU.add)
                dve.tensor_scalar(gd_last[0:8, :], ident[0:8, 0:8], R[0:8, 6, P - 1:P], None, ALU.mult)
                dve.scalar_tensor_tensor(R[0:8, 5], R[0:8, 2], 0.5, R[0:8, 6], ALU.mult, ALU.add).then_inc(gd_logs, 1)
                splits(2)
                dve.wait_ge(gd_colt, 1)
                dve.tensor_copy(gd_cols[:, :, :], PS[:, 6, 0:56].rearrange("p (k h) -> p k h", h=8)).then_inc(gd_colk, 1)
                dve.wait_ge(gd_colk, 1)
                dve.tensor_tensor(gd_gl[:, :], gd_cols[:, 6], gd_cols[:, 0], ALU.subtract).then_inc(gd_colk, 1)
                splits(1)

                def decay_args(dst):
                    for c in range(2):
                        for h in range(8):
                            o = (h % 2) * T + c * P
                            last = dve.scalar_tensor_tensor(dst[:, c, h], PS[:, 4 + h // 2, o:o + P], gd_cols[:, c, h:h + 1],
                                                            C("causal_add"), ALU.subtract, ALU.add)
                    last.then_inc(gd_args, 1)
                dve.wait_ge(gd_bcast, 1)
                decay_args(gd_U)
                splits(2)
                dve.wait_ge(gd_bcast, 2)
                decay_args(gd_E)
                splits(2)
                dve.wait_ge(gd_kk, 1)
                dve.wait_ge(gd_decayed, 1)
                for g in range(2):
                    u = gd_U[:, g].rearrange("p (b k) t -> p b k t", k=4)
                    order(dve.tensor_tensor(u, u, PS[:, 4 + 2 * g:6 + 2 * g, :].rearrange("p b (k t) -> p b k t", k=4),
                                            ALU.mult))

                def wide_mask(name):
                    return C(name).unsqueeze(1).broadcast_to([P, 8, P])

                def masked(g, level):
                    return dve.tensor_tensor(gd_um[:, g], gd_U[:, g], wide_mask(f"level{level}"), ALU.mult)\
                        .then_inc(gd_masked, 1)

                def four(v):
                    return v.rearrange("p (b k) t -> p b k t", k=4)
                masked(0, 0)
                masked(1, 0)
                dve.wait_ge(gd_qk, 1)
                dve.wait_ge(gd_decayed, 2)
                allE = gd_E[:, :, :, :].rearrange("p c (b k) t -> p (c b) k t", k=4)
                dve.tensor_tensor(allE, allE, PS[:, 0:4, :].rearrange("p b (k t) -> p b k t", k=4), ALU.mult)\
                    .then_inc(gd_made, 1)
                dve.wait_ge(gd_masked, 2)
                for g in range(2):
                    dve.tensor_tensor(gd_XT[:, g], wide_mask("ident"), gd_um[:, g], ALU.subtract)
                    dve.wait_ge(gd_xps, g + 1)
                    dve.tensor_tensor(four(gd_X[:, g]), C("ident").unsqueeze(1).unsqueeze(1).broadcast_to([P, 2, 4, P]),
                                      group_banks(g, 0), ALU.subtract).then_inc(gd_xnew, 1)
                    dve.wait_ge(gd_xnew, g + 1)
                    masked(g, 1)
                for level in range(1, LEVELS):
                    size = 2 ** level
                    if level + 1 < LEVELS:
                        for g in range(2):
                            dve.wait_ge(gd_yps, 2 * level + g - 1)
                            masked(g, level + 1)
                    for g in range(2):
                        dve.wait_ge(gd_xps, 2 * level + g + 1)
                        for dst, b, which in ((gd_X, 2, 0), (gd_XT, 0, 1)):
                            if dst is gd_XT or level + 1 < LEVELS:
                                v = halves(dst[:, g], size, which).rearrange("p h a t -> p (h a) t")
                                lo = 4 * (1 - g) + b
                                y = PS[:, lo, :].rearrange("p (n t) -> p n t", t=size)
                                last = dve.tensor_tensor(v, v, y, ALU.subtract)
                        last.then_inc(gd_xnew, 1)
                dve.wait_ge(gd_fin_pe, 3)
                dve.wait_ge(gd_scaled, 2)
                for h in range(8):
                    last = dve.scalar_tensor_tensor(gd_bv[:, 1, h], PS[:, 6 + h // 4, (h % 4) * P:(h % 4) * P + P],
                                                    gd_beg[:, h:h + 1], gd_bv[:, 1, h], ALU.mult, ALU.subtract, reverse1=True)
                last.then_inc(gd_fin_dve, 1)
                def mixed(c):
                    gate = gd_gate[:, c]
                    order(dve.tensor_tensor(gate, gd_o[:, c], gate, ALU.mult))
                    dve.wait_ge(gd_osq_s, c + 1)
                    dve.tensor_reduce(ss[:, 0:8], gd_osqt[:, c].rearrange("p (h d) -> p h d", h=8), AX.X,
                                      ALU.add).then_inc(sq_done, 1)
                    dve.wait_ge(rstd_done, root_at(f"gdn_heads{c}")[1] + 1)
                    dve.tensor_tensor(gd_o[:, c].rearrange("p (h d) -> p h d", h=8), gate.rearrange("p (h d) -> p h d", h=8),
                                      rstd[:, 0:8].unsqueeze(2).broadcast_to([P, 8, P]), ALU.mult).then_inc(gd_mixed, 1)
                dve.wait_ge(gd_osq_s, 1)
                mixed(0)
                dve.wait_ge(gd_fin_act, 4)
                dve.wait_ge(gd_fin_pe, 5)
                for h in range(8):
                    o = gd_o[:, 1, h * P:(h + 1) * P]
                    last = dve.scalar_tensor_tensor(o, PS[:, 6 + h // 4, (h % 4) * P:(h % 4) * P + P], gd_eg[:, h:h + 1], o,
                                                    ALU.mult, ALU.add)
                last.then_inc(gd_fin_dve, 1)
                dve.wait_ge(gd_fin_dve, 2)
                mixed(1)
                activations("gdn_o", lambda k: vec("c_head_gain", 0))
                square_add(UNIT0["gdn_o"])

            def pool():
                dve.wait_ge(bc_landed, 64)
                for t in range(TT):
                    dve.wait_ge(x_updates, X_COUNT["final1"] - 1 + t)
                    dve.tensor_tensor(xn[:, t], x[:, t], bc[:, 0], ALU.mult).then_inc(gained, 1)
                splits(1)
                order(dve.tensor_tensor(bc[:, 2], bc[:, 2], bc[:, 3], ALU.mult))
                dve.wait_ge(rstd_done, root_at("final1")[1] + 1)
                for t in range(TT):
                    dve.tensor_scalar(xn[:, t], xn[:, t], rstd[:, 4 + t:5 + t], None, ALU.mult).then_inc(xn_ready, 1)
                for t in range(TT):
                    dve.scalar_tensor_tensor(x[:, t], x[:, t], rstd[:, t:t + 1], bc[:, 0], ALU.mult, ALU.mult)\
                        .then_inc(x_updates, 1)
                dve.wait_ge(x_updates, X_COUNT["final1"] + 2)
                order(dve.tensor_tensor(x[:, :, :], x[:, :, :], bc[:, 2].unsqueeze(1).broadcast_to([P, TT, D]), ALU.add))
                activations("pool", lambda k: vec("norm_mix_2", k))
                splits(2)
                for c in range(2):
                    s = slice(512 * c, 512 * c + 512)
                    dve.wait_ge(w_used, UNIT0["pool"] + c + 1)
                    order(dve.tensor_tensor(xn[:, :, s], PS[:, 2 * c:2 * c + 2, :],
                                            bc[:, 3, s].unsqueeze(1).broadcast_to([P, 2, 512]), ALU.mult))
                    dve.tensor_tensor(x[:, :, s], x[:, :, s], xn[:, :, s], ALU.add).then_inc(x_updates, 1)

            def swa():
                norm("swa", lambda k: vec("norm_mix_2", 8 + k))
                b, n = vec_at("attn_b_qkv_2", 0)
                dve.tensor_scalar(sw_qb[:, :], cols[:, b, n:n + 8], 0.125, None, ALU.mult).then_inc(sw_den, 1)
                u0 = UNIT0["qkv"]
                splits(3)
                dve.wait_ge(w_used, u0 + 4)
                dve.tensor_tensor(sw_v[:, :, :], PS[:, 1, :].rearrange("p (t n) -> p t n", t=2),
                                  vbias[:, :].unsqueeze(1).broadcast_to([P, 2, T]), ALU.add).then_inc(v_kept, 1)
                splits(6)

                def maxima(grp):
                    hs, v = slice(4 * grp, 4 * grp + 4), sw_s[:, grp % 3]
                    dve.wait_ge(sw_scores, grp + 1)
                    if grp == 3:
                        dve.wait_ge(sw_turned, 1)
                    for j in range(4):
                        h = 4 * grp + j
                        last = dve.scalar_tensor_tensor(v[:, j], C("dist"), -float(2.0 ** (-8.0 / SWA_HEADS * (h + 1))),
                                                        PS[:, 4 + j, 0:384], ALU.mult, ALU.add)
                    last.then_inc(sw_kept, 1)
                    dve.wait_ge(sw_kept, grp + 1)
                    dve.tensor_reduce(sw_m[:, 0, hs], v[:, :, 0:128], AX.X, ALU.max)
                    order(dve.tensor_reduce(sw_m[:, 1, hs], v[:, :, 128:384], AX.X, ALU.max))
                    sk = sinks[:, hs].unsqueeze(1).broadcast_to([P, 2, 4])
                    order(dve.tensor_tensor(sw_m[:, :, hs], sw_m[:, :, hs], sk, ALU.max))
                    dve.tensor_scalar(sw_nm[:, :, hs], sw_m[:, :, hs], -1.0, None, ALU.mult)
                    dve.tensor_tensor(sw_es[:, :, hs], sk, sw_m[:, :, hs], ALU.subtract).then_inc(sw_max, 1)

                def normalise(grp):
                    hs, v = slice(4 * grp, 4 * grp + 4), sw_s[:, grp % 3]
                    dve.wait_ge(sw_exp, 8 * grp + 8)
                    order(dve.tensor_tensor(sw_r[:, :, hs], sw_sum[:, :, hs], sw_es[:, :, hs], ALU.add))
                    order(dve.reciprocal(sw_r[:, :, hs], sw_r[:, :, hs]))
                    for t, s in ((0, slice(0, 128)), (1, slice(128, 384))):
                        last = dve.tensor_tensor(v[:, :, s], v[:, :, s],
                                                 sw_r[:, t, hs].unsqueeze(2).broadcast_to([P, 4, s.stop - s.start]), ALU.mult)
                    last.then_inc(sw_probs, 1)
                maxima(0)
                splits(2)
                for grp in range(1, 4):
                    maxima(grp)
                    normalise(grp - 1)
                    if grp == 1:
                        splits(1)
                normalise(3)
                activations("swa_o", lambda k: one_col)
                square_add(UNIT0["swa_o"])

            ab()
            cross(0)
            mlp(0)
            gdn()
            cross(1)
            mlp(1)
            pool()
            glu(0)
            swa()
            glu(1)
            dve.wait_ge(rstd_done, root_at("final2")[1] + 1)
            for t in range(TT):
                dve.scalar_tensor_tensor(xn[:, t], x[:, t], rstd[:, t:t + 1], bc[:, 1], ALU.mult, ALU.mult)\
                    .then_inc(xn_ready, 1)

        @block.tensor
        def _(pe):
            mm = pe.matmul

            def kt_pair_wait(turn, j):
                pe.wait_ge(xt_lo, 8 * TURNS.index(turn) + 2 * j + 2)

            def three(dst, ah, al, bh, bl, first, last):
                mm(dst, ah, bh, start=first, stop=False, skip_group_check=True)
                mm(dst, ah, bl, start=False, stop=False, skip_group_check=True)
                return mm(dst, al, bh, start=False, stop=last, skip_group_check=True)

            def token_unit(slot, j, bank, i, cols_=slice(0, 512)):
                n = cols_.stop - cols_.start
                for k in range(2):
                    for t in range(TT):
                        kt = 2 * j + k
                        last = three(PS[:, ds(bank + 2 * i + t, 1), 0:n].rearrange("p a n -> p (a n)") if not isinstance(i, int)
                                     else PS[:, bank + 2 * i + t, 0:n],
                                     XTh[:, kt, t * P:t * P + P], XTl[:, kt, t * P:t * P + P],
                                     w_hi[:, slot, k, cols_], w_lo[:, slot, k, cols_], kt == 0, kt == KT - 1)
                return last

            def feature_unit(slot, j, bank, i, tiles=4):
                for k in range(2):
                    kt = 2 * j + k
                    for f in range(tiles):
                        if isinstance(i, int):
                            dst = PS[:, bank + 2 * i + f // 2, (f % 2) * T:(f % 2) * T + T]
                        else:
                            dst = PS[:, ds(bank + 2 * i + f // 2, 1), (f % 2) * T:(f % 2) * T + T].rearrange("p a n -> p (a n)")
                        s = slice(f * P, f * P + P)
                        last = three(dst, w_hi[:, slot, k, s], w_lo[:, slot, k, s], XTh[:, kt], XTl[:, kt],
                                     kt == 0 and f % 2 == 0, kt == KT - 1)
                return last

            def chunk(u, turn, unit, bank, bank_i=0, i=0, per=0):
                for j in range(4):
                    slot, n, _ = slot_of(u + j, i, per)
                    if turn:
                        kt_pair_wait(turn, j)
                    pe.wait_ge(lo_done, n + 1)
                    unit(slot, j, bank, bank_i).then_inc(w_used, 1)

            def square(u0, turn, unit):
                with pe.Fori(0, 2) as i:
                    chunk(u0, turn, unit, 0, i, i, 4)

            def turn(name, src=xn, wait=lambda b: None):
                for b in range(4):
                    wait(b)
                    for k in range(2):
                        for t in range(TT):
                            f = 2 * b + k
                            last = pe.transpose(PS[:, 4 + b, k * T + t * P:k * T + t * P + P],
                                                src[:, t, f:D:KT] if name in ("ffn0", "ffn1") else
                                                src[:, t, f * P:f * P + P], ident)
                    last.then_inc(turned, 1)

            def norm(name):
                if name in NORMS:
                    n, m = 2 * NORMS.index(name), 2 * NORMS_ACT.index(name)

                    def halves_there(b):
                        half = 1 if name in ("ffn0", "ffn1") else b // 2
                        pe.wait_ge(xn_ready, n + half + 1)
                        pe.wait_ge(xn_ready_act, m + half + 1)
                    turn(name, xn, halves_there)
                else:
                    turn(name, x, lambda b: pe.wait_ge(x_updates, X_COUNT[name] - 1 + b // 2))

            def gates(which, width):
                for k in range(KT):
                    last = three(PS[0:width, 7, 0:T], gate_hi[:, which, k, 0:width], gate_lo[:, which, k, 0:width],
                                 XTh[:, k], XTl[:, k], k == 0, k == KT - 1)
                return last

            pe.wait_ge(const_landed, 16)

            def turn_vectors(blocks, bank):
                pe.wait_ge(vec_landed[min(blocks[0], 1)], 16 * sum(len(VECTORS[b]) for b in blocks))
                for b in blocks:
                    n, o = sum(count for _, _, count in VECTORS[b]), b - blocks[0]
                    last = pe.transpose(PS[:, bank + o // 4, (o % 4) * P:(o % 4) * P + n], vec_rows[0:n, b, :],
                                        ident[0:n, 0:n])
                last.then_inc(vec_turned, 1)
            turn_vectors([0], 0)
            norm("mem")
            pe.wait_ge(pool_set, 2)
            pe.wait_ge(vec_kept, 1)
            for k, unit in enumerate((feature_unit, token_unit, feature_unit, token_unit)):
                with pe.Fori(0, 2) as i:
                    if k:
                        pe.wait_ge(evac_act, i + (2 * k - 1))
                    chunk(8 * k, "mem", unit, 0, i, i, 4)
                if k == 0:
                    turn_vectors([1, 2, 3, 4, 5], 4)

            def ab():
                pe.wait_ge(vec_kept, 2)
                norm("ab")
                pe.wait_ge(evac_act, EVAC0["ab_in"])
                pe.wait_ge(misc_landed, MISC)
                u, e = UNIT0["ab_in"], EVAC0["ab_in"]
                chunk(u, "ab", feature_unit, 0)
                pe.wait_ge(gates_lo, 1)
                gates(0, 36).then_inc(ab_gates, 1)
                chunk(u + 4, "ab", token_unit, 2)
                pe.wait_ge(ab_rows_done, 1)
                for t in range(TT):
                    pe.transpose(PS[:, 6, 4 * t:4 * t + 4], ab_rows[0:4, 9, t * P:t * P + P], ident[0:4, 0:4])
                    pe.transpose(PS[:, 6, 8 + 4 * t:12 + 4 * t], ab_rows[0:4, 12, t * P:t * P + P], ident[0:4, 0:4])
                for h in range(4):
                    last = mm(PS[:, 4 + h // 2, (h % 2) * T:(h % 2) * T + T], C(f"select{h}")[0:4, :], ab_rows[0:4, 11],
                              start=True, stop=True)
                last.then_inc(ab_turned, 1)
                pe.wait_ge(evac_act, e + 1)
                chunk(u + 8, "ab", token_unit, 0)
                pe.wait_ge(ab_args, 1)
                for h in range(4):
                    r = slice(64 * (h % 2), 64 * (h % 2) + 64)
                    mm(PS[:, 4 + h, 0:T], ab_qk[r, 2 + h // 2, 0:P], ab_qk[r, h // 2, 0:T], start=True, stop=True)
                    last = mm(PS[:, 4 + h, T:384], ab_qk[r, 2 + h // 2, P:T], ab_qk[r, h // 2, P:T], start=True, stop=True)
                last.then_inc(ab_scores, 1)
                pe.wait_ge(evac_act, e + 2)
                chunk(u + 12, "ab", feature_unit, 2)
                pe.wait_ge(ab_probs, 1)
                pe.wait_ge(pool_set, POOL_SET["ab"])
                for h in range(4):
                    mm(PS[:, 4 + h, 0:129], prob[:, h, 0:P], ab_v[:, 0, h, 0:129], start=True, stop=True)
                    mm(PS[:, 4 + h, T:T + 129], prob[:, h, P:T], ab_v[:, 0, h, 0:129], start=True, stop=False)
                    last = mm(PS[:, 4 + h, T:T + 129], prob[:, h, T:384], ab_v[:, 1, h, 0:129], start=False, stop=True)
                last.then_inc(ab_outs, 1)
                pe.wait_ge(evac_act, e + 3)
                chunk(u + 16, "ab", feature_unit, 0)
                pe.wait_ge(ab_norm, 1)
                pe.wait_ge(evac_act, e + 5)
                for h in range(4):
                    mm(PS[:, 4 + h, 0:T], sb_k[:, h, 0:P], sb_q[:, h, 0:T], start=True, stop=True)
                    last = mm(PS[:, 4 + h, T:384], sb_k[:, h, P:T], sb_q[:, h, P:T], start=True, stop=True)
                last.then_inc(sb_z, 1)
                chunk(u + 20, "ab", token_unit, 2)
                pe.wait_ge(sb_sped, 1)
                for h in range(4):
                    mm(PS[:, 4 + h, 0:T], C("suffix"), sb_sp[:, h, 0:T], start=True, stop=False, skip_group_check=True)
                    mm(PS[:, 4 + h, P:T], ones, sb_sp[:, h, T:384], start=False, stop=True, skip_group_check=True)
                    last = mm(PS[:, 4 + h, T:384], C("suffix"), sb_sp[:, h, T:384], start=True, stop=True, skip_group_check=True)
                last.then_inc(sb_cum, 1)
                pe.wait_ge(evac_act, e + 6)
                for h in range(4):
                    pe.wait_ge(sb_w, h // 2 + 1)
                    v = [sb_v[:, s, h * P:h * P + P] for s in range(2)]
                    mm(PS[:, h, 0:P], sb_ln[:, h, 0:P], v[0], start=True, stop=True)
                    mm(PS[:, h, T:T + P], sb_ln[:, h, P:T], v[0], start=True, stop=False)
                    last = mm(PS[:, h, T:T + P], sb_ln[:, h, T:384], v[1], start=False, stop=True)
                last.then_inc(sb_out, 1)
                pe.wait_ge(ab_mixed, 2)
                turn("ab_o")
                square(UNIT0["ab_o"], "ab_o", token_unit)

            def cross(l):
                norm(f"xq{l}")
                square(UNIT0[f"xq{l}"], f"xq{l}", feature_unit)
                pe.wait_ge(evac_act, EVAC0[f"xq{l}"] + 2)
                for h in range(4):
                    for t in range(TT):
                        for d in range(2):
                            last = mm(PS[:, 4 + h, t * T:t * T + T], xa_q[:, 2 * h + d, t * P:t * P + P],
                                      K_of[l][:, 2 * h + d], start=d == 0, stop=d == 1)
                    last.then_inc(xa_scores, 1)
                for h in range(4):
                    pe.wait_ge(xa_probs, 4 * l + h + 1)
                    for m in range(2):
                        for t in range(TT):
                            last = pe.transpose(PS[:, h, m * T + t * P:m * T + t * P + P], xa_p[:, h, t, m * P:m * P + P], ident)
                    last.then_inc(xa_turned, 1)
                for h in range(4):
                    pe.wait_ge((xa_pt_act, xa_pt_dve)[h % 2], 2 * l + h // 2 + 1)
                    for d in range(2):
                        for m in range(2):
                            last = mm(PS[:, 4 + h, d * T:d * T + T], V_of[l][:, m, h * T + d * P:h * T + d * P + P],
                                      xa_pt[:, h, m], start=m == 0, stop=m == 1)
                    last.then_inc(turned, 1)
                square(UNIT0[f"xo{l}"], f"xo{l}", token_unit)

            def wide(name, n, wu):
                u0, h0 = UNIT0[name], HID0[name]

                def second(u, c, q, i, per):
                    pe.wait_ge(hid_lo_done, c + (h0 + 1))
                    for j in range(wu):
                        slot, nn, _ = slot_of(u + j, i, per)
                        pe.wait_ge(lo_done, nn + 1)
                        half = j % 2
                        for k in range(2):
                            f = 2 * (j // 2) + k
                            for t in range(TT):
                                s = slice(t * P, t * P + P)
                                last = three(PS[:, 4 + 2 * t + half, :], hid_hi[:, q, f, s], hid_lo[:, q, f, s],
                                             w_hi[:, slot, k], w_lo[:, slot, k], False, False)
                        last.then_inc(w_used, 1)

                norm(name)
                chunk(u0, name, feature_unit, 0)
                for b in range(4):
                    mm(PS[:, 4 + b, :], zeros[:, 0:P], zeros[:, :], start=True, stop=False, skip_group_check=True)
                pairs = (n - 1) // 2
                per = 2 * (4 + wu)
                with pe.Fori(0, pairs) as i:
                    for q in range(2):
                        u = u0 + 4 + q * (4 + wu)
                        chunk(u, None, feature_unit, 2 * ((q + 1) % 2), 0, i, per)
                        second(u + 4, 2 * i + q, q, i, per)
                for c in range(2 * pairs, n):
                    u = u0 + 4 + c * (4 + wu)
                    if c + 1 < n:
                        chunk(u, None, feature_unit, 2 * ((c + 1) % 2))
                        second(u + 4, c, c % 2, 0, 0)
                q = (n - 1) % 2
                pe.wait_ge(hid_lo_done, h0 + n)
                for t in range(TT):
                    s = slice(t * P, t * P + P)
                    for j in range(wu):
                        pe.wait_ge(lo_done, u + j + 1)
                        for k in range(2):
                            f = 2 * (j // 2) + k
                            last = three(PS[:, 4 + 2 * t + j % 2, :], hid_hi[:, q, f, s], hid_lo[:, q, f, s],
                                         w_hi[:, (u + j) % RING, k], w_lo[:, (u + j) % RING, k], False, False)
                        if t == 1:
                            last.then_inc(w_used, 1)
                        elif j == wu - 1:
                            last.then_inc(tile_done, 1)

            def gdn():
                norm("gdn")
                u0, e = UNIT0["gdn_in"], EVAC0["gdn_in"]
                pe.wait_ge(evac_act, e)
                with pe.Fori(0, 3) as i:
                    for q in range(2):
                        pe.wait_ge(gd_free, q + 1 + 2 * i)
                        chunk(u0 + 4 * q, "gdn", feature_unit, 2 * q, 0, i, 8)

                def gate_unit(u, bank):
                    slot, n, _ = slot_of(u, 0, 0)
                    pe.wait_ge(lo_done, n + 1)
                    token_unit(slot, u % 4, bank, 0).then_inc(w_used, 1)
                pe.wait_ge(gd_free, 7)
                gate_unit(u0 + 24, 0)
                gates(1, 40).then_inc(gd_gates_s, 1)
                pe.wait_ge(evac_act, e + 6)
                for c in range(2):
                    for h in range(8):
                        n = 8 * c + h
                        last = pe.transpose(PS[:, 2 + n // 4, (n % 4) * P:(n % 4) * P + P],
                                            gd_qkv[:, 16 + h, c * P:c * P + P], ident)
                last.then_inc(gd_vt, 1)
                for b in range(2):
                    pe.wait_ge(gd_sqd, b + 1)
                    for h in range(8):
                        o = 39 - (32 * b + h)
                        last = mm(PS[0:40, 6, 0:T], C("unit_col")[:, o:o + 40], gd_sq[b][:, h], start=b == 0 and h == 0,
                                  stop=b == 1 and h == 7)
                last.then_inc(gd_sums, 1)
                for j in range(1, 4):
                    gate_unit(u0 + 24 + j, 0)
                pe.wait_ge(gd_logs, 1)
                for n, (row, c) in enumerate(((5, 0), (5, 1), (0, 0), (0, 1), (3, 1), (4, 1))):
                    pe.transpose(PS[:, 6, 8 * n:8 * n + 8], gd_rows[0:8, row, c * P:c * P + P], ident[0:8, 0:8])
                mm(PS[:, 6, 48:56], ones[0:8, :], gd_last[0:8, :], start=True, stop=True).then_inc(gd_colt, 1)

                def to_all(row):
                    for h in range(8):
                        last = mm(PS[:, 4 + h // 2, (h % 2) * T:(h % 2) * T + T], C(f"select{h}")[0:8, :], gd_rows[0:8, row],
                                  start=True, stop=True)
                    last.then_inc(gd_bcast, 1)
                pe.wait_ge(gd_colk, 1)
                pe.wait_ge(gd_tok, 1)
                to_all(3)
                gate_unit(u0 + 28, 2)
                gate_unit(u0 + 29, 2)
                pe.wait_ge(evac_act, e + 7)
                for h in range(8):
                    last = pe.transpose(PS[:, h // 4, (h % 4) * P:(h % 4) * P + P], gd_qkv[:, 8 + h, 0:P], ident)
                last.then_inc(gd_vt, 1)
                pe.wait_ge(gd_args, 1)
                to_all(4)
                gate_unit(u0 + 30, 2)
                gate_unit(u0 + 31, 2)

                def system(c, h, base=0):
                    n = 8 * c + h
                    return PS[:, base + n // 4, (n % 4) * P:(n % 4) * P + P]
                pe.wait_ge(gd_args, 2)
                for c in range(2):
                    for h in range(8):
                        k = gd_qkv[:, 8 + h, c * P:c * P + P]
                        last = mm(system(c, h, 4), k, k, start=True, stop=True)
                last.then_inc(gd_kk, 1)
                pe.wait_ge(evac_act, e + 8)
                for c in range(2):
                    for h in range(8):
                        s = slice(c * P, c * P + P)
                        last = mm(system(c, h), gd_qkv[:, 8 + h, s], gd_qkv[:, h, s], start=True, stop=True)
                last.then_inc(gd_qk, 1)

                def group(g, b, h):
                    return PS[:, 4 * (1 - g) + b + h // 4, (h % 4) * P:(h % 4) * P + P]

                for g in range(2):
                    pe.wait_ge(gd_masked, 2)
                    if g == 1:
                        pe.wait_ge(gd_made, 1)
                    for h in range(8):
                        last = pe.transpose(group(g, 0, h), gd_um[:, g, h], ident)
                    last.then_inc(gd_xps, 1)

                for level in range(1, LEVELS):
                    size = 2 ** level
                    for g in range(2):
                        pe.wait_ge(gd_masked, 2 * level + g + 1)
                        pe.wait_ge(gd_xnew, 2 * level + g - 1)
                        for h in range(8):
                            last = mm(group(g, 0, h), gd_um[:, g, h], gd_X[:, g, h], start=True, stop=True)
                        last.then_inc(gd_yps, 1)
                    for g in range(2):
                        pe.wait_ge(gd_ysb, 2 * level + g - 1)
                        lo = 4 * (1 - g)
                        for h in range(8):
                            if level + 1 < LEVELS:
                                mm(PS[:, lo + 2, 64 * h:64 * h + 64].rearrange("p (a t) -> p a t", t=size), gd_XT[:, g, h], halves(gd_Y[:, g, h:h + 1], size, 0)[:, 0],
                                   start=True, stop=True)
                            last = mm(PS[:, lo, 64 * h:64 * h + 64].rearrange("p (a t) -> p a t", t=size), gd_Y[:, g, h], halves(gd_XT[:, g, h:h + 1], size, 1)[:, 0],
                                      start=True, stop=True)
                        last.then_inc(gd_xps, 1)
                pe.wait_ge(gd_xnew, 14)
                pe.wait_ge(gd_scaled, 3)
                def bank_of(b0, b, h):
                    return PS[:, b0 + b + h // 4, (h % 4) * P:(h % 4) * P + P]
                for h in range(8):
                    last = mm(bank_of(0, 0, h), gd_XT[:, 0, h], gd_bv[:, 0, h], start=True, stop=True)
                last.then_inc(gd_fin_pe, 1)
                pe.wait_ge(gd_fin_act, 1)
                for h in range(8):
                    mm(bank_of(0, 2, h), gd_E[:, 0, h], gd_vn[:, h], start=True, stop=True)
                    last = mm(bank_of(4, 0, h), gd_kd[:, h], gd_vn[:, h], start=True, stop=True)
                last.then_inc(gd_fin_pe, 1)
                pe.wait_ge(gd_fin_act, 2)
                for h in range(8):
                    last = mm(bank_of(4, 2, h), gd_qkv[:, 8 + h, P:T], gd_S[:, h], start=True, stop=True)
                last.then_inc(gd_fin_pe, 1)
                pe.wait_ge(gd_fin_dve, 1)
                for h in range(8):
                    last = mm(bank_of(0, 0, h), gd_XT[:, 1, h], gd_bv[:, 1, h], start=True, stop=True)
                last.then_inc(gd_fin_pe, 1)
                for h in range(8):
                    mm(bank_of(4, 2, h), gd_qkv[:, h, P:T], gd_S[:, h], start=True, stop=True)
                pe.wait_ge(gd_fin_act, 3)
                for h in range(8):
                    last = mm(bank_of(4, 0, h), gd_E[:, 1, h], gd_vn[:, h], start=True, stop=True)
                last.then_inc(gd_fin_pe, 1)
                pe.wait_ge(gd_mixed, 2)
                turn("gdn_o")
                square(UNIT0["gdn_o"], "gdn_o", token_unit)

            def pool():
                pe.wait_ge(xn_ready, 2 * NORMS.index("pool") + 2)
                for b in range(4):
                    band = C(f"pool{WINDOWS[b]}")
                    for k in range(2):
                        s = slice((2 * b + k) * P, (2 * b + k) * P + P)
                        mm(PS[:, 4 + b, k * T:k * T + T], xn[:, 0, s], band[:, 0:T], start=True, stop=False, skip_group_check=True)
                        last = mm(PS[:, 4 + b, k * T + P:k * T + T], xn[:, 1, s], band[:, T:384], start=False, stop=True,
                                  skip_group_check=True)
                    last.then_inc(turned, 1)
                pe.wait_ge(evac_act, EVAC0["xq1"] + 2)
                for c in range(2):
                    u = UNIT0["pool"] + c
                    pe.wait_ge(lo_done, u + 1)
                    for g in range(2):
                        grp = 2 * c + g
                        kt_pair_wait("pool", grp)
                        for t in range(TT):
                            for k in range(2):
                                ts, ws, ks = slice(t * P, t * P + P), slice(g * T, g * T + T), slice(k * T, k * T + T)
                                last = three(PS[:, 2 * c + t, ws], XTh[:, 2 * grp + k, ts], XTl[:, 2 * grp + k, ts],
                                             w_hi[:, u % RING, g, ks], w_lo[:, u % RING, g, ks], k == 0, k == 1)
                    last.then_inc(w_used, 1)

            def swa():
                norm("swa")
                u0, e = UNIT0["qkv"], EVAC0["qkv"]
                for j in range(4):
                    slot, n, _ = slot_of(u0 + j, 0, 0)
                    kt_pair_wait("swa", j)
                    pe.wait_ge(lo_done, n + 1)
                    feature_unit(slot, j, 0, 0, tiles=2)
                    for k in range(2):
                        kt = 2 * j + k
                        for t in range(TT):
                            s = slice(t * P, t * P + P)
                            last = three(PS[:, 1, t * T:t * T + T], XTh[:, kt, s], XTl[:, kt, s], w_hi[:, slot, k, T:512],
                                         w_lo[:, slot, k, T:512], kt == 0 and t == 0, kt == KT - 1)
                    last.then_inc(w_used, 1)
                chunk(u0 + 4, None, feature_unit, 2)

                def query_units(first, last):
                    for j in range(first, last):
                        slot, n, _ = slot_of(u0 + 8 + j, 0, 0)
                        pe.wait_ge(lo_done, n + 1)
                        feature_unit(slot, j, 0, 0).then_inc(w_used, 1)

                def scores(grp):
                    if grp:
                        pe.wait_ge(sw_kept, grp)
                    for j in range(4):
                        h = 4 * grp + j
                        r = slice(64 * (h % 2), 64 * (h % 2) + 64)
                        q, k = sw_q[r, h // 2], sw_k[r, grp]
                        mm(PS[:, 4 + j, 0:P], q[:, 0:P], k[:, 0:P], start=True, stop=True)
                        last = mm(PS[:, 4 + j, P:384], q[:, P:T], k[:, 0:T], start=True, stop=True)
                    last.then_inc(sw_scores, 1)
                pe.wait_ge(evac_act, e + 1)
                pe.wait_ge(v_kept, 1)
                query_units(0, 1)
                pe.wait_ge(evac_act, e + 2)
                scores(0)
                query_units(1, 3)
                scores(1)
                query_units(3, 4)
                pe.wait_ge(evac_act, e + 3)
                for grp in range(4):
                    if grp + 2 < 4:
                        scores(grp + 2)
                    pe.wait_ge(sw_probs, grp + 1)
                    if grp:
                        pe.wait_ge(sw_pted, grp)
                    for j in range(4):
                        for b in range(3):
                            last = pe.transpose(PS[:, j, b * P:b * P + P], sw_s[:, grp % 3, j, b * P:b * P + P], ident)
                    last.then_inc(sw_turned, 1)
                pe.wait_ge(sw_pted, 4)
                for b in range(4):
                    for h in range(4 * b, 4 * b + 4):
                        f, r = h // 2, slice(64 * (h % 2), 64 * (h % 2) + 64)
                        o = (f % 2) * T
                        v = [sw_v[:, s, 64 * (h // 4):64 * (h // 4) + 64] for s in range(2)]
                        mm(PS[r, 4 + b, o:o + P], v[0], sw_pt[:, h, 0:P], start=True, stop=True)
                        mm(PS[r, 4 + b, o + P:o + T], v[0], sw_pt[:, h, P:T], start=True, stop=False)
                        last = mm(PS[r, 4 + b, o + P:o + T], v[1], sw_pt[:, h, T:384], start=False, stop=True)
                    last.then_inc(turned, 1)
                square(UNIT0["swa_o"], "swa_o", token_unit)

            ab()
            cross(0)
            wide("mlp0", FF // 512, 4)
            gdn()
            cross(1)
            wide("mlp1", FF // 512, 4)
            pool()
            wide("ffn0", GLU // 256, 2)
            swa()
            wide("ffn1", GLU // 256, 2)


_INS = ['x', 'mem', 'ab_w_in', 'ab_b_i', 'ab_b_f', 'ab_head_gain', 'ab_w_out', 'c_w_in', 'c_conv_w', 'c_a_log',
        'c_dt_bias', 'c_head_gain', 'c_w_out', 'xa_norm', 'mem_norm', 'mix_norm', 'xa_wq', 'xa_wk', 'xa_wv', 'xa_wo',
        'mlp_norm', 'mlp_w1', 'mlp_w2', 'final_norm', 'pool_w_2', 'pool_b_2', 'pool_scale_2', 'attn_w_qkv_2',
        'attn_b_qkv_2', 'attn_sinks_2', 'attn_w_o_2', 'norm_mix_2', 'norm_ffn_2', 'ffn_w_in_2', 'ffn_conv_w_2',
        'ffn_conv_b_2', 'ffn_w_out_2', 'norm_f_2']


def kernel(**inputs):
    import concourse.bacc as _bacc
    from concourse.bass_utils import run_bass_kernel_spmd as _run

    nc = _bacc.Bacc("TRN2", target_bir_lowering=False, num_devices=1)
    arrays, args = {}, {}
    for name in _INS + ["const"]:
        v = CONST if name == "const" else np.ascontiguousarray(inputs[name])
        arrays[f"in_{name}"] = v
        args[name] = nc.dram_tensor(f"in_{name}", v.shape, mybir.dt.from_np(v.dtype), kind="ExternalInput").ap()
    out = nc.dram_tensor("out_0", (1, T, D), F32, kind="ExternalOutput").ap()
    program(nc, args, out)
    r = _run(nc, [arrays], core_ids=[0])
    return r.results[0]["out_0"]
```
